# Optimizing a Trainium2 kernel written in Bass

```python
import jax
import jax.numpy as jnp
from jax import lax
import numpy as np

D_MODEL = 1024
BATCH = 1
SEQ = 512
DEPTH = 2
DEC_BATCH = 8
DEC_SEQ = 8
PAST_LEN = 2048
PAGE_SIZE = 128

N_META = 16
A_HEADS = 8
A_HEAD_DIM = 64
A_ROT = A_HEAD_DIM // 4
A_KV = 2 * A_HEAD_DIM
IDX_HEADS = 8
IDX_DIM = 32
IDX_ROT = IDX_DIM // 4
TOPK_MAX = 256
B_HEADS = 8
Q_LORA = 256
KV_LORA = 128
QK_NOPE = 64
QK_ROPE = 32
V_DIM = 64
MIX_WIDTH = A_HEADS * A_HEAD_DIM + B_HEADS * V_DIM
D_FF = 2816
ROPE_THETA = 500000.0
DEEPNORM_ALPHA = (2 * DEPTH) ** 0.25
DEEPNORM_BETA = (8 * DEPTH) ** -0.25
Q_BLOCK = 128
LN_EPS = 1e-5
RMS_EPS = 1e-6
DSA_ROW = A_KV + IDX_DIM
MLA_ROW = KV_LORA + QK_ROPE
SPLIT_SIZES = (A_HEADS * A_HEAD_DIM, A_KV, IDX_HEADS * IDX_DIM, IDX_DIM, IDX_HEADS, Q_LORA, KV_LORA, QK_ROPE)
SPLIT_POINTS = tuple(int(v) for v in np.cumsum(SPLIT_SIZES)[:-1])
N_IN = int(sum(SPLIT_SIZES))
V_COL_START = A_HEADS * A_HEAD_DIM + A_HEAD_DIM
V_COL_END = A_HEADS * A_HEAD_DIM + A_KV

kernel_name = 'hymba_dsa_mla_macaron_deepnorm_step'

def _layernorm(x, g, b):
    xf = x.astype(jnp.float32)
    mu = jnp.mean(xf, axis=-1, keepdims=True)
    var = jnp.mean(jnp.square(xf - mu), axis=-1, keepdims=True)
    return ((xf - mu) * lax.rsqrt(var + LN_EPS) * g + b).astype(x.dtype)

def _rmsnorm(x, g):
    xf = x.astype(jnp.float32)
    return (xf * lax.rsqrt(jnp.mean(xf * xf, axis=-1, keepdims=True) + RMS_EPS) * g).astype(x.dtype)

def _swiglu(x, w_in, w_out):
    g, u = jnp.split(x @ w_in, 2, axis=-1)
    return (jax.nn.silu(g) * u) @ w_out

def _rope(x, pos, rot):
    half = rot // 2
    inv = ROPE_THETA ** (-jnp.arange(half, dtype=jnp.float32) / half)
    ang = pos.astype(jnp.float32)[:, None] * inv
    ang = ang.reshape((ang.shape[0],) + (1,) * (x.ndim - 3) + (half,))
    cos = jnp.cos(ang).astype(x.dtype)
    sin = jnp.sin(ang).astype(x.dtype)
    x1, x2, rest = x[..., :half], x[..., half:rot], x[..., rot:]
    return jnp.concatenate([x1 * cos - x2 * sin, x2 * cos + x1 * sin, rest], axis=-1)

def _map_query_blocks(fn, xs, n_q):
    qb = min(Q_BLOCK, n_q)
    n_blk = -(-n_q // qb)
    pad = n_blk * qb - n_q

    def split(a):
        a = jnp.pad(a, [(0, 0), (0, pad)] + [(0, 0)] * (a.ndim - 2))
        a = a.reshape((a.shape[0], n_blk, qb) + a.shape[2:])
        return jnp.moveaxis(a, 1, 0)

    out = lax.map(fn, tuple(split(a) for a in xs))
    out = jnp.moveaxis(out, 0, 1)
    out = out.reshape((out.shape[0], n_blk * qb) + out.shape[3:])
    return out[:, :n_q]

def _dsa_attend(q, q_idx, w_idx, q_pos, k_idx, gather_kv, top_k):
    key_pos = jnp.arange(k_idx.shape[1], dtype=jnp.int32)

    def block(args):
        qa, qi, wi, pb = args
        dots = jnp.einsum('bqhd,bkd->bqhk', qi, k_idx, preferred_element_type=jnp.float32)
        score = jnp.einsum('bqh,bqhk->bqk', wi.astype(jnp.float32), jax.nn.relu(dots))
        score = jnp.where(key_pos <= pb[..., None], score, -jnp.inf)
        _, sel = lax.top_k(score, top_k)
        valid = sel <= pb[..., None]
        kv = gather_kv(sel)
        k, v = kv[..., :A_HEAD_DIM], kv[..., A_HEAD_DIM:]
        s = jnp.einsum('bqhd,bqkd->bqhk', qa, k, preferred_element_type=jnp.float32) * (A_HEAD_DIM ** -0.5)
        s = jnp.where(valid[:, :, None, :], s, -jnp.inf)
        p = jax.nn.softmax(s, axis=-1)
        return jnp.einsum('bqhk,bqkd->bqhd', p.astype(v.dtype), v)

    return _map_query_blocks(block, (q, q_idx, w_idx, q_pos), q.shape[1])

def _mla_attend(q_lat, q_pe, q_pos, c_kv, k_pe):
    key_pos = jnp.arange(c_kv.shape[1], dtype=jnp.int32)
    scale = (QK_NOPE + QK_ROPE) ** -0.5

    def block(args):
        ql, qp, pb = args
        s = (jnp.einsum('bqhr,bkr->bhqk', ql, c_kv, preferred_element_type=jnp.float32)
             + jnp.einsum('bqhd,bkd->bhqk', qp, k_pe, preferred_element_type=jnp.float32)) * scale
        s = jnp.where(key_pos <= pb[:, None, :, None], s, -jnp.inf)
        p = jax.nn.softmax(s, axis=-1)
        return jnp.einsum('bhqk,bkr->bqhr', p.astype(c_kv.dtype), c_kv)

    return _map_query_blocks(block, (q_lat, q_pe, q_pos), q_lat.shape[1])

def _project(h, pos, w_in_l, q_norm_l, w_uq_l, kv_norm_l, w_uk_l):
    b, t, _ = h.shape
    z = h @ w_in_l
    a_q, a_kv, i_q, i_k, i_w, b_cq, b_ckv, b_kpe = jnp.split(z, SPLIT_POINTS, axis=-1)
    a_q = _rope(a_q.reshape(b, t, A_HEADS, A_HEAD_DIM), pos, A_ROT)
    a_k = _rope(a_kv[..., :A_HEAD_DIM], pos, A_ROT)
    a_v = a_kv[..., A_HEAD_DIM:]
    i_q = _rope(i_q.reshape(b, t, IDX_HEADS, IDX_DIM), pos, IDX_ROT)
    i_k = _rope(i_k, pos, IDX_ROT)
    i_w = i_w * ((IDX_HEADS * IDX_DIM) ** -0.5)
    qb = (_rmsnorm(b_cq, q_norm_l) @ w_uq_l).reshape(b, t, B_HEADS, QK_NOPE + QK_ROPE)
    q_nope = qb[..., :QK_NOPE]
    q_pe = _rope(qb[..., QK_NOPE:], pos, QK_ROPE)
    q_lat = jnp.einsum('bthn,rhn->bthr', q_nope, w_uk_l)
    c_kv = _rmsnorm(b_ckv, kv_norm_l)
    k_pe = _rope(b_kpe, pos, QK_ROPE)
    dsa_row = jnp.concatenate([a_k, a_v, i_k], axis=-1)
    mla_row = jnp.concatenate([c_kv, k_pe], axis=-1)
    return a_q, i_q, i_w, q_lat, q_pe, dsa_row, mla_row

def _merge(o_a, o_lat, w_uv_l, w_o_l):
    b, t = o_a.shape[:2]
    o_b = jnp.einsum('bthr,rhd->bthd', o_lat, w_uv_l)
    o = jnp.concatenate([o_a.reshape(b, t, -1), o_b.reshape(b, t, -1)], axis=-1)
    return o @ w_o_l

def _mix_prompt(h, mw):
    w_in_l, q_norm_l, w_uq_l, kv_norm_l, w_uk_l, w_uv_l, w_o_l = mw
    b, t, _ = h.shape
    pos = jnp.arange(t, dtype=jnp.int32)
    a_q, i_q, i_w, q_lat, q_pe, dsa_row, mla_row = _project(h, pos, w_in_l, q_norm_l, w_uq_l, kv_norm_l, w_uk_l)
    q_pos = jnp.broadcast_to(pos, (b, t))
    kv_rows = dsa_row[..., :A_KV]

    def gather_kv(sel):
        return jax.vmap(lambda kv, s: kv[s])(kv_rows, sel)

    top_k = min(TOPK_MAX, t // 4)
    o_a = _dsa_attend(a_q, i_q, i_w, q_pos, dsa_row[..., A_KV:], gather_kv, top_k)
    o_lat = _mla_attend(q_lat, q_pe, q_pos, mla_row[..., :KV_LORA], mla_row[..., KV_LORA:])
    return _merge(o_a, o_lat, w_uv_l, w_o_l), dsa_row, mla_row

def _mix_sample(h, cache_dsa_l, cache_mla_l, page_table, mw):
    w_in_l, q_norm_l, w_uq_l, kv_norm_l, w_uk_l, w_uv_l, w_o_l = mw
    b, t, _ = h.shape
    past_len = page_table.shape[1] * PAGE_SIZE
    pos = past_len + jnp.arange(t, dtype=jnp.int32)
    a_q, i_q, i_w, q_lat, q_pe, dsa_row, mla_row = _project(h, pos, w_in_l, q_norm_l, w_uq_l, kv_norm_l, w_uk_l)
    q_pos = jnp.broadcast_to(pos, (b, t))
    idx_past = cache_dsa_l[:, :, A_KV:][page_table].reshape(b, past_len, IDX_DIM)
    k_idx = jnp.concatenate([idx_past, dsa_row[..., A_KV:]], axis=1)
    new_kv = dsa_row[..., :A_KV]

    def gather_kv(sel):
        def one(pt, nkv, s):
            sp = jnp.minimum(s, past_len - 1)
            past = cache_dsa_l[pt[sp // PAGE_SIZE], sp % PAGE_SIZE, :A_KV]
            new = nkv[jnp.clip(s - past_len, 0, t - 1)]
            return jnp.where((s < past_len)[..., None], past, new)
        return jax.vmap(one)(page_table, new_kv, sel)

    top_k = min(TOPK_MAX, (past_len + t) // 4)
    o_a = _dsa_attend(a_q, i_q, i_w, q_pos, k_idx, gather_kv, top_k)
    mla_past = cache_mla_l[page_table].reshape(b, past_len, MLA_ROW)
    mla_all = jnp.concatenate([mla_past, mla_row], axis=1)
    o_lat = _mla_attend(q_lat, q_pe, q_pos, mla_all[..., :KV_LORA], mla_all[..., KV_LORA:])
    return _merge(o_a, o_lat, w_uv_l, w_o_l), dsa_row, mla_row

def setup_inputs(seed: int = 0) -> dict:
    key = jax.random.key(seed)
    ks = jax.random.split(key, 24)
    n_pages = PAST_LEN // PAGE_SIZE
    n_pool = (DEC_BATCH * n_pages * 5) // 4

    def nrm(k, shape, scale):
        return jax.random.normal(k, shape, jnp.float32) * scale

    def gain(k, shape):
        return 1.0 + 0.02 * jax.random.normal(k, shape, jnp.float32)

    page_table = jax.random.permutation(ks[4], n_pool)[: DEC_BATCH * n_pages].reshape(DEC_BATCH, n_pages).astype(jnp.int32)
    w_in = nrm(ks[10], (DEPTH, D_MODEL, N_IN), D_MODEL ** -0.5)
    w_in = w_in.at[:, :, V_COL_START:V_COL_END].multiply(DEEPNORM_BETA)
    return {
        'x_prompt': nrm(ks[0], (BATCH, SEQ, D_MODEL), 1.0),
        'x_sample': nrm(ks[1], (DEC_BATCH, DEC_SEQ, D_MODEL), 1.0),
        'cache_dsa': nrm(ks[2], (DEPTH, n_pool, PAGE_SIZE, DSA_ROW), 1.0),
        'cache_mla': nrm(ks[3], (DEPTH, n_pool, PAGE_SIZE, MLA_ROW), 1.0),
        'page_table': page_table,
        'meta_tokens': nrm(ks[5], (N_META, D_MODEL), 1.0),
        'ln1_g': gain(ks[6], (DEPTH, D_MODEL)),
        'ln1_b': nrm(ks[7], (DEPTH, D_MODEL), 0.02),
        'ffn1_w_in': nrm(ks[8], (DEPTH, D_MODEL, 2 * D_FF), D_MODEL ** -0.5),
        'ffn1_w_out': nrm(ks[9], (DEPTH, D_FF, D_MODEL), D_FF ** -0.5 * DEEPNORM_BETA),
        'w_in': w_in,
        'mla_q_norm': gain(ks[11], (DEPTH, Q_LORA)),
        'mla_w_uq': nrm(ks[12], (DEPTH, Q_LORA, B_HEADS * (QK_NOPE + QK_ROPE)), Q_LORA ** -0.5),
        'mla_kv_norm': gain(ks[13], (DEPTH, KV_LORA)),
        'mla_w_uk': nrm(ks[14], (DEPTH, KV_LORA, B_HEADS, QK_NOPE), KV_LORA ** -0.5),
        'mla_w_uv': nrm(ks[15], (DEPTH, KV_LORA, B_HEADS, V_DIM), KV_LORA ** -0.5 * DEEPNORM_BETA),
        'w_o': nrm(ks[16], (DEPTH, MIX_WIDTH, D_MODEL), MIX_WIDTH ** -0.5 * DEEPNORM_BETA),
        'ln2_g': gain(ks[17], (DEPTH, D_MODEL)),
        'ln2_b': nrm(ks[18], (DEPTH, D_MODEL), 0.02),
        'ffn2_w_in': nrm(ks[19], (DEPTH, D_MODEL, 2 * D_FF), D_MODEL ** -0.5),
        'ffn2_w_out': nrm(ks[20], (DEPTH, D_FF, D_MODEL), D_FF ** -0.5 * DEEPNORM_BETA),
        'ln3_g': gain(ks[21], (DEPTH, D_MODEL)),
        'ln3_b': nrm(ks[22], (DEPTH, D_MODEL), 0.02),
    }

def reference(x_prompt, x_sample, cache_dsa, cache_mla, page_table, meta_tokens,
              ln1_g, ln1_b, ffn1_w_in, ffn1_w_out, w_in, mla_q_norm, mla_w_uq, mla_kv_norm,
              mla_w_uk, mla_w_uv, w_o, ln2_g, ln2_b, ffn2_w_in, ffn2_w_out, ln3_g, ln3_b):
    b = x_prompt.shape[0]
    meta = jnp.broadcast_to(meta_tokens[None].astype(x_prompt.dtype), (b, N_META, D_MODEL))
    xp = jnp.concatenate([meta, x_prompt], axis=1)
    xs = x_sample
    dsa_p, mla_p, dsa_s, mla_s = [], [], [], []
    for l in range(DEPTH):
        mw = (w_in[l], mla_q_norm[l], mla_w_uq[l], mla_kv_norm[l], mla_w_uk[l], mla_w_uv[l], w_o[l])
        xp = _layernorm(DEEPNORM_ALPHA * xp + 0.5 * _swiglu(xp, ffn1_w_in[l], ffn1_w_out[l]), ln1_g[l], ln1_b[l])
        xs = _layernorm(DEEPNORM_ALPHA * xs + 0.5 * _swiglu(xs, ffn1_w_in[l], ffn1_w_out[l]), ln1_g[l], ln1_b[l])
        mix_p, rows_dp, rows_mp = _mix_prompt(xp, mw)
        mix_s, rows_ds, rows_ms = _mix_sample(xs, cache_dsa[l], cache_mla[l], page_table, mw)
        xp = _layernorm(DEEPNORM_ALPHA * xp + mix_p, ln2_g[l], ln2_b[l])
        xs = _layernorm(DEEPNORM_ALPHA * xs + mix_s, ln2_g[l], ln2_b[l])
        xp = _layernorm(DEEPNORM_ALPHA * xp + 0.5 * _swiglu(xp, ffn2_w_in[l], ffn2_w_out[l]), ln3_g[l], ln3_b[l])
        xs = _layernorm(DEEPNORM_ALPHA * xs + 0.5 * _swiglu(xs, ffn2_w_in[l], ffn2_w_out[l]), ln3_g[l], ln3_b[l])
        dsa_p.append(rows_dp)
        mla_p.append(rows_mp)
        dsa_s.append(rows_ds)
        mla_s.append(rows_ms)
    y_prompt = xp[:, N_META:]
    return (y_prompt, xs, jnp.stack(dsa_p), jnp.stack(mla_p), jnp.stack(dsa_s), jnp.stack(mla_s))


_drawn_inputs = setup_inputs


def setup_inputs(seed=0):
    import zlib

    import numpy as np

    out = dict(_drawn_inputs(seed))
    spreads = {}
    factors = {'cache_mla': 8.0, 'mla_q_norm': 8.0, 'mla_kv_norm': 2.999, 'mla_w_uk': 2.726}
    for name, (base, spread) in spreads.items():
        noise = np.random.default_rng([zlib.crc32(name.encode()), seed]).standard_normal(out[name].shape)
        drawn = base * np.exp(spread * noise) if base else spread * noise
        out[name] = jnp.asarray(drawn.astype(out[name].dtype))
    for name, factor in factors.items():
        out[name] = (out[name] * factor).astype(out[name].dtype)
    return out
```

```python
import numpy as np
import concourse.bass as bass
from concourse import mybir
from contextlib import ExitStack

F32 = mybir.dt.float32
F32R = mybir.dt.float32r
BF16 = mybir.dt.bfloat16
I32 = mybir.dt.int32
ALU = mybir.AluOpType
ACT = mybir.ActivationFunctionType
AX = mybir.AxisListType.X

P = 128
DEPTH, D, D_FF = 2, 1024, 2816
SEQ, N_META, DEC_B, DEC_T = 512, 16, 8, 8
PROMPT = SEQ + N_META
SAMPLE = DEC_B * DEC_T
PAST, PAGE = 2048, 128
PAGES = PAST // PAGE
POOL_PAGES = DEC_B * PAGES * 5 // 4
TOK = PROMPT + SAMPLE
TILES = 5
ROWS = [P, P, P, P, TOK - 4 * P]
S0, TAIL = 4 * P, 4 * P + SAMPLE
KD = D // P
KF = D_FF // P
HALF = TOK // 2
ALPHA = (2 * DEPTH) ** 0.25
LN_EPS, RMS_EPS = 1e-5, 1e-6
AH, AD, AROT = 8, 64, 16
IH, ID, IROT = 8, 32, 8
BH, NOPE, PE_D, RL, QL, VD = 8, 64, 32, 128, 256, 64
ROW = 2 * AD + ID
N_IN = AH * AD + 2 * AD + IH * ID + ID + IH + QL + RL + PE_D
Z_AQ, Z_AK, Z_AV, Z_IQ = 0, AH * AD, AH * AD + AD, AH * AD + 2 * AD
Z_IK = Z_IQ + IH * ID
Z_IW = Z_IK + ID
Z_CQ = Z_IW + IH
Z_CKV = Z_CQ + QL
Z_KPE = Z_CKV + RL
QB = BH * (NOPE + PE_D)
TOPK_P = min(256, PROMPT // 4)
TOPK_S = min(256, (PAST + DEC_T) // 4)
ROPE_THETA = 500000.0
RAW = 4
SPLIT = 2
BLK = 1024
NEG = -1.0e30
TAKEN = -3.0e38


def rope_tables():
    pos = np.zeros(TILES * P, np.float32)
    pos[:S0] = np.arange(S0)
    pos[S0:TAIL] = PAST + np.arange(SAMPLE) % DEC_T
    pos[TAIL:TOK] = np.arange(S0, PROMPT)
    cos, sin = [], []
    for rot in (AROT, IROT, PE_D):
        half = rot // 2
        inv = (np.float32(ROPE_THETA) ** (-np.arange(half, dtype=np.float32) / np.float32(half))).astype(np.float32)
        ang = (pos[:, None] * inv).astype(np.float32)
        cos.append(np.cos(ang).astype(np.float32))
        sin.append(np.sin(ang).astype(np.float32))
    return np.ascontiguousarray(np.concatenate(cos + sin, axis=1), np.float32)


ROPE_W = AROT // 2 + IROT // 2 + PE_D // 2


class Sems:

    def __init__(self, ctx, nc, block, names):
        self.all = {}
        for n in names:
            self.all[n] = ctx.enter_context(nc.semaphore(f"{block}_{n}"))
        nums = sorted(s.num for s in self.all.values())
        assert nums == list(range(nums[0], nums[0] + len(nums)))
        self.range = range(nums[0], nums[-1] + 1)

    def __getattr__(self, n):
        return self.all[n]


class Map:

    def __init__(self, nc, base):
        self.nc, self.top = nc, (base + 63) // 64 * 64

    def region(self, nbytes):
        at = self.top
        self.top += (nbytes + 63) // 64 * 64
        return at

    def put(self, name, shape, dt, at):
        return self.nc.alloc_sbuf_tensor_at(name, shape, dt, offset=at)


LN_SEMS = ["evac_done", "stats_done", "aggr_done", "std_done", "rstd_done", "nb_done",
           "norm_done", "gain_done", "x_done", "xt_ps", "xth_done", "xtl_done", "gb_in", "alpha_done"]
STREAM_SEMS = ["raw_in0", "raw_in1", "raw_in2", "raw_in3", "hi_done", "split_done", "w_used"]


def stream_ops(T, S):
    raw_in = [S.raw_in0, S.raw_in1, S.raw_in2, S.raw_in3]

    def load(e, n, s, src, shape=None, first=False, round_=None):
        if not first:
            e.wait_ge(S.split_done, n - (RAW - 1))
        dst = T.raw[:, s, 0:(BLK if shape is None else shape[0] * shape[1])]
        if shape is not None:
            dst = dst.rearrange("p (k c) -> p k c", k=shape[0])
        e.dma_start(dst, src).then_inc(raw_in[s], 16)

    def hi(e, n, s, round_, width=BLK, first=False):
        e.wait_ge(raw_in[s], round_ * 16 + 16)
        if not first:
            e.wait_ge(S.w_used, n - (SPLIT - 1))
        e.activation(T.whi[:, s % SPLIT, 0:width], T.raw[:, s, 0:width], ACT.Copy).then_inc(S.hi_done, 1)

    def lo(e, n, s, width=BLK):
        e.wait_ge(S.hi_done, n + 1)
        e.tensor_tensor(T.wlo[:, s % SPLIT, 0:width], T.raw[:, s, 0:width],
                        T.whi[:, s % SPLIT, 0:width].bitcast(F32), ALU.subtract).then_inc(S.split_done, 1)

    return load, hi, lo


def three(e, out, lhi, llo, rhi, rlo, start, stop):
    e.matmul(out, lhi, rhi, start=start, stop=False)
    e.matmul(out, lhi, rlo, start=False, stop=False)
    return e.matmul(out, llo, rhi, start=False, stop=stop)


GROUPS = [(0, 1, 2), (3, 4)]
ACC = {0: (0, 1), 1: (2, 3), 2: (4, 5), 3: (6, 7), 4: (0, 1)}
TPB = {0: 2, 1: 4, 2: 2, 3: 4, 4: 2}


def out_stage(nc, T, S, kt, n0, lhs_hi, lhs_lo, scale, first_wait):
    load, hi, lo = stream_ops(T, S)
    nA = n0 + kt
    per = max(1, (kt - 2) // 5)
    turn = {min(kt - 1, 2 + 2 * per + per * t): t for t in range(3)} if kt > 12 else {}

    def sp(e, weight, ln_g, ln_b, l):
        for g in range(2):
            for k in range(kt):
                n = n0 + g * kt + k
                load(e, n, n % RAW, weight(k), first=n < RAW)
                if g == 0 and k == kt // 2:
                    ln_wait = T.gb_free(S)
                    if ln_wait:
                        e.wait_ge(*ln_wait)
                    for i, a in enumerate((ln_g, ln_b)):
                        e.dma_start(T.gb[:, i, :], a[bass.ds(l, 1), :].partition_broadcast(P)).then_inc(S.gb_in, 16)

    def act_split(e, n, first=False):
        hi(e, n, n % RAW, n // RAW, first=first)

    def ln_a(e, t):
        r = ROWS[t]
        if t == 0:
            e.wait_ge(S.alpha_done, TILES)
        for h in range(2):
            if h == 0:
                e.wait_ge(S.w_used, n0 + (kt if t in GROUPS[0] else 2 * kt))
            x = T.x[0:r, t, h * 512:(h + 1) * 512]
            e.scalar_tensor_tensor(x, T.ps[0:r, ACC[t][h], :], scale, x, ALU.mult, ALU.add)\
             .then_inc(S.evac_done, 1)
        for h in range(2):
            e.wait_ge(S.evac_done, 2 * t + h + 1)
            e.bn_stats(T.stats[0:r, h, :], T.x[0:r, t, h * 512:(h + 1) * 512]).then_inc(S.stats_done, 1)
        e.wait_ge(S.stats_done, 2 * t + 2)
        e.bn_aggr(T.mv[0:r, t, :], T.stats[0:r, :, :]).then_inc(S.aggr_done, 1)

    def ln_b(e, t):
        e.wait_ge(S.aggr_done, t + 1)
        e.activation(T.std[0:ROWS[t], t:t + 1], T.mv[0:ROWS[t], t, 1:2], ACT.Sqrt,
                     bias=T.eps[0:ROWS[t], 0:1]).then_inc(S.std_done, 1)

    def ln_c(e, t):
        r = ROWS[t]
        e.wait_ge(S.std_done, t + 1)
        e.reciprocal(T.rstd[0:r, t:t + 1], T.std[0:r, t:t + 1]).then_inc(S.rstd_done, 1)
        e.wait_ge(S.rstd_done, t + 1)
        e.scalar_tensor_tensor(T.nb[0:r, t:t + 1], T.mv[0:r, t, 0:1], -1.0, T.rstd[0:r, t:t + 1],
                               ALU.mult, ALU.mult).then_inc(S.nb_done, 1)

    def ln_d(e, t):
        r = ROWS[t]
        x = T.x[0:r, t, :]
        e.wait_ge(S.nb_done, t + 1)
        e.tensor_scalar(x, x, T.rstd[0:r, t:t + 1], T.nb[0:r, t:t + 1], ALU.mult, ALU.add).then_inc(S.norm_done, 1)
        if t == 0:
            e.wait_ge(S.gb_in, 32)
        e.wait_ge(S.norm_done, t + 1)
        e.tensor_tensor(x, x, T.gb[0:r, 0, :], ALU.mult).then_inc(S.gain_done, 1)
        e.wait_ge(S.gain_done, t + 1)
        e.tensor_tensor(x, x, T.gb[0:r, 1, :], ALU.add).then_inc(S.x_done, 1)

    def ln_e(e, t):
        r = ROWS[t]
        e.wait_ge(S.x_done, t + 1)
        if t < 2:
            e.wait_ge(S.evac_done, 2 * (t + 1) + 2)
        else:
            e.wait_ge(S.xtl_done, t - 1)
        for k in range(KD):
            mm = e.transpose(T.ps[:, TPB[t] + k // 4, (k % 4) * P:(k % 4) * P + r],
                             T.x[0:r, t, k * P:(k + 1) * P], T.ident[0:r, 0:r])
        mm.then_inc(S.xt_ps, 1)

    def tp(t):
        return T.ps[:, TPB[t]:TPB[t] + 2, :].rearrange("p b (q c) -> p (b q) c", q=4)[:, :, 0:ROWS[t]]

    def ln_f(e, t):
        e.wait_ge(S.xt_ps, t + 1)
        e.activation(T.xth[:, :, t * P:t * P + ROWS[t]], tp(t), ACT.Copy).then_inc(S.xth_done, 1)

    def ln_g(e, t):
        e.wait_ge(S.xth_done, t + 1)
        o = slice(t * P, t * P + ROWS[t])
        e.tensor_tensor(T.xtl[:, :, o], tp(t), T.xth[:, :, o].bitcast(F32), ALU.subtract).then_inc(S.xtl_done, 1)

    def act(e):
        for g in range(2):
            for k in range(kt):
                n = n0 + g * kt + k + 2
                if n < n0 + 2 * kt:
                    act_split(e, n)
                if g == 1 and kt > 12 and k % per == 0 and 0 < k // per <= 3:
                    ln_b(e, k // per - 1)
                if g == 1 and k in turn:
                    ln_f(e, turn[k])
        if kt <= 12:
            for t in range(3):
                ln_b(e, t)
            ln_f(e, 0)
            ln_b(e, 3)
            ln_f(e, 1)
            ln_b(e, 4)
            ln_f(e, 2)
        else:
            ln_b(e, 3)
            ln_b(e, 4)
        ln_f(e, 3)
        ln_f(e, 4)

    def dve(e):
        for g in range(2):
            for k in range(kt):
                n = n0 + g * kt + k + 2
                if g == 1 and k == 0:
                    ln_a(e, 0)
                if n < n0 + 2 * kt:
                    lo(e, n, n % RAW)
                if g == 1 and kt > 12:
                    if k % per == 0 and 0 < k // per < 3:
                        ln_a(e, k // per)
                    if k % per == min(1, per - 1) and 0 < k // per <= 3:
                        ln_c(e, k // per - 1)
                    if k in turn:
                        ln_g(e, turn[k])
                if g == 1 and kt <= 12 and k in (2, 4):
                    ln_a(e, k // 2)
        if kt <= 12:
            for t in range(3):
                ln_c(e, t)
            ln_g(e, 0)
            ln_a(e, 3)
            ln_c(e, 3)
            ln_g(e, 1)
            ln_a(e, 4)
            ln_c(e, 4)
            ln_g(e, 2)
        else:
            ln_a(e, 3)
            ln_c(e, 3)
            ln_a(e, 4)
            ln_c(e, 4)
        ln_g(e, 3)
        ln_g(e, 4)

    def pool(e):
        for t in range(TILES):
            ln_d(e, t)

    def pe(e):
        for g in range(2):
            for k in range(kt):
                n = n0 + g * kt + k
                s = n % SPLIT
                e.wait_ge(S.split_done, n + 1)
                for t in GROUPS[g]:
                    first_wait(e, g, k, t)
                    if k == 0 and g == 1 and t == 4:
                        e.wait_ge(S.evac_done, 2)
                    o = slice(t * P, t * P + ROWS[t])
                    for h in range(2):
                        c = slice(h * 512, h * 512 + 512)
                        out = T.ps[0:ROWS[t], ACC[t][h], :]
                        mm = three(e, out, lhs_hi[:, k, o], lhs_lo[:, k, o], T.whi[:, s, c], T.wlo[:, s, c],
                                   k == 0, k == kt - 1)
                mm.then_inc(S.w_used, 1)
                if g == 1 and k in turn:
                    ln_e(e, turn[k])
        for t in range(0 if kt <= 12 else 3, TILES):
            ln_e(e, t)

    return sp, act, dve, pool, pe


FFN_SEMS = LN_SEMS + STREAM_SEMS + ["silu_done", "hmul_done", "hhi_done", "hlo_done"]


def ffn_block(nc, T, S, l, w_in, w_out, ln_g, ln_b):
    load, hi, lo = stream_ops(T, S)
    N1 = 2 * KF

    def first_wait(e, g, k, t):
        if g == 0 and k == 0 and t in (0, 2):
            e.wait_ge(S.hmul_done, KF - 1 + t // 2)
        if g == 0 and t == 0 and (k == 0 or k >= KF - 2):
            e.wait_ge(S.hlo_done, max(k + 1, KF - 2))
    T.gb_free = lambda S_: (S_.hlo_done, KF)
    sp2, act2, dve2, pool2, pe2 = out_stage(nc, T, S, KF, N1, T.hth, T.htl, 0.5, first_wait)

    def bank(j2, up):
        return T.ps[:, 4 * j2 + 2 * up:4 * j2 + 2 * up + 2, 0:HALF]

    with nc.Block() as block:
        @block.sync
        def _(e):
            def four(i, first):
                for u in range(4):
                    j = 2 * i + u // 2
                    col = (u % 2) * D_FF + j * P
                    src = w_in[bass.ds(l, 1), :, bass.ds(col, P)].rearrange("l (k p) c -> p (l k) c", p=P)
                    load(e, 4 * i + u, u, src, shape=(KD, P), first=first)
            four(0, True)
            with e.Fori(1, KF // 2) as i:
                four(i, False)
            sp2(e, lambda k: w_out[bass.ds(l, 1), k * P:(k + 1) * P, :].rearrange("l p n -> p (l n)"), ln_g, ln_b, l)

        @block.scalar
        def _(e):
            def silu(i, u, first=False):
                e.wait_ge(S.w_used, 4 * i + 2 * u + 2)
                if not (first and u == 0):
                    e.wait_ge(S.hmul_done, 2 * i + u)
                e.activation(T.silu[:, :].rearrange("p (h c) -> p h c", h=2), bank(u, 0), ACT.Silu).then_inc(S.silu_done, 1)

            def body(i, first):
                for u in range(2):
                    for b in range(2):
                        n = 2 + 2 * u + b
                        hi(e, 4 * i + n, n % RAW, i + n // RAW)
                    silu(i, u, first)
            hi(e, 0, 0, 0, first=True)
            hi(e, 1, 1, 0, first=True)
            body(0, True)
            with e.Fori(1, KF // 2) as i:
                body(i, False)
            act2(e)

        @block.vector
        def _(e):
            def hmul(i, u, first=False):
                e.wait_ge(S.silu_done, 2 * i + u + 1)
                if not first:
                    e.wait_ge(S.hlo_done, 2 * i + u - 1)
                e.tensor_tensor(T.hf[:, u, :].rearrange("p (h c) -> p h c", h=2),
                                T.silu[:, :].rearrange("p (h c) -> p h c", h=2), bank(u, 1), ALU.mult)\
                 .then_inc(S.hmul_done, 1)

            def body(i, first):
                for u in range(2):
                    for b in range(2):
                        n = 2 + 2 * u + b
                        lo(e, 4 * i + n, n % RAW)
                    hmul(i, u, first)
            lo(e, 0, 0)
            lo(e, 1, 1)
            body(0, True)
            with e.Fori(1, KF // 2) as i:
                body(i, False)
            dve2(e)

        @block.gpsimd
        def _(e):
            for t in range(TILES):
                x = T.x[0:ROWS[t], t, :]
                e.tensor_scalar(x, x, ALPHA, 1.0, ALU.mult, ALU.mult).then_inc(S.alpha_done, 1)

            with e.Fori(0, KF // 2) as i:
                for u in range(2):
                    j = bass.ds(2 * i + u, 1)
                    e.wait_ge(S.hmul_done, 2 * i + u + 1)
                    h_hi = T.hth[:, j, :].rearrange("p j c -> p (j c)")
                    h_lo = T.htl[:, j, :].rearrange("p j c -> p (j c)")
                    e.tensor_copy(h_hi, T.hf[:, u, :]).then_inc(S.hhi_done, 1)
                    e.wait_ge(S.hhi_done, 2 * i + u + 1)
                    e.tensor_tensor(h_lo, T.hf[:, u, :], h_hi.bitcast(F32), ALU.subtract).then_inc(S.hlo_done, 1)
            pool2(e)

        @block.tensor
        def _(e):
            def body(i, first):
                for u in range(2):
                    for up in range(2):
                        n = 4 * i + 2 * u + up
                        s = up % SPLIT
                        e.wait_ge(S.split_done, n + 1)
                        if up == 0 and not first:
                            e.wait_ge(S.hmul_done, 2 * i + u - 1)
                        for k in range(KD):
                            w = slice(k * P, (k + 1) * P)
                            for part, xs in ((T.whi, (T.xth, T.xtl)), (T.wlo, (T.xth,))):
                                for h in range(2):
                                    o = slice(h * HALF, (h + 1) * HALF)
                                    for xp in xs:
                                        mm = e.matmul(bank(u, up)[:, h, :], part[:, s, w], xp[:, k, o],
                                                      start=(k == 0 and part is T.whi and xp is T.xth),
                                                      stop=(k == KD - 1 and part is T.wlo))
                        mm.then_inc(S.w_used, 1)
            body(0, True)
            with e.Fori(1, KF // 2) as i:
                body(i, False)
            pe2(e)
    nc.all_engine_barrier(sems_to_clear=S.range)


C_ROPE = 0
C_DELTA = C_ROPE + TILES * 2 * ROPE_W
C_TRI8 = C_DELTA + DEC_T
C_TRI = C_TRI8 + DEC_T
C_SEL = C_TRI + P
C_END = C_SEL + DEC_B // 2 * P


def constants():
    c = np.zeros((P, C_END), np.float32)
    c[:, C_ROPE:C_DELTA] = rope_tables().reshape(TILES, P, -1).transpose(1, 0, 2).reshape(P, -1)
    row, t = np.arange(P)[:, None], np.arange(DEC_T)[None, :]
    c[:, C_DELTA:C_TRI8] = (row % DEC_T == t)
    c[:, C_TRI8:C_TRI] = np.where(t <= row % DEC_T, 0.0, NEG)
    c[:, C_TRI:C_SEL] = np.where(np.arange(P)[None, :] <= row, 0.0, NEG)
    for pair in range(DEC_B // 2):
        for m in range(P):
            token = (2 * pair + m // (P // 2)) * DEC_T + m % DEC_T
            c[token, C_SEL + pair * P + m] = 1.0
    return c


INIT_SEMS = ["x_in", "const_in", "casts", "pages_in", "ident_zero", "ident_done", "xt_ps", "xth_done", "xtl_done"]


def init_block(nc, T, S, x_prompt, x_sample, meta, consts, page_table):
    nc_loads = 5
    with nc.Block() as block:
        @block.sync
        def _(e):
            e.dma_start(T.x[0:N_META, 0, :], meta).then_inc(S.x_in, 16)
            e.dma_start(T.pages[:, :], page_table.rearrange("(a b) n -> a (b n)", a=1)).then_inc(S.pages_in, 16)
            e.dma_start(T.cin[:, :], consts).then_inc(S.const_in, 16)
            e.dma_start(T.x[N_META:P, 0, :], x_prompt[0, 0:P - N_META, :]).then_inc(S.x_in, 16)
            e.dma_start(T.x[:, 1:4, :], x_prompt[0, P - N_META:S0 - N_META, :].rearrange("(t p) d -> p t d", p=P))\
             .then_inc(S.x_in, 16)
            e.dma_start(T.x[0:SAMPLE, 4, :], x_sample.rearrange("b t d -> (b t) d")).then_inc(S.x_in, 16)
            e.dma_start(T.x[SAMPLE:ROWS[4], 4, :], x_prompt[0, S0 - N_META:SEQ, :]).then_inc(S.x_in, 16)
            e.wait_ge(S.pages_in, 16)

        @block.gpsimd
        def _(e):
            e.memset(T.ident[:, :], 0.0).then_inc(S.ident_zero, 1)
            e.memset(T.eps[:, 0:1], LN_EPS)
            e.memset(T.eps[:, 1:2], RMS_EPS)
            e.wait_ge(S.ident_zero, 1)
            e.affine_select(out=T.ident[:, :], in_=T.ident[:, :], compare_op=ALU.not_equal, fill=1.0,
                            base=0, pattern=[[-1, P]], channel_multiplier=1).then_inc(S.ident_done, 1)
            e.wait_ge(S.const_in, 16)
            e.wait_ge(S.ident_done, 1)
            c = T.cin
            e.tensor_copy(T.identb[:, :], T.ident[:, :])
            e.tensor_copy(T.rope[:, :, :].rearrange("p t c -> p (t c)"), c[:, C_ROPE:C_DELTA])
            e.tensor_copy(T.qdelta[:, :], c[:, C_DELTA:C_TRI8])
            e.tensor_copy(T.tri8[:, :], c[:, C_TRI8:C_TRI])
            e.tensor_copy(T.tri8b[:, :], c[:, C_TRI8:C_TRI])
            e.tensor_copy(T.trib[:, :], c[:, C_TRI:C_SEL])
            e.tensor_copy(T.selb[:, :, :].rearrange("p a c -> p (a c)"), c[0:SAMPLE, C_SEL:C_END]).then_inc(S.casts, 1)

        @block.tensor
        def _(e):
            e.wait_ge(S.ident_done, 1)
            e.wait_ge(S.x_in, 16 * nc_loads)
            for t in range(TILES):
                r = ROWS[t]
                if t >= 4:
                    e.wait_ge(S.xtl_done, t - 3)
                for k in range(KD):
                    mm = e.transpose(T.ps[:, 2 * (t % 4) + k // 4, (k % 4) * P:(k % 4) * P + r],
                                     T.x[0:r, t, k * P:(k + 1) * P], T.ident[0:r, 0:r])
                mm.then_inc(S.xt_ps, 1)

        def tp(t):
            b = 2 * (t % 4)
            return T.ps[:, b:b + 2, :].rearrange("p b (q c) -> p (b q) c", q=4)[:, :, 0:ROWS[t]]

        @block.scalar
        def _(e):
            for t in range(TILES):
                e.wait_ge(S.xt_ps, t + 1)
                e.activation(T.xth[:, :, t * P:t * P + ROWS[t]], tp(t), ACT.Copy).then_inc(S.xth_done, 1)

        @block.vector
        def _(e):
            for t in range(TILES):
                e.wait_ge(S.xth_done, t + 1)
                o = slice(t * P, t * P + ROWS[t])
                e.tensor_tensor(T.xtl[:, :, o], tp(t), T.xth[:, :, o].bitcast(F32), ALU.subtract)\
                 .then_inc(S.xtl_done, 1)
    nc.all_engine_barrier(sems_to_clear=S.range)


class Tensors:
    pass


def make_tensors(nc, ctx):
    T = Tensors()
    M = Map(nc, nc.sbuf_base)
    T.ps = ctx.enter_context(nc.psum_tensor("ps", [P, 8, 512], F32))
    T.x = M.put("x", [P, TILES, D], F32, M.region(TILES * D * 4))
    T.nc = nc
    T.xth_at = M.region(KD * TOK * 4)
    T.xth = M.put("xth", [P, KD, TOK], F32R, T.xth_at)
    T.xtl = M.put("xtl", [P, KD, TOK], F32R, M.region(KD * TOK * 4))
    T.raw_at = M.region(RAW * BLK * 4)
    T.raw = M.put("raw", [P, RAW, BLK], F32, T.raw_at)
    T.hi_at = M.region(SPLIT * BLK * 4)
    T.whi = M.put("whi", [P, SPLIT, BLK], F32R, T.hi_at)
    T.lo_at = M.region(SPLIT * BLK * 4)
    T.wlo = M.put("wlo", [P, SPLIT, BLK], F32R, T.lo_at)
    T.gb_at = M.region(2 * D * 4)
    T.gb = M.put("gb", [P, 2, D], F32, T.gb_at)
    T.silu = M.put("silu", [P, TOK], F32, T.gb_at)
    T.hf = M.put("hf", [P, 2, TOK], F32, T.gb_at + TOK * 4)
    T.small_at = M.region(8192)
    M2 = Map(nc, T.small_at)
    T.ident = M2.put("ident", [P, P], F32, M2.region(P * 4))
    T.eps = M2.put("eps", [P, 2], F32, M2.region(8))
    T.stats = M2.put("stats", [P, 2, 6], F32, M2.region(48))
    T.mv = M2.put("mv", [P, TILES, 2], F32, M2.region(40))
    T.std = M2.put("std", [P, TILES], F32, M2.region(20))
    T.rstd = M2.put("rstd", [P, TILES], F32, M2.region(20))
    T.nb = M2.put("nb", [P, TILES], F32, M2.region(20))
    T.rope = M2.put("rope", [P, TILES, 2 * ROPE_W], F32, M2.region(TILES * 2 * ROPE_W * 4))
    T.qdelta = M2.put("qdelta", [P, DEC_T], F32, M2.region(DEC_T * 4))
    T.tri8 = M2.put("tri8", [P, DEC_T], F32, M2.region(DEC_T * 4))
    T.identb = M2.put("identb", [P, P], BF16, M2.region(P * 2))
    T.trib = M2.put("trib", [P, P], BF16, M2.region(P * 2))
    T.selb = M2.put("selb", [SAMPLE, DEC_B // 2, P], BF16, M2.region(DEC_B // 2 * P * 2))
    T.tri8b = M2.put("tri8b", [P, DEC_T], BF16, M2.region(DEC_T * 2))
    T.iw = M2.put("iw", [P, TILES, IH], F32, M2.region(TILES * IH * 4))
    T.pages = M2.put("pages", [1, DEC_B * PAGES], I32, M2.region(DEC_B * PAGES * 4))
    T.misc = M2.put("misc", [P, 256], F32, M2.region(1024))
    assert M2.top <= T.small_at + 8192
    T.arena = M.region(2 * KF * TOK * 4)
    T.hth = M.put("hth", [P, KF, TOK], F32R, T.arena)
    T.cin = M.put("cin", [P, C_END], F32, T.arena)
    T.htl = M.put("htl", [P, KF, TOK], F32R, T.arena + KF * TOK * 4)
    T.M = M
    assert M.top <= nc.sbuf_usable_end, (M.top, nc.sbuf_usable_end)
    return T


ZC = N_IN // 4
ZK = [(0, 3), (3, 6), (6, 8)]
UC = QB // 2
IW_SCALE = (IH * ID) ** -0.5
PROJ_SEMS = STREAM_SEMS + [
    "par_in", "pad_zero", "z_act", "z_dve", "sq_done", "rms_std", "rms_rstd", "dve_step", "rope_done",
    "norm_q", "norm_kv", "rows_out", "stacked", "sb_done", "stack_zero", "late_done", "rows_back", "kcomb_done", "kdup_done", "icomb_done", "iw_done",
    "turned", "turned_act", "turned_dve", "cqh_done", "cql_done", "qb_act", "qb_dve", "qlat_ps", "qlat_done"]


def proj_tensors(T):
    A = Map(T.nc, T.arena)
    p = lambda name, shape, at=None: T.M.put(name, shape, F32, A.region(int(np.prod(shape[1:])) * 4) if at is None else at)
    T.qlatT = p("qlatT", [P, BH, TOK])
    T.qaT = p("qaT", [P, AH // 2, TOK])
    T.combT = p("combT", [P, 4, TOK])
    T.kT2 = p("kT2", [P, TOK])
    T.kcT = p("kcT", [P, TOK])
    T.ckvT = p("ckvT", [P, TOK])
    r = lambda name, shape, at=None: T.M.put(name, shape, F32R, A.region(int(np.prod(shape[1:])) * 4) if at is None else at)
    T.QLh = r("QLh", [P, DEC_B, P], T.gb_at + 4096)
    T.QLl = r("QLl", [P, DEC_B, P], T.gb_at - 4096)
    T.newT_at = A.top
    T.newT = r("newT", [P, 3, SAMPLE])
    T.newcT = r("newcT", [P, 2, SAMPLE])
    T.z_at = A.top
    T.z = p("z", [P, TILES, N_IN])
    T.comb_at = A.top
    T.QI = r("QI", [P, DEC_B, P], A.top)
    T.QP = r("QP", [P, DEC_B, P], A.top + 4096)
    T.QA = r("QA", [P, DEC_B, P], A.top + 8192)
    T.QB = r("QB", [P, DEC_B, P], A.top + 12288)
    T.score_at = A.top + 16384
    T.comb = p("comb", [P, TILES, IH, ID + PE_D])
    T.qn = p("qn", [P, TILES, BH * NOPE])
    T.qpe = p("qpe", [P, TILES, BH, PE_D])
    assert A.top <= T.arena + 2 * KF * TOK * 4, A.top - T.arena
    X = Map(T.nc, T.xth_at)
    T.cqh = T.M.put("cqh", [P, 2, TOK], F32R, X.region(2 * TOK * 4))
    T.cql = T.M.put("cql", [P, 2, TOK], F32R, X.region(2 * TOK * 4))
    T.qnT = T.M.put("qnT", [P, BH // 2, TOK], F32, X.region(BH // 2 * TOK * 4))
    T.wukT = T.M.put("wukT", [P, BH // 2, P], F32, X.region(BH // 2 * P * 4))
    T.kcomb = T.M.put("kcomb", [P, TILES, 2, ID + PE_D], F32, X.region(TILES * P * 4))
    T.kdup = T.M.put("kdup", [P, TILES, 2, AD], F32, X.region(TILES * P * 4))
    T.sI = T.M.put("sI", [SAMPLE, IH, P], F32R, X.region(IH * P * 4))
    T.sA = T.M.put("sA", [SAMPLE, AH, P], F32R, T.xth_at)
    T.sB = T.M.put("sB", [SAMPLE, AH, P], F32R, T.xth_at + 4096)
    T.sN = T.M.put("sN", [SAMPLE, 3, P], F32R, T.gb_at + 2048)
    T.tmp_at = X.top
    T.tmp = [T.M.put(f"rope{i}", [P, TILES * 8 * 16], F32, X.region(TILES * 8 * 16 * 4)) for i in range(2)]
    T.sP = T.M.put("sP", [SAMPLE, BH, P], F32R, T.tmp_at)
    assert X.top <= T.xth_at + 2 * KD * TOK * 4
    G = Map(T.nc, T.gb_at)
    T.wuv = T.M.put("wuv", [P, BH, VD], F32, G.region(BH * VD * 4))
    T.wuk = T.M.put("wuk", [P, BH, NOPE], F32, G.region(BH * NOPE * 4))
    T.gains = T.M.put("gains", [P, QL + RL], F32, G.region((QL + RL) * 4))
    T.tmp += [T.M.put("rope2", [P, TILES * 8 * 16], F32, G.region(TILES * 8 * 16 * 4))]
    assert G.top <= T.gb_at + 2 * D * 4
    T.ssq = T.misc[:, 0:10]
    T.sstd = T.misc[:, 10:20]
    T.srstd = T.misc[:, 20:30]
    T.wcol = T.misc[:, 32:40]
    T.junk = T.ps


def proj_block(nc, T, S, l, W, O):
    load, hi, lo = stream_ops(T, S)
    NZ = 12

    class Group:
        def __init__(s, src, dst, wait, engine, only=None):
            s.src, s.dst, s.wait, s.engine, s.only = src, dst, wait, engine, only

    z = T.z
    tiles = range(TILES)

    def colsT(bank, w=TOK):
        return T.ps[:, :, :].rearrange("p b c -> p (b c)")[:, bank * 512:bank * 512 + w]

    def half_cols(q, half):
        return q[:, :, :].rearrange("p (b u) (w h t) -> p b u w h t", u=2, w=2, h=8)[:, :, half, half]

    def aq(i):
        return lambda r, t: z[0:r, t, i * P:(i + 1) * P]

    g1 = [Group(lambda r, t: z[0:r, t, Z_CQ:Z_CQ + P], 0, ("norm_q", TILES), "both"),
          Group(lambda r, t: z[0:r, t, Z_CQ + P:Z_CQ + 2 * P], 1, ("norm_q", TILES), "both")]
    g1 += [Group(aq(i), T.qaT[:, i, :], ("rope_done", 2), "act" if i % 2 else "dve") for i in range(4)]
    g1 += [Group(lambda r, t: T.kdup[0:r, t, :, :].rearrange("p a c -> p (a c)"), T.kT2[:, :], ("kdup_done", 2), "dve"),
           Group(lambda r, t: T.kcomb[0:r, t, :, :].rearrange("p a c -> p (a c)"), T.kcT[:, :], ("kcomb_done", 4), "act"),
           Group(lambda r, t: z[0:r, t, Z_CKV:Z_KPE], T.ckvT[:, :], ("norm_kv", TILES), "dve"),
           Group(lambda r, h: T.wuk[:, 2 * h:2 * h + 2, :].rearrange("p h c -> p (h c)"), T.wukT,
                 ("par_in", 64), "act", "wuk")]
    g2 = [Group(lambda r, t, i=i: T.comb[0:r, t, 2 * i:2 * i + 2, :].rearrange("p h c -> p (h c)"), T.combT[:, i, :],
                ("icomb_done", 1), "act" if i % 2 else "dve") for i in range(4)]
    g2 += [Group(lambda r, t, i=i: T.qn[0:r, t, i * P:(i + 1) * P],
                 T.qnT[:, i, :], ("qb_dve", 8), "dve" if i % 2 else "act") for i in range(4)]
    for i, (src, dst) in enumerate(((T.sA, T.QA), (T.sB, T.QB), (T.sI, T.QI), (T.sP, T.QP))):
        g2.append(Group(lambda r, h, src=src: src[:, h, :].bitcast(F32), dst, ("stacked", 12), "act" if i % 2 else "dve", "heads"))
    g2.append(Group(lambda r, h: T.sN[:, h, :].bitcast(F32), T.newT, ("stacked", 12), "act", "new"))
    groups = g1 + g2
    outs = []
    nact = ndve = 0
    for g in groups:
        if g.engine == "both":
            outs.append(("cql_done", g.dst + 1))
        elif g.engine == "act":
            nact += 1
            outs.append(("turned_act", nact))
        else:
            ndve += 1
            outs.append(("turned_dve", ndve))

    def turn(e, gi, first_bank_wait):
        g = groups[gi]
        e.wait_ge(S.all[g.wait[0]], g.wait[1])
        if g.wait[0] == "stacked":
            e.wait_ge(S.sb_done, 2)
        if g.wait[0] == "icomb_done":
            e.wait_ge(S.rope_done, 8)
        if first_bank_wait is not None:
            e.wait_ge(S.all[outs[first_bank_wait][0]], outs[first_bank_wait][1])
        b = 2 * (gi % 4)
        if g.only is None:
            for t in tiles:
                r = ROWS[t]
                mm = e.transpose(colsT(b)[:, t * P:t * P + r], g.src(r, t), T.ident[0:r, 0:r])
        elif g.only == "new":
            for h in range(3):
                mm = e.transpose(colsT(b)[:, h * SAMPLE:(h + 1) * SAMPLE], g.src(0, h), T.ident[0:SAMPLE, 0:SAMPLE])
        elif g.only == "heads":
            for h in range(8):
                mm = e.transpose(colsT(b)[:, h * SAMPLE:(h + 1) * SAMPLE], g.src(0, h), T.ident[0:SAMPLE, 0:SAMPLE])
        else:
            for h in range(4):
                mm = e.transpose(colsT(b)[:, h * P:(h + 1) * P], g.src(0, h), T.ident[:, :])
        mm.then_inc(S.turned, 1)

    def out(e, gi, who):
        g = groups[gi]
        if g.engine != who and g.engine != "both":
            return
        e.wait_ge(S.turned, gi + 1)
        b = 2 * (gi % 4)
        if g.engine == "both":
            if who == "act":
                e.activation(T.cqh[:, g.dst, :], colsT(b), ACT.Copy).then_inc(S.cqh_done, 1)
            else:
                e.wait_ge(S.cqh_done, g.dst + 1)
                e.tensor_tensor(T.cql[:, g.dst, :], colsT(b), T.cqh[:, g.dst, :].bitcast(F32), ALU.subtract)\
                 .then_inc(S.cql_done, 1)
            return
        if g.only is None:
            dst, src = g.dst, colsT(b)
        elif g.only == "new":
            dst, src = g.dst[:, :, :].rearrange("p n c -> p (n c)"), colsT(b, 3 * SAMPLE)
        elif g.only == "heads":
            for half in range(2):
                dst = half_cols(g.dst, half)
                src = colsT(b, 512).rearrange("p (h b u t) -> p b u h t", h=8, b=DEC_B // 2, u=2)[:, :, half]
                e.wait_ge(S.stack_zero, 4)
                ins = e.activation(dst, src, ACT.Copy) if who == "act" else e.tensor_copy(dst, src)
            ins.then_inc(S.turned_act if who == "act" else S.turned_dve, 1)
            return
        else:
            dst, src = g.dst[:, :, :].rearrange("p h c -> p (h c)"), colsT(b, 512)
        if who == "act":
            e.activation(dst, src, ACT.Copy).then_inc(S.turned_act, 1)
        else:
            e.tensor_copy(dst, src).then_inc(S.turned_dve, 1)

    def q_out(copy, c, t):
        r = ROWS[t]
        q = T.ps[0:r, (5 * c + t) % 8, 0:UC].rearrange("p (h c) -> p h c", h=4)
        copy(T.qn[0:r, t, c * 4 * NOPE:(c + 1) * 4 * NOPE].rearrange("p (h c) -> p h c", h=4), q[:, :, 0:NOPE])
        copy(T.qpe[0:r, t, 4 * c:4 * c + 4, :], q[:, :, NOPE:NOPE + PE_D])

    def z_free(e, ev):
        c, t = ev // 5, ev % 5
        e.wait_ge(*((S.z_act, 3 * c + t // 2 + 1) if t % 2 == 0 else (S.z_dve, 2 * c + t // 2 + 1)))

    with nc.Block() as block:
        @block.sync
        def _(e):
            e.dma_start(T.gains[:, 0:QL], W["mla_q_norm"][bass.ds(l, 1), :].partition_broadcast(P)).then_inc(S.par_in, 16)
            e.dma_start(T.gains[:, QL:QL + RL], W["mla_kv_norm"][bass.ds(l, 1), :].partition_broadcast(P)).then_inc(S.par_in, 16)
            e.dma_start(T.wuk[:, :, :], W["mla_w_uk"][bass.ds(l, 1)].rearrange("l r h n -> r (l h) n")).then_inc(S.par_in, 16)
            e.dma_start(T.wuv[:, :, :], W["mla_w_uv"][bass.ds(l, 1)].rearrange("l r h n -> r (l h) n")).then_inc(S.par_in, 16)
            for n in range(NZ + 2):
                if n < NZ:
                    c, (k0, k1) = n // 3, ZK[n % 3]
                    src = W["w_in"][bass.ds(l, 1), k0 * P:k1 * P, c * ZC:(c + 1) * ZC].rearrange("l (k p) c -> p (l k) c", p=P)
                    load(e, n, n % RAW, src, shape=(k1 - k0, ZC), first=n < RAW)
                else:
                    c = n - NZ
                    src = W["mla_w_uq"][bass.ds(l, 1), :, c * UC:(c + 1) * UC].rearrange("l (k p) c -> p (l k) c", p=P)
                    load(e, n, n % RAW, src, shape=(2, UC))
            e.wait_ge(S.rope_done, 6)
            e.wait_ge(S.norm_kv, TILES)
            for pr, sm, lo_, hi_, at in (("dsa_p", "dsa_s", Z_AK, Z_IQ, 0), ("dsa_p", "dsa_s", Z_IK, Z_IW, 2 * AD),
                                         ("mla_p", "mla_s", Z_CKV, N_IN, 0)):
                w = hi_ - lo_
                e.dma_start(O[pr][bass.ds(l, 1), 0, 0:S0, at:at + w].rearrange("l (t p) c -> p (l t) c", p=P),
                            z[:, 0:4, lo_:hi_]).then_inc(S.rows_out, 16)
                e.dma_start(O[pr][bass.ds(l, 1), 0, S0:PROMPT, at:at + w].rearrange("l p c -> (l p) c"),
                            z[SAMPLE:ROWS[4], 4, lo_:hi_]).then_inc(S.rows_out, 16)
                e.dma_start(O[sm][bass.ds(l, 1), :, :, at:at + w].rearrange("l b t c -> (l b t) c"),
                            z[0:SAMPLE, 4, lo_:hi_]).then_inc(S.rows_out, 16)
            e.wait_ge(S.iw_done, 1)
            e.dma_start(O["iw_scratch"][:, :], T.iw[0:SAMPLE, 4, :]).then_inc(S.rows_out, 16)
            e.wait_ge(S.rows_out, 160)
            e.wait_ge(S.norm_q, TILES)
            for h in range(IH):
                for b2 in range(2):
                    e.dma_start(T.wcol[64 * b2 + 8 * h:64 * b2 + 8 * h + 8, :],
                                O["iw_scratch"].rearrange("(b t) h -> t b h", t=DEC_T)[:, :, h:h + 1]
                                .rearrange("t b h -> t (b h)"), allow_slow_non_contiguous=True)\
                     .then_inc(S.rows_back, 16)
            e.wait_ge(S.rows_back, 16 * 16)

        @block.gpsimd
        def _(e):
            e.wait_ge(S.rope_done, 2)
            for i in range(2):
                e.tensor_copy(T.kdup[:, :, i, :], z[:, :, Z_AK:Z_AV]).then_inc(S.kdup_done, 1)
            e.wait_ge(S.rope_done, 4)
            e.tensor_copy(T.comb[:, :, :, 0:ID], z[:, :, Z_IQ:Z_IK].rearrange("p t (h c) -> p t h c", h=IH))\
             .then_inc(S.icomb_done, 1)
            for i in range(2):
                e.tensor_copy(T.kcomb[:, :, i, 0:ID], z[:, :, Z_IK:Z_IW]).then_inc(S.kcomb_done, 1)
            e.tensor_scalar(T.iw[:, :, :], z[:, :, Z_IW:Z_CQ], IW_SCALE, 1.0, ALU.mult, ALU.mult).then_inc(S.iw_done, 1)
            e.wait_ge(S.rope_done, 6)
            for i in range(2):
                e.tensor_copy(T.kcomb[:, :, i, ID:ID + PE_D], z[:, :, Z_KPE:N_IN]).then_inc(S.kcomb_done, 1)
            e.wait_ge(S.rope_done, 8)
            e.wait_ge(S.w_used, NZ + 2)
            e.wait_ge(S.turned, len(g1))
            zs = z[0:SAMPLE, 4, :]
            nst = 0

            def halves(hi_dst, lo_dst, src, shape=None):
                nonlocal nst
                e.tensor_copy(hi_dst, src).then_inc(S.stacked, 1)
                nst += 1
                e.wait_ge(S.stacked, nst)
                e.tensor_tensor(lo_dst, src, hi_dst.bitcast(F32), ALU.subtract).then_inc(S.stacked, 1)
                nst += 1

            def four(dst, src, heads):
                return src.unsqueeze(2).to_broadcast([SAMPLE, heads, 2, 32])

            halves(T.sA[:, :, 0:AD], T.sA[:, :, AD:P], zs[:, 0:Z_AK].rearrange("p (h c) -> p h c", h=AH))
            for dst, c in ((T.sI, 0), (T.sP, ID)):
                v = dst[:, :, :].rearrange("p h (a b c) -> p h a b c", a=2, b=2)
                halves(v[:, :, :, 0], v[:, :, :, 1], four(dst, T.comb[0:SAMPLE, 4, :, c:c + 32], 8))
            halves(T.sN[:, 0, 0:AD], T.sN[:, 0, AD:P], zs[:, Z_AK:Z_AV])
            for i, c in ((1, Z_IK), (2, Z_KPE)):
                v = T.sN[:, i, :].rearrange("p (a b c) -> p a b c", a=2, b=2)
                halves(v[:, 0], v[:, 1], zs[:, c:c + 32].unsqueeze(1).to_broadcast([SAMPLE, 2, 32]))
            e.wait_ge(S.stacked, nst)
            e.tensor_copy(T.sB[:, :, 0:AD], T.sA[:, :, AD:P].bitcast(F32)).then_inc(S.sb_done, 1)
            e.tensor_copy(T.sB[:, :, AD:P], T.sA[:, :, 0:AD].bitcast(F32)).then_inc(S.sb_done, 1)

        @block.scalar
        def _(e):
            def z_out(c):
                for t in range(0, TILES, 2):
                    if c == 0 and t == 0:
                        e.wait_ge(S.pad_zero, 1)
                        e.wait_ge(S.w_used, 3)
                    elif t == 0:
                        e.wait_ge(S.w_used, 3 * c + 3)
                    r = ROWS[t]
                    e.activation(z[0:r, t, c * ZC:(c + 1) * ZC], T.ps[0:r, (5 * c + t) % 8, 0:ZC], ACT.Copy)\
                     .then_inc(S.z_act, 1)
            for n in range(NZ + 2):
                w = (ZK[n % 3][1] - ZK[n % 3][0]) * ZC if n < NZ else QB
                hi(e, n, n % RAW, n // RAW, width=w, first=n < SPLIT)
                if n >= 4 and (n - 4) % 3 == 0:
                    z_out((n - 4) // 3)
            e.wait_ge(S.z_act, 12)
            e.wait_ge(S.z_dve, 8)
            for i, (c0, c1) in enumerate(((Z_CQ, Z_CKV), (Z_CKV, Z_KPE))):
                for t in tiles:
                    e.activation(T.ps[:, t, QL * i:QL * i + c1 - c0], z[:, t, c0:c1], ACT.Square,
                                 accum_out=T.ssq[:, 5 * i + t:5 * i + t + 1]).then_inc(S.sq_done, 1)
            for i, w in enumerate((QL, RL)):
                e.wait_ge(S.sq_done, 5 * i + 5)
                e.activation(T.sstd[:, 5 * i:5 * i + 5], T.ssq[:, 5 * i:5 * i + 5], ACT.Sqrt, scale=1.0 / w,
                             bias=T.eps[:, 1:2]).then_inc(S.rms_std, 1)
            for gi in range(len(g1)):
                out(e, gi, "act")
            for c in range(2):
                e.wait_ge(S.w_used, NZ + 1 + c)
                if c == 0:
                    e.wait_ge(S.pad_zero, 2)
                for t in (0, 2, 4):
                    r = ROWS[t]
                    q_out(lambda d, s_: e.activation(d, s_, ACT.Copy).then_inc(S.qb_act, 1), c, t)
            for gi in range(len(g1), len(groups)):
                out(e, gi, "act")
            for h in range(BH):
                e.wait_ge(S.qlat_ps, h + 1)
                b = 2 * (h % 4)
                e.activation(T.qlatT[:, h, :].rearrange("p (a c) -> p a c", a=2), T.ps[:, b:b + 2, 0:HALF], ACT.Copy)\
                 .then_inc(S.qlat_done, 1)
            e.wait_ge(S.qlat_done, BH)
            e.wait_ge(S.late_done, 2)
            e.wait_ge(S.turned_dve, ndve)
            for half in range(2):
                src = T.qlatT[:, :, S0:TAIL].rearrange("p h (b u t) -> p b u h t", u=2, t=DEC_T)[:, :, half]
                e.activation(half_cols(T.QLh, half), src, ACT.Copy).then_inc(S.late_done, 1)
            e.activation(T.newcT[:, 0, :], T.ckvT[:, S0:TAIL], ACT.Copy).then_inc(S.late_done, 1)

        @block.vector
        def _(e):
            step = [0]

            def chain(ins):
                step[0] += 1
                ins.then_inc(S.dve_step, 1)
                e.wait_ge(S.dve_step, step[0])

            def z_out(c):
                for t in (1, 3):
                    if t == 1:
                        e.wait_ge(S.w_used, 3 * c + 3)
                    e.tensor_copy(z[:, t, c * ZC:(c + 1) * ZC], T.ps[:, (5 * c + t) % 8, 0:ZC]).then_inc(S.z_dve, 1)

            def rope(x, heads, half, off, dst):
                def table(o):
                    return T.rope[:, :, o:o + half].unsqueeze(2).to_broadcast([P, TILES, heads, half])
                n = TILES * heads * half
                m = [t[:, 0:n].rearrange("p (t h c) -> p t h c", t=TILES, h=heads) for t in T.tmp]
                x1, x2 = x[:, :, :, 0:half], x[:, :, :, half:2 * half]
                cos, sin = table(off), table(ROPE_W + off)
                e.tensor_tensor(m[0], x1, cos, ALU.mult)
                e.tensor_tensor(m[1], x2, sin, ALU.mult)
                chain(e.tensor_tensor(m[2], x1, sin, ALU.mult))
                chain(e.tensor_tensor(m[0], m[0], m[1], ALU.subtract))
                chain(e.tensor_tensor(m[1], x2, cos, ALU.mult))
                e.tensor_copy(dst[:, :, :, 0:half], m[0]).then_inc(S.rope_done, 1)
                e.tensor_tensor(dst[:, :, :, half:2 * half], m[1], m[2], ALU.add).then_inc(S.rope_done, 1)
                rope.n += 2
                e.wait_ge(S.rope_done, rope.n)
            rope.n = 0

            e.memset(z[64:P, 4, :], 0.0).then_inc(S.pad_zero, 1)
            e.memset(T.qpe[64:P, 4, :, :], 0.0).then_inc(S.pad_zero, 1)
            for n in range(NZ + 2):
                w = (ZK[n % 3][1] - ZK[n % 3][0]) * ZC if n < NZ else QB
                lo(e, n, n % RAW, width=w)
                if n >= 4 and (n - 4) % 3 == 0:
                    z_out((n - 4) // 3)
            e.wait_ge(S.z_act, 12)
            e.wait_ge(S.z_dve, 8)
            v = z[:, :, 0:Z_AV].rearrange("p t (h c) -> p t h c", h=AH + 1)
            rope(v, AH + 1, AROT // 2, 0, v)
            v = z[:, :, Z_IQ:Z_IW].rearrange("p t (h c) -> p t h c", h=IH + 1)
            rope(v, IH + 1, IROT // 2, AROT // 2, v)
            v = z[:, :, Z_KPE:N_IN].rearrange("p t (h c) -> p t h c", h=1)
            rope(v, 1, PE_D // 2, AROT // 2 + IROT // 2, v)
            for i, (c0, c1, s) in enumerate(((Z_CQ, Z_CKV, S.norm_q), (Z_CKV, Z_KPE, S.norm_kv))):
                e.wait_ge(S.rms_std, i + 1)
                e.reciprocal(T.srstd[:, 5 * i:5 * i + 5], T.sstd[:, 5 * i:5 * i + 5]).then_inc(S.rms_rstd, 1)
                e.wait_ge(S.rms_rstd, i + 1)
                if i == 0:
                    e.wait_ge(S.par_in, 64)
                for t in tiles:
                    e.scalar_tensor_tensor(z[:, t, c0:c1], z[:, t, c0:c1], T.srstd[:, 5 * i + t:5 * i + t + 1],
                                           T.gains[:, c0 - Z_CQ:c1 - Z_CQ], ALU.mult, ALU.mult).then_inc(s, 1)
            for gi in range(len(g1)):
                out(e, gi, "dve")
            for c in range(2):
                e.wait_ge(S.w_used, NZ + 1 + c)
                for t in (1, 3):
                    q_out(lambda d, s_: e.tensor_copy(d, s_).then_inc(S.qb_dve, 1), c, t)
            e.wait_ge(S.qb_act, 12)
            e.wait_ge(S.qb_dve, 8)
            rope(T.qpe[:, :, :, :], BH, PE_D // 2, AROT // 2 + IROT // 2, T.comb[:, :, :, ID:ID + PE_D])
            for gi in range(len(g1), len(groups)):
                if gi == len(g1) + 8:
                    e.wait_ge(S.turned, gi)
                    e.wait_ge(S.stacked, 6)
                    for q in (T.QA, T.QB, T.QI, T.QP):
                        e.memset(q[:, :, :].bitcast(F32), 0.0).then_inc(S.stack_zero, 1)
                out(e, gi, "dve")
            for q in (T.QLh, T.QLl):
                e.memset(q[:, :, :].bitcast(F32), 0.0).then_inc(S.late_done, 1)
            e.wait_ge(S.late_done, 5)
            for half in range(2):
                src = T.qlatT[:, :, S0:TAIL].rearrange("p h (b u t) -> p b u h t", u=2, t=DEC_T)[:, :, half]
                e.tensor_tensor(half_cols(T.QLl, half), src, half_cols(T.QLh, half).bitcast(F32), ALU.subtract)
            e.tensor_tensor(T.newcT[:, 1, :], T.ckvT[:, S0:TAIL], T.newcT[:, 0, :].bitcast(F32), ALU.subtract)

        @block.tensor
        def _(e):
            for n in range(NZ):
                c, (k0, k1) = n // 3, ZK[n % 3]
                s = n % SPLIT
                e.wait_ge(S.split_done, n + 1)
                for t in tiles:
                    ev = 5 * c + t
                    if n % 3 == 0 and ev >= 8:
                        z_free(e, ev - 8)
                    o = slice(t * P, t * P + ROWS[t])
                    for k in range(k0, k1):
                        w = slice((k - k0) * ZC, (k - k0 + 1) * ZC)
                        mm = three(e, T.ps[0:ROWS[t], ev % 8, 0:ZC], T.xth[:, k, o], T.xtl[:, k, o],
                                   T.whi[:, s, w], T.wlo[:, s, w], k == 0, k == KD - 1)
                mm.then_inc(S.w_used, 1)
            for gi in range(len(g1)):
                if gi == 0:
                    e.wait_ge(S.z_act, 12)
                    e.wait_ge(S.z_dve, 8)
                    e.wait_ge(S.sq_done, 10)
                turn(e, gi, gi - 4 if gi >= 4 else None)
            for gi in range(len(g1) - 4, len(g1)):
                e.wait_ge(S.all[outs[gi][0]], outs[gi][1])
            for c in range(2):
                n = NZ + c
                s = n % SPLIT
                e.wait_ge(S.split_done, n + 1)
                e.wait_ge(S.cql_done, 2)
                for t in tiles:
                    if 5 * c + t >= 8:
                        e.wait_ge(S.qb_act, 2)
                        e.wait_ge(S.qb_dve, 2)
                    o = slice(t * P, t * P + ROWS[t])
                    for k in range(2):
                        w = slice(k * UC, (k + 1) * UC)
                        mm = three(e, T.ps[0:ROWS[t], (5 * c + t) % 8, 0:UC], T.cqh[:, k, o], T.cql[:, k, o],
                                   T.whi[:, s, w], T.wlo[:, s, w], k == 0, k == 1)
                mm.then_inc(S.w_used, 1)
            e.wait_ge(S.qb_act, 12)
            e.wait_ge(S.qb_dve, 8)
            for gi in range(len(g1), len(groups)):
                turn(e, gi, gi - 4 if gi >= len(g1) + 4 else None)
            for gi in range(len(groups) - 5, len(groups)):
                e.wait_ge(S.all[outs[gi][0]], outs[gi][1])
            for h in range(BH):
                if h >= 4:
                    e.wait_ge(S.qlat_done, h - 3)
                base = 64 * (h % 2)
                for a in range(2):
                    mm = e.matmul(T.ps[:, 2 * (h % 4) + a, 0:HALF], T.wukT[base:base + NOPE, h // 2, :],
                                  T.qnT[base:base + NOPE, h // 2, a * HALF:(a + 1) * HALF], start=True, stop=True)
                mm.then_inc(S.qlat_ps, 1)
    nc.all_engine_barrier(sems_to_clear=S.range)


PROMPT_SEMS = ["s_round_max", "s_round_done", "tail_in", "tri_set", "s_ps", "s_read", "scored", "max_done", "nmax_done", "round_max", "round_done",
               "biased", "bias_done", "b_ps", "b_out", "pv_done", "rinv_done", "o_done", "mix_lo", "mix_hi"]
ROUNDS = (TOPK_P + 7) // 8
GIVEN = ROUNDS * 8 - TOPK_P
QT = [P, P, P, P, PROMPT - 4 * P]
QC = [0, P, 2 * P, 3 * P, TAIL]
NK = [P, 2 * P, 3 * P, 4 * P, PROMPT]
D_SCALE = AD ** -0.5
M_SCALE = (NOPE + PE_D) ** -0.5


def prompt_block(nc, T, S):
    units = [(kind, t, h) for t in range(5) for kind in "MD" for h in range(8)]
    rounds = [3, 3, 3, 3, 3, 2, 0, 0]
    assert sum(rounds) == ROUNDS
    n = len(units)
    A = Map(T.nc, T.raw_at)
    Pb = T.M.put("pP", [P, 3, PROMPT], F32, A.region(3 * PROMPT * 4))
    PT = T.M.put("pPT", [P, 2, 512], F32, A.region(2 * 512 * 4))
    work = T.M.put("pwork", [P, GIVEN + PROMPT], F32, A.region((GIVEN + PROMPT) * 4))
    relu = T.M.put("prelu", [P, 2, PROMPT], F32, A.region(2 * PROMPT * 4))
    osb = T.M.put("posb", [P, 1024], F32, A.region(4096))
    olT = T.M.put("polT", [P, 8, P], F32, A.region(4096))
    bias = T.M.put("pbias", [P, PROMPT], BF16, A.region(PROMPT * 2))
    vt = T.M.put("pvt", [P, AD + RL], F32, A.region((AD + RL) * 4))
    iwt = T.M.put("piwt", [P, IH], F32, A.region(IH * 4))
    tri = T.M.put("ptri", [P, P], F32, A.region(P * 4))
    mx = T.M.put("pmx", [P, 3], F32, A.region(12))
    nmx = T.M.put("pnmx", [P, 3], F32, A.region(12))
    stop = T.M.put("stop", [SAMPLE, 8], F32, A.region(32))
    top = T.M.put("ptop", [P, 8], F32, A.region(32))
    rsum = T.M.put("prsum", [P, 2, 8], F32, A.region(64))
    rinv = T.M.put("prinv", [P, 2, 8], F32, A.region(64))
    assert A.top <= T.gb_at - 4096
    flat = T.ps[:, :, :].rearrange("p b c -> p (b c)")
    SB = lambda s, r, w: flat[0:r, (s % 2) * 1024:(s % 2) * 1024 + w]
    BB = lambda q: flat[:, (4 + q % 2) * 512:(5 + q % 2) * 512]

    plan, s_job, b_job = [], 0, 0
    b_kind = []
    lag = n + 6
    last = {}
    for i in range(lag):
        p = dict(idx=None, s=None, t=None, pv=None, norm=None, ot=[], uv=None)
        if i < n:
            kind, t, h = units[i]
            if kind == "D" and t < 4:
                p["idx"] = (s_job, t + 1, h)
                s_job += 1
            p["s"] = s_job
            s_job += 1
            if h == 7:
                last[i] = (kind, t)
        if 0 <= i - 1 < n:
            p["t"] = b_job
            b_kind.append("P")
            b_job += 1
        if 0 <= i - 2 < n:
            p["pv"] = i - 2
        if i - 2 in last:
            p["norm"] = last[i - 2]
        if i - 3 in last:
            kind, t = last[i - 3]
            for a in range(2 if kind == "M" else 1):
                p["ot"].append((b_job, kind, t, a))
                b_kind.append("O" if kind == "M" else "X")
                b_job += 1
        if i - 4 in last and last[i - 4][0] == "M":
            p["uv"] = (b_job, last[i - 4][1])
            b_kind.append("X")
            b_job += 1
        plan.append(p)
    tjob = {i - 1: p["t"] for i, p in enumerate(plan) if p["t"] is not None}

    def b_free(e, q):
        if q < 2:
            return
        kinds = b_kind[:q - 1]
        if kinds[-1] == "X":
            e.wait_ge(S.mix_lo, kinds.count("X"))
        else:
            e.wait_ge(S.b_out, len(kinds) - kinds.count("X"))

    def groups_before(i):
        return sum(1 for g in last if g <= i)

    def keys(t):
        return [(0, 0, min(NK[t], 512))] + ([(512, TAIL, 16)] if t == 4 else [])

    def key_tiles(t):
        return [(k, P) for k in range(min(t + 1, 4))] + ([(4, 16)] if t == 4 else [])

    with nc.Block() as block:
        @block.sync
        def _(e):
            src = T.z[SAMPLE:ROWS[4], 4, :]
            e.dma_start(vt[0:16, 0:AD], src[:, Z_AV:Z_IQ]).then_inc(S.tail_in, 16)
            e.dma_start(vt[0:16, AD:AD + RL], src[:, Z_CKV:Z_KPE]).then_inc(S.tail_in, 16)
            e.dma_start(iwt[0:16, :], T.iw[SAMPLE:ROWS[4], 4, :]).then_inc(S.tail_in, 16)

        @block.gpsimd
        def _(e):
            e.tensor_copy(tri[:, :], T.trib[:, :]).then_inc(S.tri_set, 1)
            e.memset(work[:, 0:GIVEN], 3.0e38).then_inc(S.tri_set, 1)
            for t in range(1, 4):
                e.wait_ge(S.biased, t)
                e.memset(work[:, 0:GIVEN], 3.0e38).then_inc(S.tri_set, 1)

        @block.tensor
        def _(e):
            for i, p in enumerate(plan):
                if p["idx"]:
                    s, t, h = p["idx"]
                    if s >= 2:
                        e.wait_ge(S.s_read, s - 1)
                    r, b = QT[t], 64 * (h % 2)
                    for c, k0, w in keys(t):
                        mm = e.matmul(SB(s, r, PROMPT)[:, c:c + w], T.combT[b:b + ID, h // 2, QC[t]:QC[t] + r],
                                      T.kcT[b:b + ID, k0:k0 + w], start=True, stop=True)
                    mm.then_inc(S.s_ps, 1)
                if p["s"] is not None:
                    kind, t, h = units[i]
                    s = p["s"]
                    r, q, b = QT[t], slice(QC[t], QC[t] + QT[t]), 64 * (h % 2)
                    if s >= 2:
                        e.wait_ge(S.s_read, s - 1)
                    if kind == "D" and h == 0:
                        e.wait_ge(S.bias_done, t + 1)
                    for c, k0, w in keys(t):
                        out = SB(s, r, PROMPT)[:, c:c + w]
                        if kind == "M":
                            e.matmul(out, T.qlatT[:, h, q], T.ckvT[:, k0:k0 + w], start=True, stop=False)
                            diag = t if t < 4 else (4 if c else None)
                            mm = e.matmul(out, T.combT[b + 32:b + 64, h // 2, q], T.kcT[b + 32:b + 64, k0:k0 + w],
                                          start=False, stop=diag is None)
                            if diag is not None:
                                d = SB(s, r, PROMPT)[:, diag * P:diag * P + r]
                                mm = e.matmul(d, T.identb[:, 0:r], T.trib[:, 0:r], start=False, stop=True)
                        else:
                            e.matmul(out, T.qaT[b:b + AD, h // 2, q], T.kT2[b:b + AD, k0:k0 + w], start=True, stop=False)
                            mm = e.matmul(out, T.identb[:, 0:r], bias[:, c:c + w], start=False, stop=True)
                    mm.then_inc(S.s_ps, 1)
                if p["t"] is not None:
                    u = i - 1
                    kind, t, h = units[u]
                    q = p["t"]
                    e.wait_ge(S.s_read, plan[u]["s"] + 1)
                    b_free(e, q)
                    r = QT[t]
                    for k, kr in key_tiles(t):
                        mm = e.transpose(BB(q)[0:kr, k * P:k * P + r] if t < 4 else BB(q)[0:kr, k * 16:k * 16 + 16],
                                         Pb[0:r, u % 3, k * P:k * P + kr], T.ident[0:r, 0:r])
                    mm.then_inc(S.b_ps, 1)
                if p["pv"] is not None:
                    u = p["pv"]
                    kind, t, h = units[u]
                    q = tjob[u]
                    e.wait_ge(S.b_out, sum(1 for x in b_kind[:q + 1] if x != "X"))
                    if h == 0 and u > 0:
                        e.wait_ge(S.o_done, groups_before(u - 1))
                    r = QT[t]
                    w, at = (RL, Z_CKV) if kind == "M" else (AD, Z_AV)
                    kts = key_tiles(t)
                    if t == 4:
                        e.wait_ge(S.tail_in, 48)
                    for k, kr in kts:
                        lhs = PT[0:kr, u % 2, k * P:k * P + r] if t < 4 else PT[0:kr, u % 2, k * 16:k * 16 + 16]
                        if k < 4:
                            v = T.z[0:kr, k, at:at + w]
                        else:
                            v = vt[0:16, 0:AD] if kind == "D" else vt[0:16, AD:AD + RL]
                        mm = e.matmul(flat[0:r, 6 * 512 + h * w:6 * 512 + (h + 1) * w], lhs, v,
                                      start=k == kts[0][0], stop=k == kts[-1][0])
                    mm.then_inc(S.pv_done, 1)
                for q, kind, t, a in p["ot"]:
                    r = QT[t]
                    e.wait_ge(S.o_done, groups_before(i - 3))
                    b_free(e, q)
                    for k in range(4):
                        c = (4 * a + k) * P
                        mm = e.transpose(BB(q)[:, k * P:k * P + r], osb[0:r, c:c + P], T.ident[0:r, 0:r])
                    mm.then_inc(S.b_ps, 1)
                if p["uv"]:
                    q, t = p["uv"]
                    r = QT[t]
                    b_free(e, q)
                    e.wait_ge(S.b_out, sum(1 for x in b_kind[:q] if x != "X"))
                    for h in range(8):
                        b = 64 * (h % 2)
                        mm = e.matmul(BB(q)[b:b + VD, (h // 2) * P:(h // 2) * P + r], T.wuv[:, h, :], olT[:, h, 0:r],
                                      start=True, stop=True)
                    mm.then_inc(S.b_ps, 1)

        def mix(t, kind):
            return slice(4 if kind == "M" else 0, 8 if kind == "M" else 4), slice(QC[t], QC[t] + QT[t])

        @block.scalar
        def _(e):
            nx = [0]

            def mix_hi(q, kind, t):
                k, c = mix(t, kind)
                e.wait_ge(S.b_ps, q + 1)
                nx[0] += 1
                e.activation(T.xth[:, k, c], BB(q).rearrange("p (k c) -> p k c", k=4)[:, :, 0:QT[t]], ACT.Copy)\
                 .then_inc(S.mix_hi, 1)

            for i, p in enumerate(plan):
                if p["idx"]:
                    s, t, h = p["idx"]
                    j = 8 * (t - 1) + h
                    e.wait_ge(S.s_ps, s + 1)
                    if j >= 2:
                        e.wait_ge(S.scored, j - 1)
                    e.activation(relu[0:QT[t], j % 2, 0:NK[t]], SB(s, QT[t], NK[t]), ACT.Relu).then_inc(S.s_read, 1)
                if p["s"] is not None:
                    kind, t, h = units[i]
                    r = QT[t]
                    e.wait_ge(S.nmax_done, i + 1)
                    if i >= 3:
                        e.wait_ge(S.b_ps, tjob[i - 3] + 1)
                    e.activation(Pb[0:r, i % 3, 0:NK[t]], SB(p["s"], r, NK[t]), ACT.Exp, bias=nmx[0:r, i % 3:i % 3 + 1],
                                 scale=M_SCALE if kind == "M" else D_SCALE,
                                 accum_out=rsum[0:r, 0 if kind == "M" else 1, h:h + 1]).then_inc(S.s_read, 1)
                if p["t"] is not None:
                    u, q = i - 1, p["t"]
                    kind, t, h = units[u]
                    e.wait_ge(S.b_ps, q + 1)
                    if u >= 2:
                        e.wait_ge(S.pv_done, u - 1)
                    if t < 4:
                        e.activation(PT[:, u % 2, 0:NK[t]], BB(q)[:, 0:NK[t]], ACT.Copy).then_inc(S.b_out, 1)
                    else:
                        e.activation(PT[:, u % 2, 0:64], BB(q)[:, 0:64], ACT.Copy)
                        e.activation(PT[0:16, u % 2, 64:80], BB(q)[0:16, 64:80], ACT.Copy).then_inc(S.b_out, 1)
                for q, kind, t, a in p["ot"]:
                    if kind == "D":
                        mix_hi(q, kind, t)
                    else:
                        e.wait_ge(S.b_ps, q + 1)
                        e.activation(olT[:, 4 * a:4 * a + 4, 0:QT[t]],
                                     BB(q).rearrange("p (k c) -> p k c", k=4)[:, :, 0:QT[t]], ACT.Copy).then_inc(S.b_out, 1)
                if p["uv"]:
                    mix_hi(p["uv"][0], "M", p["uv"][1])

        @block.vector
        def _(e):
            nround, nlo, nsround = [0], [0], [0]

            def mix_lo(q, kind, t):
                k, c = mix(t, kind)
                nlo[0] += 1
                e.wait_ge(S.mix_hi, nlo[0])
                e.tensor_tensor(T.xtl[:, k, c], BB(q).rearrange("p (k c) -> p k c", k=4)[:, :, 0:QT[t]],
                                T.xth[:, k, c].bitcast(F32), ALU.subtract).then_inc(S.mix_lo, 1)

            e.wait_ge(S.tri_set, 2)
            e.memset(bias[:, 4 * P:PROMPT], 0.0)
            e.tensor_copy(bias[:, 0:P], T.trib[:, :]).then_inc(S.bias_done, 1)
            for i, p in enumerate(plan):
                if p["idx"]:
                    s, t, h = p["idx"]
                    r = QT[t]
                    e.wait_ge(S.s_read, s + 1)
                    w = T.iw[0:r, t, h:h + 1] if t < 4 else iwt[0:r, h:h + 1]
                    if t == 4 and h == 0:
                        e.wait_ge(S.tail_in, 48)
                    sc, re = work[0:r, GIVEN:GIVEN + NK[t]], relu[0:r, (8 * (t - 1) + h) % 2, 0:NK[t]]
                    if h == 0:
                        if t > 1:
                            e.wait_ge(S.biased, t - 1)
                        e.tensor_scalar(sc, re, w, None, ALU.mult).then_inc(S.scored, 1)
                    else:
                        e.wait_ge(S.scored, 8 * (t - 1) + h)
                        e.scalar_tensor_tensor(sc, re, w, sc, ALU.mult, ALU.add).then_inc(S.scored, 1)
                if i < n:
                    kind, t, h = units[i]
                    r = QT[t]
                    e.wait_ge(S.s_ps, p["s"] + 1)
                    if i >= 3:
                        e.wait_ge(S.s_read, plan[i - 3]["s"] + 1)
                    e.tensor_reduce(mx[0:r, i % 3:i % 3 + 1], SB(p["s"], r, NK[t]), AX, ALU.max).then_inc(S.max_done, 1)
                    e.wait_ge(S.max_done, i + 1)
                    e.tensor_scalar(nmx[0:r, i % 3:i % 3 + 1], mx[0:r, i % 3:i % 3 + 1],
                                    -(M_SCALE if kind == "M" else D_SCALE), None, ALU.mult).then_inc(S.nmax_done, 1)
                    if kind == "M" and t > 0:
                        ww = work[0:r, 0:GIVEN + NK[t]]
                        if h == 0:
                            d = work[0:r, GIVEN + t * P:GIVEN + t * P + r]
                            e.wait_ge(S.scored, 8 * t)
                            e.tensor_tensor(d, d, tri[0:r, 0:r], ALU.add).then_inc(S.round_done, 1)
                            nround[0] += 1
                            e.wait_ge(S.tri_set, t + 1)
                            e.wait_ge(S.round_done, nround[0])
                        for _ in range(rounds[h]):
                            e.max(top[0:r, :], ww).then_inc(S.round_max, 1)
                            e.wait_ge(S.round_max, nround[0] - (t - 1))
                            e.match_replace(ww, top[0:r, :], ww, TAKEN).then_inc(S.round_done, 1)
                            nround[0] += 1
                            e.wait_ge(S.round_done, nround[0])
                        if h == 7:
                            e.tensor_scalar(bias[0:r, 0:NK[t]], work[0:r, GIVEN:GIVEN + NK[t]], 2 / 3 * TAKEN, NEG,
                                            ALU.is_gt, ALU.mult).then_inc(S.biased, 1)
                            e.wait_ge(S.biased, t)
                            d = bias[0:r, t * P:t * P + r]
                            e.tensor_tensor(d, d, T.trib[0:r, 0:r], ALU.add).then_inc(S.bias_done, 1)
                if i < n and units[i][1] in (2, 3):
                    e.max(stop[:, :], T.score[:, :]).then_inc(S.s_round_max, 1)
                    e.wait_ge(S.s_round_max, nsround[0] + 1)
                    e.match_replace(T.score[:, :], stop[:, :], T.score[:, :], TAKEN).then_inc(S.s_round_done, 1)
                    nsround[0] += 1
                    e.wait_ge(S.s_round_done, nsround[0])
                if p["norm"]:
                    kind, t = p["norm"]
                    r = QT[t]
                    g = groups_before(i - 2)
                    a = 0 if kind == "M" else 1
                    w = RL if kind == "M" else AD
                    e.wait_ge(S.pv_done, i - 1)
                    e.reciprocal(rinv[0:r, a, :], rsum[0:r, a, :]).then_inc(S.rinv_done, 1)
                    e.wait_ge(S.rinv_done, g)
                    if g >= 2:
                        prev = [q for pp in plan[:i] for q, *_ in pp["ot"]]
                        e.wait_ge(S.b_ps, prev[-1] + 1)
                    e.tensor_tensor(osb[0:r, 0:8 * w].rearrange("p (h c) -> p h c", h=8),
                                    flat[0:r, 6 * 512:6 * 512 + 8 * w].rearrange("p (h c) -> p h c", h=8),
                                    rinv[0:r, a, :].unsqueeze(2).to_broadcast([r, 8, w]), ALU.mult).then_inc(S.o_done, 1)
                for q, kind, t, a in p["ot"]:
                    if kind == "D":
                        mix_lo(q, kind, t)
                if p["uv"]:
                    mix_lo(p["uv"][0], "M", p["uv"][1])
    nc.all_engine_barrier(sems_to_clear=S.range)


SKEYS = PAST + DEC_T
INDEX_SEMS = ["page_in0", "page_in1", "page_in2", "page_in3", "w_zero", "w_set", "kh_done", "kl_done", "turned",
              "out_act", "out_dve", "dots_done", "relu_done", "weighed", "scored", "newv_in"]


def page_loads(e, T, l, r, dst, sources, sem):
    with e.Fori(0, PAGES) as i:
        page = e.value_load(T.pages[0:1, bass.ds(r * PAGES + i, 1)], min_val=0, max_val=POOL_PAGES - 1)
        for cache, c0, c1, at in sources:
            e.dma_start(dst[:, bass.ds(i, 1), at:at + c1 - c0].rearrange("p i c -> p (i c)"),
                        cache[bass.ds(l, 1), bass.ds(page, 1), :, c0:c1].rearrange("l n p c -> (l n p) c"))\
             .then_inc(sem, 16)


def index_block(nc, T, S, l, cache_dsa):
    A = Map(T.nc, T.raw_at)
    ks = T.M.put("iks", [P, 2, PAGES, P], F32R, A.region(2 * PAGES * P * 4))
    ip = T.M.put("ip", [P, 3, PAGES, ID], F32, A.region(3 * PAGES * ID * 4))
    X = Map(T.nc, T.xth_at)
    kT = T.M.put("ikT", [P, 2, PAST], F32R, X.region(2 * PAST * 4))
    R = T.M.put("irelu", [P, SKEYS], F32, X.region(SKEYS * 4))
    wall = T.M.put("wall", [P, DEC_B // 2, SAMPLE], F32, X.region(DEC_B // 2 * SAMPLE * 4))
    T.score = T.M.put("score", [SAMPLE, SKEYS], F32, T.score_at)
    flat = T.ps[:, :, :].rearrange("p b c -> p (b c)")
    page_in = [S.page_in0, S.page_in1, S.page_in2]
    jobs = [(r, g) for r in range(DEC_B) for g in range(4)]

    def freed(e, q):
        if q >= 0:
            e.wait_ge(S.out_dve if jobs[q][1] % 2 else S.out_act, q // 2 + 1)

    with nc.Block() as block:
        @block.sync
        def _(e):
            for r in range(DEC_B):
                if r >= 3:
                    e.wait_ge(S.kl_done, r - 2)
                page_loads(e, T, l, r, ip[:, r % 3, :, :], [(cache_dsa, 2 * AD, ROW, 0)], page_in[r % 3])

        @block.tensor
        def _(e):
            def turn(r):
                e.wait_ge(S.kl_done, r + 1)
                for g in range(4):
                    q = 4 * r + g
                    freed(e, q - 3)
                    for k in range(4):
                        mm = e.transpose(T.ps[:, 5 + q % 3, k * P:(k + 1) * P], ks[:, r % 2, 4 * g + k, :].bitcast(F32),
                                         T.ident[:, :])
                    mm.then_inc(S.turned, 1)

            def dots(r):
                if r % 2 == 0 and r > 0:
                    e.wait_ge(S.scored, r // 2)
                e.wait_ge(S.out_act, 2 * r + 2)
                e.wait_ge(S.out_dve, 2 * r + 2)
                for c in range(5):
                    out = T.ps[:, c, :] if c < 4 else T.ps[:, 4, 0:DEC_T]
                    rhs = kT[:, r % 2, c * 512:(c + 1) * 512] if c < 4 else T.newT[:, 1, r * DEC_T:(r + 1) * DEC_T]
                    mm = e.matmul(out, T.QI[:, r, :], rhs, start=r % 2 == 0, stop=r % 2 == 1)
                mm.then_inc(S.dots_done, 1)

            def weigh(p):
                e.wait_ge(S.relu_done, p + 1)
                if p == 0:
                    e.wait_ge(S.w_set, DEC_B)
                for c in range(5):
                    w = 512 if c < 4 else DEC_T
                    mm = e.matmul(T.ps[0:SAMPLE, c, 0:w], wall[:, p, :], R[:, c * 512:c * 512 + w], start=True, stop=True)
                mm.then_inc(S.weighed, 1)
            turn(0)
            turn(1)
            for p in range(DEC_B // 2):
                dots(2 * p)
                dots(2 * p + 1)
                for r in (2 * p + 2, 2 * p + 3):
                    if r < DEC_B:
                        turn(r)
                weigh(p)

        def outs(e, r, par, copy, sem):
            for g in (par, par + 2):
                q = 4 * r + g
                e.wait_ge(S.turned, q + 1)
                if r >= 2:
                    e.wait_ge(S.dots_done, r - 1)
                copy(kT[:, r % 2, g * 512:(g + 1) * 512], T.ps[:, 5 + q % 3, :]).then_inc(sem, 1)

        @block.scalar
        def _(e):
            def high(r):
                e.wait_ge(page_in[r % 3], 16 * PAGES * (r // 3 + 1))
                if r >= 2:
                    e.wait_ge(S.turned, 4 * (r - 1))
                e.activation(ks[:, r % 2, :, 0:64].rearrange("p i (a c) -> p i a c", a=2),
                             ip[:, r % 3, :, :].unsqueeze(2).to_broadcast([P, PAGES, 2, ID]), ACT.Copy).then_inc(S.kh_done, 1)
            cp = lambda d, s: e.activation(d, s, ACT.Copy)
            high(0)
            high(1)
            outs(e, 0, 0, cp, S.out_act)
            outs(e, 1, 0, cp, S.out_act)
            for p in range(DEC_B // 2):
                for r in (2 * p + 2, 2 * p + 3):
                    if r < DEC_B:
                        high(r)
                e.wait_ge(S.dots_done, 2 * p + 2)
                if p > 0:
                    e.wait_ge(S.weighed, p)
                e.activation(R[:, :], flat[:, 0:SKEYS], ACT.Relu).then_inc(S.relu_done, 1)
                for r in (2 * p + 2, 2 * p + 3):
                    if r < DEC_B:
                        outs(e, r, 0, cp, S.out_act)

        @block.vector
        def _(e):
            def low(r):
                e.wait_ge(S.kh_done, r + 1)
                e.tensor_tensor(ks[:, r % 2, :, 64:P].rearrange("p i (a c) -> p i a c", a=2),
                                ip[:, r % 3, :, :].unsqueeze(2).to_broadcast([P, PAGES, 2, ID]),
                                ks[:, r % 2, :, 0:64].rearrange("p i (a c) -> p i a c", a=2).bitcast(F32),
                                ALU.subtract).then_inc(S.kl_done, 1)
            e.memset(wall[:, :, :], 0.0).then_inc(S.w_zero, 1)
            e.wait_ge(S.w_zero, 1)
            for r in range(DEC_B):
                h = slice(64 * (r % 2), 64 * (r % 2) + 64)
                e.tensor_scalar(wall[h, r // 2, r * DEC_T:(r + 1) * DEC_T], T.qdelta[h, :], T.wcol[h, r:r + 1], None,
                                ALU.mult).then_inc(S.w_set, 1)
            low(0)
            low(1)
            outs(e, 0, 1, e.tensor_copy, S.out_dve)
            outs(e, 1, 1, e.tensor_copy, S.out_dve)
            for p in range(DEC_B // 2):
                for r in (2 * p + 2, 2 * p + 3):
                    if r < DEC_B:
                        low(r)
                for r in (2 * p + 2, 2 * p + 3):
                    if r < DEC_B:
                        outs(e, r, 1, e.tensor_copy, S.out_dve)
                e.wait_ge(S.weighed, p + 1)
                if p == 0:
                    e.tensor_copy(T.score[:, :], flat[0:SAMPLE, 0:SKEYS]).then_inc(S.scored, 1)
                else:
                    e.wait_ge(S.scored, p)
                    e.tensor_tensor(T.score[:, :], T.score[:, :], flat[0:SAMPLE, 0:SKEYS], ALU.add).then_inc(S.scored, 1)
            e.wait_ge(S.scored, DEC_B // 2)
            new = T.score[:, PAST:SKEYS]
            e.tensor_tensor(new, new, T.tri8[0:SAMPLE, :], ALU.add)
    nc.all_engine_barrier(sems_to_clear=S.range)


SAMPLE_SEMS = ["page_in0", "page_in1", "page_in2", "page_in3", "newv_in", "kh_done", "kl_done", "bank_ps", "out_act", "out_dve",
               "chunk_used", "s_done", "max_done", "nmax_done", "exp_done", "pv_done", "rinv_done", "o_done", "o_ps", "ol_done",
               "uv_ps", "mix_hi", "mix_lo", "bias_set"]


def sample_block(nc, T, S, l, kind, cache, new_rows):
    M = kind == "M"
    W_ = RL + PE_D if M else 2 * AD
    VW, VAT = (RL, 0) if M else (AD, AD)
    n = kind
    C1 = Map(T.nc, T.arena)
    pg = T.M.put(n + "pg", [P, 4, PAGES, W_], F32, C1.region(4 * PAGES * W_ * 4))
    olS = T.M.put(n + "olS", [P, DEC_B, BH, DEC_T], F32, C1.region(2048))
    osb = T.M.put(n + "osb", [P, P], F32, C1.region(512))
    st = T.M.put(n + "st", [P, 8], F32, C1.region(32))
    assert C1.top <= T.newT_at
    Z = Map(T.nc, T.z_at)
    ks = T.M.put(n + "ks", [P, 2, PAGES, P], F32R, Z.region(2 * PAGES * P * 4))
    Pb = T.M.put(n + "P", [P, SKEYS], F32, Z.region(SKEYS * 4))
    assert Z.top <= T.comb_at
    A = Map(T.nc, T.raw_at)
    kT = T.M.put(n + "kT", [P, 3, 512], F32R, A.region(3 * 2048))
    if M:
        cTh = T.M.put(n + "cTh", [P, 3, 512], F32R, A.region(3 * 2048))
        cTl = T.M.put(n + "cTl", [P, 3, 512], F32R, A.region(3 * 2048))
    else:
        bias = T.M.put("sbias", [SAMPLE, SKEYS], BF16, A.region(SKEYS * 2))
    PT = T.M.put(n + "PT", [P, 2, 512], F32, A.region(4096))
    newv = T.M.put(n + "newv", [DEC_T, DEC_B, VW], F32, A.region(DEC_B * VW * 4))
    assert A.top <= T.gb_at - 4096
    flat = T.ps[:, :, :].rearrange("p b c -> p (b c)")
    page_in = [S.page_in0, S.page_in1, S.page_in2, S.page_in3]
    PAIRS = DEC_B // 2
    scale = M_SCALE if M else D_SCALE

    order = []
    for p in range(PAIRS):
        for ch in range(8 * p, 8 * p + 8):
            order += ([("c", ch)] if M else []) + [("k", ch)]
        if p > 0:
            order.append(("o", p - 1))
        order += [("p", p, g) for g in range(5)]
    order.append(("o", PAIRS - 1))
    jobs, na, nd = {}, 0, 0
    for q, j in enumerate(order):
        who = {"c": "AD", "k": "D" if j[1] % 2 and M else "A", "p": "A" if j[-1] % 2 else "D", "o": "A" if M else "O"}[j[0]]
        if not M and j[0] == "k":
            who = "A" if j[1] % 2 else "D"
        if "A" in who:
            na += 1
        if "D" in who:
            nd += 1
        jobs[j] = (q, who, na, nd)

    def gone(e, j):
        q, who, a, d = jobs[j]
        if who == "O":
            e.wait_ge(S.mix_lo, 2 * (j[1] + 1))
        elif "D" in who:
            e.wait_ge(S.out_dve, d)
        else:
            e.wait_ge(S.out_act, a)

    def bank(j):
        return T.ps[:, 6 + jobs[j][0] % 2, :]

    def take(e, j):
        q = jobs[j][0]
        if q >= 2:
            gone(e, order[q - 2])

    with nc.Block() as block:
        @block.sync
        def _(e):
            c0 = 0 if M else AD
            e.dma_start(newv[:, :, :], new_rows[bass.ds(l, 1), :, :, c0:c0 + VW].rearrange("l b t c -> t (l b) c"))\
             .then_inc(S.newv_in, 16)
            for r in range(DEC_B):
                if r >= 4:
                    e.wait_ge(S.pv_done, r // 2 - 1)
                page_loads(e, T, l, r, pg[:, r % 4, :, :], [(cache, 0, W_, 0)], page_in[r % 4])

        def kview(r, part):
            if M:
                d = ks[:, r % 2, :, 64 * part:64 * part + 64].rearrange("p i (a c) -> p i a c", a=2)
                return d, pg[:, r % 4, :, RL:RL + PE_D].unsqueeze(2).to_broadcast([P, PAGES, 2, PE_D])
            return ks[:, r % 2, :, 64 * part:64 * part + 64], pg[:, r % 4, :, 0:AD]

        @block.gpsimd
        def _(e):
            for r in range(DEC_B):
                e.wait_ge(S.kh_done, r + 1)
                d, s = kview(r, 1)
                e.tensor_tensor(d, s, kview(r, 0)[0].bitcast(F32), ALU.subtract).then_inc(S.kl_done, 1)

        @block.tensor
        def _(e):
            def turn_chunk(ch):
                r, g = ch // 4, ch % 4
                if M:
                    take(e, ("c", ch))
                    if g == 0:
                        e.wait_ge(page_in[r % 4], 16 * PAGES * (r // 4 + 1))
                    for k in range(4):
                        mm = e.transpose(bank(("c", ch))[:, k * P:(k + 1) * P], pg[:, r % 4, 4 * g + k, 0:RL], T.ident[:, :])
                    mm.then_inc(S.bank_ps, 1)
                take(e, ("k", ch))
                if g == 0:
                    e.wait_ge(S.kl_done, r + 1)
                for k in range(4):
                    mm = e.transpose(bank(("k", ch))[:, k * P:(k + 1) * P], ks[:, r % 2, 4 * g + k, :].bitcast(F32),
                                     T.ident[:, :])
                mm.then_inc(S.bank_ps, 1)

            def scores(ch):
                r, g = ch // 4, ch % 4
                b0, s = r % 2 == 0, ch % 3
                if b0 and g == 0 and r > 0:
                    e.wait_ge(S.exp_done, r // 2)
                gone(e, ("k", ch))
                out = T.ps[:, g, :]
                if M:
                    gone(e, ("c", ch))
                    ops = [(T.QLh, cTh), (T.QLh, cTl), (T.QLl, cTh), (T.QP, kT)]
                else:
                    ops = [(T.QA, kT), (T.QB, kT)]
                for i, (q, k) in enumerate(ops):
                    mm = e.matmul(out, q[:, r, :], k[:, s, :], start=b0 and i == 0, stop=not b0 and i == len(ops) - 1 and M)
                mm.then_inc(S.chunk_used, 1)
                if not M and not b0:
                    if ch == 4:
                        e.wait_ge(S.bias_set, 2)
                    e.matmul(out, T.selb[:, r // 2, :], bias[:, g * 512:(g + 1) * 512], start=False, stop=True)
                if g == 3:
                    out = T.ps[:, 4, 0:DEC_T]
                    c = slice(r * DEC_T, (r + 1) * DEC_T)
                    if M:
                        ops = [(T.QLh, T.newcT[:, 0, c]), (T.QLh, T.newcT[:, 1, c]), (T.QLl, T.newcT[:, 0, c]),
                               (T.QP, T.newT[:, 2, c])]
                    else:
                        ops = [(T.QA, T.newT[:, 0, c]), (T.QB, T.newT[:, 0, c])]
                    for i, (q, k) in enumerate(ops):
                        mm = e.matmul(out, q[:, r, :], k, start=b0 and i == 0, stop=False)
                    if not b0:
                        if M:
                            mm = e.matmul(out, T.identb[:, :], T.tri8b[:, :], start=False, stop=True)
                        else:
                            mm = e.matmul(out, T.selb[:, r // 2, :], bias[:, PAST:SKEYS], start=False, stop=True)
                        mm.then_inc(S.s_done, 1)

            def turn_p(p, g):
                j = ("p", p, g)
                take(e, j)
                if g == 0:
                    e.wait_ge(S.exp_done, p + 1)
                if g < 4:
                    for k in range(4):
                        c = (4 * g + k) * P
                        mm = e.transpose(bank(j)[:, k * P:(k + 1) * P], Pb[:, c:c + P], T.ident[:, :])
                else:
                    mm = e.transpose(bank(j)[0:DEC_T, 0:P], Pb[:, PAST:SKEYS], T.ident[:, :])
                mm.then_inc(S.bank_ps, 1)

            def values(p, g):
                gone(e, ("p", p, g))
                if g == 0 and p > 0:
                    e.wait_ge(S.o_done, p)
                if p == 0 and g == 4:
                    e.wait_ge(S.newv_in, 16)
                for b in range(2):
                    r = 2 * p + b
                    out = T.ps[64 * b:64 * b + 64, 5, 0:VW]
                    for k in range(4 if g < 4 else 1):
                        kr = P if g < 4 else DEC_T
                        c = k * P + 64 * b
                        rhs = pg[:, r % 4, 4 * g + k, VAT:VAT + VW] if g < 4 else newv[:, r, :]
                        mm = e.matmul(out, PT[0:kr, (5 * p + g) % 2, c:c + 64], rhs, start=g == 0 and k == 0, stop=g == 4)
                mm.then_inc(S.pv_done, 1) if g == 4 else mm.then_inc(S.o_ps, 1)

            def turn_o(p):
                j = ("o", p)
                take(e, j)
                e.wait_ge(S.o_done, p + 1)
                e.transpose(bank(j)[:, 0:P], osb[:, :], T.ident[:, :]).then_inc(S.bank_ps, 1)

            for p in range(PAIRS):
                turn_chunk(8 * p)
                for ch in range(8 * p, 8 * p + 8):
                    if ch + 1 < 8 * p + 8:
                        turn_chunk(ch + 1)
                    scores(ch)
                if p > 0:
                    turn_o(p - 1)
                turn_p(p, 0)
                for g in range(5):
                    if g < 4:
                        turn_p(p, g + 1)
                    values(p, g)
            turn_o(PAIRS - 1)
            if M:
                e.wait_ge(S.ol_done, PAIRS)
                for h in range(BH):
                    b = 64 * (h % 2)
                    mm = e.matmul(T.ps[b:b + VD, 0, (h // 2) * SAMPLE:(h // 2 + 1) * SAMPLE], T.wuv[:, h, :],
                                  olS[:, :, h, :], start=True, stop=True)
                mm.then_inc(S.uv_ps, 1)

        def dsa_out(p, par):
            rows = slice(64 * par, 64 * par + 64)
            c = S0 + 2 * p * DEC_T
            dst = lambda x: x[rows, 0:4, c:c + 2 * DEC_T].rearrange("p k (b t) -> p k b t", b=2)
            src = bank(("o", p))[rows, 0:P].rearrange("p (b k u t) -> p u k b t", b=2, u=2, k=4)[:, par]
            return dst, src

        def pt_out(e, p, g, me):
            j = ("p", p, g)
            q, who, a, d = jobs[j]
            if who != me:
                return
            i = 5 * p + g
            e.wait_ge(S.bank_ps, q + 1)
            if i >= 2:
                if g >= 2:
                    e.wait_ge(S.o_ps, 4 * p + g - 1)
                elif g == 1:
                    e.wait_ge(S.pv_done, p)
                else:
                    e.wait_ge(S.o_ps, 4 * p)
            rows, w = (P, 512) if g < 4 else (DEC_T, P)
            if me == "A":
                e.activation(PT[0:rows, i % 2, 0:w], bank(j)[0:rows, 0:w], ACT.Copy).then_inc(S.out_act, 1)
            else:
                e.tensor_copy(PT[0:rows, i % 2, 0:w], bank(j)[0:rows, 0:w]).then_inc(S.out_dve, 1)

        def mix_out(e, p):
            act = e.engine == mybir.EngineType.Activation
            e.wait_ge(S.bank_ps, jobs[("o", p)][0] + 1)
            for par in range(2):
                dst, src = dsa_out(p, par)
                if act:
                    e.activation(dst(T.xth), src, ACT.Copy).then_inc(S.mix_hi, 1)
                else:
                    e.wait_ge(S.mix_hi, 2 * p + par + 1)
                    e.tensor_tensor(dst(T.xtl), src, dst(T.xth).bitcast(F32), ALU.subtract).then_inc(S.mix_lo, 1)

        @block.scalar
        def _(e):
            def high(r):
                e.wait_ge(page_in[r % 4], 16 * PAGES * (r // 4 + 1))
                if r >= 2:
                    e.wait_ge(S.bank_ps, jobs[("k", 4 * (r - 2) + 3)][0] + 1)
                d, s = kview(r, 0)
                e.activation(d, s, ACT.Copy).then_inc(S.kh_done, 1)

            def chunk_out(ch):
                s = ch % 3
                for kd in ("c", "k"):
                    if (kd, ch) not in jobs:
                        continue
                    q, who, a, d = jobs[(kd, ch)]
                    if "A" in who:
                        e.wait_ge(S.bank_ps, q + 1)
                        if ch >= 3:
                            e.wait_ge(S.chunk_used, ch - 2)
                        e.activation(cTh[:, s, :] if kd == "c" else kT[:, s, :], bank((kd, ch)), ACT.Copy).then_inc(S.out_act, 1)

            high(0)
            high(1)
            for p in range(PAIRS):
                for ch in range(8 * p, 8 * p + 8):
                    chunk_out(ch)
                    if ch % 4 == 3 and ch // 4 + 2 < DEC_B:
                        high(ch // 4 + 2)
                e.wait_ge(S.nmax_done, p + 1)
                if p > 0:
                    e.wait_ge(S.bank_ps, jobs[("p", p - 1, 4)][0] + 1)
                e.activation(Pb[:, :], flat[:, 0:SKEYS], ACT.Exp, bias=st[:, 1:2], scale=scale,
                             accum_out=st[:, 2:3]).then_inc(S.exp_done, 1)
                if p > 0 and M:
                    j = ("o", p - 1)
                    e.wait_ge(S.bank_ps, jobs[j][0] + 1)
                    e.activation(olS[:, 2 * p - 2:2 * p, :, :].rearrange("p b h t -> p (b h t)"), bank(j)[:, 0:P], ACT.Copy)\
                     .then_inc(S.out_act, 1)
                if p > 0 and not M:
                    mix_out(e, p - 1)
                for g in range(5):
                    pt_out(e, p, g, "A")
            if M:
                j = ("o", PAIRS - 1)
                e.wait_ge(S.bank_ps, jobs[j][0] + 1)
                e.activation(olS[:, DEC_B - 2:DEC_B, :, :].rearrange("p b h t -> p (b h t)"), bank(j)[:, 0:P], ACT.Copy)\
                 .then_inc(S.ol_done, PAIRS)
                e.wait_ge(S.uv_ps, 1)
                e.activation(T.xth[:, 4:8, S0:TAIL], T.ps[:, 0, 0:4 * SAMPLE].rearrange("p (k c) -> p k c", k=4), ACT.Copy)\
                 .then_inc(S.mix_hi, 1)
            else:
                mix_out(e, PAIRS - 1)

        @block.vector
        def _(e):
            if not M:
                e.tensor_scalar(bias[:, :], T.score[:, :], 2 / 3 * TAKEN, NEG, ALU.is_gt, ALU.mult).then_inc(S.bias_set, 1)
                e.wait_ge(S.bias_set, 1)
                e.tensor_tensor(bias[:, PAST:SKEYS], bias[:, PAST:SKEYS], T.tri8b[0:SAMPLE, :], ALU.add).then_inc(S.bias_set, 1)
            for p in range(PAIRS):
                for ch in range(8 * p, 8 * p + 8):
                    s = ch % 3
                    for kd in ("c", "k"):
                        if (kd, ch) not in jobs:
                            continue
                        q, who, a, d = jobs[(kd, ch)]
                        if "D" not in who:
                            continue
                        e.wait_ge(S.bank_ps, q + 1)
                        if ch >= 3:
                            e.wait_ge(S.chunk_used, ch - 2)
                        if kd == "c":
                            e.wait_ge(S.out_act, a)
                            e.tensor_tensor(cTl[:, s, :], bank((kd, ch)), cTh[:, s, :].bitcast(F32), ALU.subtract)\
                             .then_inc(S.out_dve, 1)
                        else:
                            e.tensor_copy(kT[:, s, :], bank((kd, ch))).then_inc(S.out_dve, 1)
                e.wait_ge(S.s_done, p + 1)
                e.tensor_reduce(st[:, 0:1], flat[:, 0:SKEYS], AX, ALU.max).then_inc(S.max_done, 1)
                e.wait_ge(S.max_done, p + 1)
                if p > 0:
                    e.wait_ge(S.exp_done, p)
                e.tensor_scalar(st[:, 1:2], st[:, 0:1], -scale, None, ALU.mult).then_inc(S.nmax_done, 1)
                if p > 0 and not M:
                    mix_out(e, p - 1)
                for g in range(5):
                    pt_out(e, p, g, "D")
                e.wait_ge(S.pv_done, p + 1)
                e.reciprocal(st[:, 3:4], st[:, 2:3]).then_inc(S.rinv_done, 1)
                e.wait_ge(S.rinv_done, p + 1)
                if p > 0:
                    e.wait_ge(S.bank_ps, jobs[("o", p - 1)][0] + 1)
                if M:
                    e.tensor_scalar(osb[:, :], T.ps[:, 5, 0:P], st[:, 3:4], None, ALU.mult).then_inc(S.o_done, 1)
                else:
                    e.tensor_scalar(osb[:, :].rearrange("p (a c) -> p a c", a=2),
                                    T.ps[:, 5, 0:AD].unsqueeze(1).to_broadcast([P, 2, AD]), st[:, 3:4], None,
                                    ALU.mult).then_inc(S.o_done, 1)
            if M:
                e.wait_ge(S.mix_hi, 1)
                e.tensor_tensor(T.xtl[:, 4:8, S0:TAIL], T.ps[:, 0, 0:4 * SAMPLE].rearrange("p (k c) -> p k c", k=4),
                                T.xth[:, 4:8, S0:TAIL].bitcast(F32), ALU.subtract).then_inc(S.mix_lo, 1)
            else:
                mix_out(e, PAIRS - 1)
    nc.all_engine_barrier(sems_to_clear=S.range)


MIX_OUT_SEMS = LN_SEMS + STREAM_SEMS


def mix_out_block(nc, T, S, l, w_o, ln_g, ln_b):
    load, hi, lo = stream_ops(T, S)
    T.gb_free = lambda S_: None
    sp2, act2, dve2, pool2, pe2 = out_stage(nc, T, S, KD, 0, T.xth, T.xtl, 1.0, lambda e, g, k, t: None)
    with nc.Block() as block:
        @block.sync
        def _(e):
            sp2(e, lambda k: w_o[bass.ds(l, 1), k * P:(k + 1) * P, :].rearrange("l p n -> p (l n)"), ln_g, ln_b, l)

        @block.scalar
        def _(e):
            hi(e, 0, 0, 0, first=True)
            hi(e, 1, 1, 0, first=True)
            act2(e)

        @block.vector
        def _(e):
            lo(e, 0, 0)
            lo(e, 1, 1)
            dve2(e)

        @block.gpsimd
        def _(e):
            for t in range(TILES):
                x = T.x[0:ROWS[t], t, :]
                e.tensor_scalar(x, x, ALPHA, 1.0, ALU.mult, ALU.mult).then_inc(S.alpha_done, 1)
            pool2(e)

        @block.tensor
        def _(e):
            pe2(e)
    nc.all_engine_barrier(sems_to_clear=S.range)


def build(nc, W, O):
    with ExitStack() as ctx:
        T = make_tensors(nc, ctx)
        proj_tensors(T)
        init_s = Sems(ctx, nc, "init", INIT_SEMS)
        ffn_s = Sems(ctx, nc, "ffn", FFN_SEMS)
        proj_s = Sems(ctx, nc, "proj", PROJ_SEMS)
        index_s = Sems(ctx, nc, "index", INDEX_SEMS)
        prompt_s = Sems(ctx, nc, "prompt", PROMPT_SEMS)
        sample_s = Sems(ctx, nc, "sample", SAMPLE_SEMS)
        y_out = ctx.enter_context(nc.semaphore("y_out"))
        init_block(nc, T, init_s, W["x_prompt"], W["x_sample"], W["meta_tokens"], W["consts"], W["page_table"])
        with nc.Fori(0, DEPTH) as l:
            ffn_block(nc, T, ffn_s, l, W["ffn1_w_in"], W["ffn1_w_out"], W["ln1_g"], W["ln1_b"])
            proj_block(nc, T, proj_s, l, W, O)
            index_block(nc, T, index_s, l, W["cache_dsa"])
            prompt_block(nc, T, prompt_s)
            sample_block(nc, T, sample_s, l, "M", W["cache_mla"], O["mla_s"])
            sample_block(nc, T, sample_s, l, "D", W["cache_dsa"], O["dsa_s"])
            mix_out_block(nc, T, ffn_s, l, W["w_o"], W["ln2_g"], W["ln2_b"])
            ffn_block(nc, T, ffn_s, l, W["ffn2_w_in"], W["ffn2_w_out"], W["ln3_g"], W["ln3_b"])
        with nc.Block() as block:
            @block.sync
            def _(e):
                e.dma_start(O["y_prompt"][0, 0:P - N_META, :], T.x[N_META:P, 0, :]).then_inc(y_out, 16)
                e.dma_start(O["y_prompt"][0, P - N_META:S0 - N_META, :].rearrange("(t p) d -> p t d", p=P),
                            T.x[:, 1:4, :]).then_inc(y_out, 16)
                e.dma_start(O["y_prompt"][0, S0 - N_META:SEQ, :], T.x[SAMPLE:ROWS[4], 4, :]).then_inc(y_out, 16)
                e.dma_start(O["y_sample"].rearrange("b t d -> (b t) d"), T.x[0:SAMPLE, 4, :]).then_inc(y_out, 16)
                e.wait_ge(y_out, 64)


_OUTS = [("y_prompt", (1, SEQ, D)), ("y_sample", (DEC_B, DEC_T, D)), ("dsa_p", (DEPTH, 1, PROMPT, ROW)),
         ("mla_p", (DEPTH, 1, PROMPT, ROW)), ("dsa_s", (DEPTH, DEC_B, DEC_T, ROW)), ("mla_s", (DEPTH, DEC_B, DEC_T, ROW))]


def kernel(**inputs):
    import concourse.bacc as _bacc
    from concourse.bass_utils import run_bass_kernel_spmd as _run

    nc = _bacc.Bacc("TRN2", target_bir_lowering=False, num_devices=1)
    arrays, W, O = {}, {}, {}
    for name, a in [*inputs.items(), ("consts", constants())]:
        a = np.ascontiguousarray(a)
        arrays[f"in_{name}"] = a
        W[name] = nc.dram_tensor(f"in_{name}", a.shape, mybir.dt.from_np(a.dtype), kind="ExternalInput").ap()
    for name, shape in _OUTS:
        O[name] = nc.dram_tensor(f"out_{name}", shape, F32, kind="ExternalOutput").ap()
    O["iw_scratch"] = nc.dram_tensor("iw_scratch", (SAMPLE, IH), F32, kind="Internal").ap()
    build(nc, W, O)
    r = _run(nc, [arrays], core_ids=[0])
    return tuple(r.results[0][f"out_{name}"] for name, _ in _OUTS)
```

```python
import numpy as np
import concourse.bass as bass
from concourse import mybir
from contextlib import ExitStack

F32 = mybir.dt.float32
F32R = mybir.dt.float32r
BF16 = mybir.dt.bfloat16
I32 = mybir.dt.int32
ALU = mybir.AluOpType
ACT = mybir.ActivationFunctionType
AX = mybir.AxisListType.X

P = 128
DEPTH, D, D_FF = 2, 1024, 2816
SEQ, N_META, DEC_B, DEC_T = 512, 16, 8, 8
PROMPT = SEQ + N_META
SAMPLE = DEC_B * DEC_T
PAST, PAGE = 2048, 128
PAGES = PAST // PAGE
POOL_PAGES = DEC_B * PAGES * 5 // 4
CHUNKS = P // PAGES
TOK = PROMPT + SAMPLE
TILES = 5
ROWS = [P, P, P, P, TOK - 4 * P]
S0, TAIL = 4 * P, 4 * P + SAMPLE
KD = D // P
KF = D_FF // P
HALF = TOK // 2
ALPHA = (2 * DEPTH) ** 0.25
LN_EPS, RMS_EPS = 1e-5, 1e-6
AH, AD, AROT = 8, 64, 16
IH, ID, IROT = 8, 32, 8
BH, NOPE, PE_D, RL, QL, VD = 8, 64, 32, 128, 256, 64
ROW = 2 * AD + ID
N_IN = AH * AD + 2 * AD + IH * ID + ID + IH + QL + RL + PE_D
Z_AQ, Z_AK, Z_AV, Z_IQ = 0, AH * AD, AH * AD + AD, AH * AD + 2 * AD
Z_IK = Z_IQ + IH * ID
Z_IW = Z_IK + ID
Z_CQ = Z_IW + IH
Z_CKV = Z_CQ + QL
Z_KPE = Z_CKV + RL
QB = BH * (NOPE + PE_D)
TOPK_P = min(256, PROMPT // 4)
TOPK_S = min(256, (PAST + DEC_T) // 4)
ROPE_THETA = 500000.0
RAW = 4
SPLIT = 2
BLK = 1024
NEG = -1.0e30
TAKEN = -3.0e38


def rope_tables():
    pos = np.zeros(TILES * P, np.float32)
    pos[:S0] = np.arange(S0)
    pos[S0:TAIL] = PAST + np.arange(SAMPLE) % DEC_T
    pos[TAIL:TOK] = np.arange(S0, PROMPT)
    cos, sin = [], []
    for rot in (AROT, IROT, PE_D):
        half = rot // 2
        inv = (np.float32(ROPE_THETA) ** (-np.arange(half, dtype=np.float32) / np.float32(half))).astype(np.float32)
        ang = (pos[:, None] * inv).astype(np.float32)
        cos.append(np.cos(ang).astype(np.float32))
        sin.append(np.sin(ang).astype(np.float32))
    return np.ascontiguousarray(np.concatenate(cos + sin, axis=1), np.float32)


ROPE_W = AROT // 2 + IROT // 2 + PE_D // 2


class Sems:

    def __init__(self, ctx, nc, block, names):
        self.all = {}
        for n in names:
            self.all[n] = ctx.enter_context(nc.semaphore(f"{block}_{n}"))
        nums = sorted(s.num for s in self.all.values())
        assert nums == list(range(nums[0], nums[0] + len(nums)))
        self.range = range(nums[0], nums[-1] + 1)

    def __getattr__(self, n):
        return self.all[n]


class Map:

    def __init__(self, nc, base):
        self.nc, self.top = nc, (base + 63) // 64 * 64

    def region(self, nbytes):
        at = self.top
        self.top += (nbytes + 63) // 64 * 64
        return at

    def put(self, name, shape, dt, at):
        return self.nc.alloc_sbuf_tensor_at(name, shape, dt, offset=at)


LN_SEMS = ["evac_done", "stats_done", "aggr_done", "std_done", "rstd_done", "tile3_done",
           "nb_done", "norm_done", "gain_done", "x_done", "gain_v_done", "x_v_done", "xt_ps", "xth_done", "xtl_done", "gb_in", "alpha_done"]
STREAM_SEMS = ["raw_in0", "raw_in1", "raw_in2", "raw_in3", "hi_done", "split_done", "w_used"]


def stream_ops(T, S):
    raw_in = [S.raw_in0, S.raw_in1, S.raw_in2, S.raw_in3]

    def load(e, n, s, src, shape=None, first=False, round_=None):
        if not first:
            e.wait_ge(S.split_done, n - (RAW - 1))
        dst = T.raw[:, s, 0:(BLK if shape is None else shape[0] * shape[1])]
        if shape is not None:
            dst = dst.rearrange("p (k c) -> p k c", k=shape[0])
        e.dma_start(dst, src).then_inc(raw_in[s], 16)

    def hi(e, n, s, round_, width=BLK, first=False):
        e.wait_ge(raw_in[s], round_ * 16 + 16)
        if not first:
            e.wait_ge(S.w_used, n - (SPLIT - 1))
        e.activation(T.whi[:, s % SPLIT, 0:width], T.raw[:, s, 0:width], ACT.Copy).then_inc(S.hi_done, 1)

    def lo(e, n, s, width=BLK):
        e.wait_ge(S.hi_done, n + 1)
        e.tensor_tensor(T.wlo[:, s % SPLIT, 0:width], T.raw[:, s, 0:width],
                        T.whi[:, s % SPLIT, 0:width].bitcast(F32), ALU.subtract).then_inc(S.split_done, 1)

    return load, hi, lo


def three(e, out, lhi, llo, rhi, rlo, start, stop):
    e.matmul(out, lhi, rhi, start=start, stop=False)
    e.matmul(out, lhi, rlo, start=False, stop=False)
    return e.matmul(out, llo, rhi, start=False, stop=stop)


NV = 640
GROUPS = [(0, 1, 2), (3, 4)]
ACC = {0: (0, 1), 1: (2, 3), 2: (4, 5), 3: (6, 7), 4: (0, 1)}
TPB = {0: 2, 1: 4, 2: 2, 3: 4, 4: 2}


def out_stage(nc, T, S, kt, n0, lhs_hi, lhs_lo, scale, first_wait):
    load, hi, lo = stream_ops(T, S)
    if kt > 12:
        per = (kt - 2) // 5
        sum_at = {0: 0, per: 1, 2 * per: 2}
        stats_at = {0: 0, per + 1: 1, 2 * per + 1: 2}
        std_at = {per - 1: 0, 2 * per - 1: 1, 3 * per - 1: 2}
        turn = {min(kt - 1, 2 + 2 * per + per * t): t for t in range(3)}
    else:
        sum_at, std_at, turn = {0: 0, 2: 1, 4: 2}, {1: 0, 3: 1, 5: 2}, {4: 0, 5: 1}
        stats_at = sum_at
    rest = [t for t in GROUPS[0] if t not in turn.values()]

    def sp(e, weight, ln_g, ln_b, l):
        for g in range(2):
            for k in range(kt):
                n = n0 + g * kt + k
                load(e, n, n % RAW, weight(k), first=n < RAW)
                if g == 0 and k == kt // 2:
                    ln_wait = T.gb_free(S)
                    if ln_wait:
                        e.wait_ge(*ln_wait)
                    for i, a in enumerate((ln_g, ln_b)):
                        e.dma_start(T.gb[:, i, :], a[bass.ds(l, 1), :].partition_broadcast(P)).then_inc(S.gb_in, 16)

    def act_split(e, n, first=False):
        hi(e, n, n % RAW, n // RAW, first=first)

    def ln_sum(e, t):
        r = ROWS[t]
        if t == 0:
            e.wait_ge(S.alpha_done, TILES)
        for h in range(2):
            if h == 0 and t == 3:
                e.wait_ge(S.tile3_done, 1)
            elif h == 0:
                e.wait_ge(S.w_used, n0 + (kt if t in GROUPS[0] else 2 * kt))
            x = T.x[0:r, t, h * 512:(h + 1) * 512]
            e.scalar_tensor_tensor(x, T.ps[0:r, ACC[t][h], :], scale, x, ALU.mult, ALU.add)\
             .then_inc(S.evac_done, 1)

    def ln_stats(e, t):
        r = ROWS[t]
        for h in range(2):
            e.wait_ge(S.evac_done, 2 * t + h + 1)
            e.bn_stats(T.stats[0:r, h, :], T.x[0:r, t, h * 512:(h + 1) * 512]).then_inc(S.stats_done, 1)
        e.wait_ge(S.stats_done, 2 * t + 2)
        e.bn_aggr(T.mv[0:r, t, :], T.stats[0:r, :, :]).then_inc(S.aggr_done, 1)

    def ln_a(e, t):
        ln_sum(e, t)
        ln_stats(e, t)

    def ln_b(e, t):
        e.wait_ge(S.aggr_done, t + 1)
        e.activation(T.std[0:ROWS[t], t:t + 1], T.mv[0:ROWS[t], t, 1:2], ACT.Sqrt,
                     bias=T.eps[0:ROWS[t], 0:1]).then_inc(S.std_done, 1)

    def ln_c(e, t):
        e.wait_ge(S.std_done, t + 1)
        r = ROWS[t]
        e.reciprocal(T.rstd[0:r, t:t + 1], T.std[0:r, t:t + 1]).then_inc(S.rstd_done, 1)
        e.wait_ge(S.rstd_done, t + 1)
        e.scalar_tensor_tensor(T.nb[0:r, t:t + 1], T.mv[0:r, t, 0:1], -1.0, T.rstd[0:r, t:t + 1],
                               ALU.mult, ALU.mult).then_inc(S.nb_done, 1)

    def ln_d(e, t):
        r = ROWS[t]
        c = slice(0 if t < 3 else NV, D)
        x = T.x[0:r, t, c]
        e.wait_ge(S.nb_done, t + 1)
        e.tensor_scalar(x, x, T.rstd[0:r, t:t + 1], T.nb[0:r, t:t + 1], ALU.mult, ALU.add).then_inc(S.norm_done, 1)
        if t == 0:
            e.wait_ge(S.gb_in, 32)
        e.wait_ge(S.norm_done, t + 1)
        e.tensor_tensor(x, x, T.gb[0:r, 0, c], ALU.mult).then_inc(S.gain_done, 1)
        e.wait_ge(S.gain_done, t + 1)
        e.tensor_tensor(x, x, T.gb[0:r, 1, c], ALU.add).then_inc(S.x_done, 1)

    def ln_dv(e, t):
        r = ROWS[t]
        x = T.x[0:r, t, 0:NV]
        if t == 3:
            e.wait_ge(S.gb_in, 32)
        e.scalar_tensor_tensor(x, x, T.mv[0:r, t, 0:1], T.gb[0:r, 0, 0:NV], ALU.subtract, ALU.mult)\
         .then_inc(S.gain_v_done, 1)
        e.wait_ge(S.rstd_done, t + 1)
        e.wait_ge(S.gain_v_done, t - 2)
        e.scalar_tensor_tensor(x, x, T.rstd[0:r, t:t + 1], T.gb[0:r, 1, 0:NV], ALU.mult, ALU.add)\
         .then_inc(S.x_v_done, 1)

    def ln_e(e, t):
        r = ROWS[t]
        if t < 3:
            e.wait_ge(S.x_done, t + 1)
        else:
            e.wait_ge(S.x_v_done, t - 2)
        if t < 2:
            e.wait_ge(S.evac_done, 2 * (t + 1) + 2)
        else:
            e.wait_ge(S.xtl_done, t - 1)
        for k in range(KD):
            if t >= 3 and k == NV // P:
                e.wait_ge(S.x_done, t + 1)
            mm = e.transpose(T.ps[:, TPB[t] + k // 4, (k % 4) * P:(k % 4) * P + r],
                             T.x[0:r, t, k * P:(k + 1) * P], T.ident[0:r, 0:r])
        mm.then_inc(S.xt_ps, 1)

    def tp(t):
        return T.ps[:, TPB[t]:TPB[t] + 2, :].rearrange("p b (q c) -> p (b q) c", q=4)[:, :, 0:ROWS[t]]

    def ln_f(e, t):
        e.wait_ge(S.xt_ps, t + 1)
        e.activation(T.xth[:, :, t * P:t * P + ROWS[t]], tp(t), ACT.Copy).then_inc(S.xth_done, 1)

    def ln_g(e, t):
        e.wait_ge(S.xth_done, t + 1)
        o = slice(t * P, t * P + ROWS[t])
        e.tensor_tensor(T.xtl[:, :, o], tp(t), T.xth[:, :, o].bitcast(F32), ALU.subtract).then_inc(S.xtl_done, 1)

    def act(e):
        for g in range(2):
            for k in range(kt):
                n = n0 + g * kt + k + 2
                if n < n0 + 2 * kt:
                    act_split(e, n)
                if g == 1 and k in std_at:
                    ln_b(e, std_at[k])
                if g == 1 and k in turn:
                    ln_f(e, turn[k])
        ln_b(e, 3)
        for t in rest:
            ln_f(e, t)
        ln_b(e, 4)
        ln_f(e, 3)
        ln_f(e, 4)

    def dve(e):
        for g in range(2):
            for k in range(kt):
                n = n0 + g * kt + k + 2
                if g == 0 and k == kt - 1:
                    ln_sum(e, 0)
                if n < n0 + 2 * kt:
                    lo(e, n, n % RAW)
                if g == 1 and k > 0 and k in sum_at:
                    ln_sum(e, sum_at[k])
                if g == 1 and k in stats_at:
                    ln_stats(e, stats_at[k])
                if g == 1 and k in std_at:
                    ln_c(e, std_at[k])
                if g == 1 and k in turn:
                    ln_g(e, turn[k])
        ln_a(e, 3)
        ln_c(e, 3)
        ln_a(e, 4)
        for t in rest:
            ln_g(e, t)
        ln_dv(e, 3)
        ln_c(e, 4)
        ln_dv(e, 4)
        ln_g(e, 3)
        ln_g(e, 4)

    def pool(e):
        for t in range(TILES):
            ln_d(e, t)

    def pe(e):
        def block(g, k, tiles):
            n = n0 + g * kt + k
            s = n % SPLIT
            e.wait_ge(S.split_done, n + 1)
            for t in tiles:
                first_wait(e, g, k, t)
                if k == 0 and g == 1 and t == 4:
                    e.wait_ge(S.evac_done, 2)
                o = slice(t * P, t * P + ROWS[t])
                for h in range(2):
                    c = slice(h * 512, h * 512 + 512)
                    out = T.ps[0:ROWS[t], ACC[t][h], :]
                    mm = three(e, out, lhs_hi[:, k, o], lhs_lo[:, k, o], T.whi[:, s, c], T.wlo[:, s, c],
                               k == 0, k == kt - 1)
            return mm

        for g in range(2):
            for k in range(kt - g):
                block(g, k, GROUPS[g]).then_inc(S.w_used, 1)
                if g == 1 and k in turn:
                    ln_e(e, turn[k])
        block(1, kt - 1, (3,)).then_inc(S.tile3_done, 1)
        block(1, kt - 1, (4,)).then_inc(S.w_used, 1)
        for t in [*rest, 3, 4]:
            ln_e(e, t)

    return sp, act, dve, pool, pe


FFN_SEMS = LN_SEMS + STREAM_SEMS + ["silu_done", "hmul_done", "hhi_done", "hlo_done"]


def ffn_block(nc, T, S, l, w_in, w_out, ln_g, ln_b):
    load, hi, lo = stream_ops(T, S)
    N1 = 2 * KF

    def first_wait(e, g, k, t):
        if g == 0 and k == 0 and t in (0, 2):
            e.wait_ge(S.hmul_done, KF - 1 + t // 2)
        if g == 0 and t == 0 and (k == 0 or k >= KF - 2):
            e.wait_ge(S.hlo_done, max(k + 1, KF - 2))
    T.gb_free = lambda S_: (S_.hlo_done, KF)
    sp2, act2, dve2, pool2, pe2 = out_stage(nc, T, S, KF, N1, T.hth, T.htl, 0.5, first_wait)

    def bank(j2, up):
        return T.ps[:, 4 * j2 + 2 * up:4 * j2 + 2 * up + 2, 0:HALF]

    with nc.Block() as block:
        @block.sync
        def _(e):
            def four(i, first):
                for u in range(4):
                    j = 2 * i + u // 2
                    col = (u % 2) * D_FF + j * P
                    src = w_in[bass.ds(l, 1), :, bass.ds(col, P)].rearrange("l (k p) c -> p (l k) c", p=P)
                    load(e, 4 * i + u, u, src, shape=(KD, P), first=first)
            four(0, True)
            with e.Fori(1, KF // 2) as i:
                four(i, False)
            sp2(e, lambda k: w_out[bass.ds(l, 1), k * P:(k + 1) * P, :].rearrange("l p n -> p (l n)"), ln_g, ln_b, l)

        @block.scalar
        def _(e):
            def silu(i, u, first=False):
                e.wait_ge(S.w_used, 4 * i + 2 * u + 2)
                if not (first and u == 0):
                    e.wait_ge(S.hmul_done, 2 * i + u)
                e.activation(T.silu[:, :].rearrange("p (h c) -> p h c", h=2), bank(u, 0), ACT.Silu).then_inc(S.silu_done, 1)

            def body(i, first):
                for u in range(2):
                    for b in range(2):
                        n = 2 + 2 * u + b
                        hi(e, 4 * i + n, n % RAW, i + n // RAW)
                    silu(i, u, first)
            hi(e, 0, 0, 0, first=True)
            hi(e, 1, 1, 0, first=True)
            body(0, True)
            with e.Fori(1, KF // 2) as i:
                body(i, False)
            act2(e)

        @block.vector
        def _(e):
            def hmul(i, u, first=False):
                e.wait_ge(S.silu_done, 2 * i + u + 1)
                if not first:
                    e.wait_ge(S.hlo_done, 2 * i + u - 1)
                e.tensor_tensor(T.hf[:, u, :].rearrange("p (h c) -> p h c", h=2),
                                T.silu[:, :].rearrange("p (h c) -> p h c", h=2), bank(u, 1), ALU.mult)\
                 .then_inc(S.hmul_done, 1)

            def body(i, first):
                for u in range(2):
                    for b in range(2):
                        n = 2 + 2 * u + b
                        lo(e, 4 * i + n, n % RAW)
                    hmul(i, u, first)
            lo(e, 0, 0)
            lo(e, 1, 1)
            body(0, True)
            with e.Fori(1, KF // 2) as i:
                body(i, False)
            dve2(e)

        @block.gpsimd
        def _(e):
            for t in range(TILES):
                x = T.x[0:ROWS[t], t, :]
                e.tensor_scalar(x, x, ALPHA, 1.0, ALU.mult, ALU.mult).then_inc(S.alpha_done, 1)

            with e.Fori(0, KF // 2) as i:
                for u in range(2):
                    j = bass.ds(2 * i + u, 1)
                    e.wait_ge(S.hmul_done, 2 * i + u + 1)
                    h_hi = T.hth[:, j, :].rearrange("p j c -> p (j c)")
                    h_lo = T.htl[:, j, :].rearrange("p j c -> p (j c)")
                    e.tensor_copy(h_hi, T.hf[:, u, :]).then_inc(S.hhi_done, 1)
                    e.wait_ge(S.hhi_done, 2 * i + u + 1)
                    e.tensor_tensor(h_lo, T.hf[:, u, :], h_hi.bitcast(F32), ALU.subtract).then_inc(S.hlo_done, 1)
            pool2(e)

        @block.tensor
        def _(e):
            def body(i, first):
                for u in range(2):
                    for up in range(2):
                        n = 4 * i + 2 * u + up
                        s = up % SPLIT
                        e.wait_ge(S.split_done, n + 1)
                        if up == 0 and not first:
                            e.wait_ge(S.hmul_done, 2 * i + u - 1)
                        for k in range(KD):
                            w = slice(k * P, (k + 1) * P)
                            for part, xs in ((T.whi, (T.xth, T.xtl)), (T.wlo, (T.xth,))):
                                for h in range(2):
                                    o = slice(h * HALF, (h + 1) * HALF)
                                    for xp in xs:
                                        mm = e.matmul(bank(u, up)[:, h, :], part[:, s, w], xp[:, k, o],
                                                      start=(k == 0 and part is T.whi and xp is T.xth),
                                                      stop=(k == KD - 1 and part is T.wlo))
                        mm.then_inc(S.w_used, 1)
            body(0, True)
            with e.Fori(1, KF // 2) as i:
                body(i, False)
            pe2(e)
    nc.all_engine_barrier(sems_to_clear=S.range)


C_ROPE = 0
C_DELTA = C_ROPE + TILES * 2 * ROPE_W
C_TRI8 = C_DELTA + DEC_T
C_TRI = C_TRI8 + DEC_T
C_SEL = C_TRI + P
C_PAGE = C_SEL + DEC_B // 2 * P
C_CHUNK = C_PAGE + PAGES
C_END = C_CHUNK + 1


def constants():
    c = np.zeros((P, C_END), np.float32)
    c[:, C_ROPE:C_DELTA] = rope_tables().reshape(TILES, P, -1).transpose(1, 0, 2).reshape(P, -1)
    row, t = np.arange(P)[:, None], np.arange(DEC_T)[None, :]
    c[:, C_DELTA:C_TRI8] = (row % DEC_T == t)
    c[:, C_TRI8:C_TRI] = np.where(t <= row % DEC_T, 0.0, NEG)
    c[:, C_TRI:C_SEL] = np.where(np.arange(P)[None, :] <= row, 0.0, NEG)
    for pair in range(DEC_B // 2):
        for m in range(P):
            token = (2 * pair + m // (P // 2)) * DEC_T + m % DEC_T
            c[token, C_SEL + pair * P + m] = 1.0
    c[:, C_PAGE:C_CHUNK] = (row // CHUNKS == np.arange(PAGES)[None, :])
    c[:, C_CHUNK:] = row % CHUNKS
    return c


INIT_SEMS = ["x_in", "const_in", "casts", "pages_in", "ident_zero", "ident_done", "index_step", "xt_ps", "xth_done", "xtl_done"]


def init_block(nc, T, S, x_prompt, x_sample, meta, consts, page_table):
    nc_loads = 5
    with nc.Block() as block:
        @block.sync
        def _(e):
            e.dma_start(T.x[0:N_META, 0, :], meta).then_inc(S.x_in, 16)
            e.dma_start(T.pages[:, :, :].rearrange("p b n -> p (b n)"),
                        page_table.rearrange("(a b) n -> a (b n)", a=1).partition_broadcast(P)).then_inc(S.pages_in, 16)
            e.dma_start(T.cin[:, :], consts).then_inc(S.const_in, 16)
            e.dma_start(T.x[N_META:P, 0, :], x_prompt[0, 0:P - N_META, :]).then_inc(S.x_in, 16)
            e.dma_start(T.x[:, 1:4, :], x_prompt[0, P - N_META:S0 - N_META, :].rearrange("(t p) d -> p t d", p=P))\
             .then_inc(S.x_in, 16)
            e.dma_start(T.x[0:SAMPLE, 4, :], x_sample.rearrange("b t d -> (b t) d")).then_inc(S.x_in, 16)
            e.dma_start(T.x[SAMPLE:ROWS[4], 4, :], x_prompt[0, S0 - N_META:SEQ, :]).then_inc(S.x_in, 16)

        @block.gpsimd
        def _(e):
            e.memset(T.ident[:, :], 0.0).then_inc(S.ident_zero, 1)
            e.memset(T.eps[:, 0:1], LN_EPS)
            e.memset(T.eps[:, 1:2], RMS_EPS)
            e.wait_ge(S.ident_zero, 1)
            e.affine_select(out=T.ident[:, :], in_=T.ident[:, :], compare_op=ALU.not_equal, fill=1.0,
                            base=0, pattern=[[-1, P]], channel_multiplier=1).then_inc(S.ident_done, 1)
            e.wait_ge(S.const_in, 16)
            e.wait_ge(S.ident_done, 1)
            c = T.cin
            e.tensor_copy(T.identb[:, :], T.ident[:, :])
            e.tensor_copy(T.rope[:, :, :].rearrange("p t c -> p (t c)"), c[:, C_ROPE:C_DELTA])
            e.tensor_copy(T.qdelta[:, :], c[:, C_DELTA:C_TRI8])
            e.tensor_copy(T.tri8[:, :], c[:, C_TRI8:C_TRI])
            e.tensor_copy(T.tri8b[:, :], c[:, C_TRI8:C_TRI])
            e.tensor_copy(T.trib[:, :], c[:, C_TRI:C_SEL])
            e.tensor_copy(T.selb[:, :, :].rearrange("p a c -> p (a c)"), c[0:SAMPLE, C_SEL:C_PAGE]).then_inc(S.casts, 1)

        @block.tensor
        def _(e):
            e.wait_ge(S.ident_done, 1)
            e.wait_ge(S.x_in, 16 * nc_loads)
            for t in range(TILES):
                r = ROWS[t]
                if t >= 4:
                    e.wait_ge(S.xtl_done, t - 3)
                for k in range(KD):
                    mm = e.transpose(T.ps[:, 2 * (t % 4) + k // 4, (k % 4) * P:(k % 4) * P + r],
                                     T.x[0:r, t, k * P:(k + 1) * P], T.ident[0:r, 0:r])
                mm.then_inc(S.xt_ps, 1)

        def tp(t):
            b = 2 * (t % 4)
            return T.ps[:, b:b + 2, :].rearrange("p b (q c) -> p (b q) c", q=4)[:, :, 0:ROWS[t]]

        @block.scalar
        def _(e):
            for t in range(TILES):
                e.wait_ge(S.xt_ps, t + 1)
                e.activation(T.xth[:, :, t * P:t * P + ROWS[t]], tp(t), ACT.Copy).then_inc(S.xth_done, 1)

        @block.vector
        def _(e):
            for t in range(TILES):
                e.wait_ge(S.xth_done, t + 1)
                o = slice(t * P, t * P + ROWS[t])
                e.tensor_tensor(T.xtl[:, :, o], tp(t), T.xth[:, :, o].bitcast(F32), ALU.subtract)\
                 .then_inc(S.xtl_done, 1)
            e.wait_ge(S.pages_in, 16)
            e.wait_ge(S.const_in, 16)
            pf = T.pagef[:, :, :]
            e.tensor_copy(pf, T.pages[:, :, :]).then_inc(S.index_step, 1)
            e.wait_ge(S.index_step, 1)
            e.tensor_tensor(pf, pf, T.cin[:, C_PAGE:C_CHUNK].unsqueeze(1).to_broadcast([P, DEC_B, PAGES]), ALU.mult)\
             .then_inc(S.index_step, 1)
            e.wait_ge(S.index_step, 2)
            e.tensor_reduce(T.rowf[:, :], pf, AX, ALU.add).then_inc(S.index_step, 1)
            e.wait_ge(S.index_step, 3)
            e.tensor_scalar(T.rowf[:, :], T.rowf[:, :], float(CHUNKS), T.cin[:, C_CHUNK:C_END], ALU.mult, ALU.add)\
             .then_inc(S.index_step, 1)
            e.wait_ge(S.index_step, 4)
            e.tensor_scalar(T.rowf[:, :], T.rowf[:, :], float(-CHUNKS * POOL_PAGES), None, ALU.add)
    nc.all_engine_barrier(sems_to_clear=S.range)


class Tensors:
    pass


def make_tensors(nc, ctx):
    T = Tensors()
    M = Map(nc, nc.sbuf_base)
    T.ps = ctx.enter_context(nc.psum_tensor("ps", [P, 8, 512], F32))
    T.x = M.put("x", [P, TILES, D], F32, M.region(TILES * D * 4))
    T.nc = nc
    T.xth_at = M.region(KD * TOK * 4)
    T.xth = M.put("xth", [P, KD, TOK], F32R, T.xth_at)
    T.xtl = M.put("xtl", [P, KD, TOK], F32R, M.region(KD * TOK * 4))
    T.raw_at = M.region(RAW * BLK * 4)
    T.raw = M.put("raw", [P, RAW, BLK], F32, T.raw_at)
    T.hi_at = M.region(SPLIT * BLK * 4)
    T.whi = M.put("whi", [P, SPLIT, BLK], F32R, T.hi_at)
    T.lo_at = M.region(SPLIT * BLK * 4)
    T.wlo = M.put("wlo", [P, SPLIT, BLK], F32R, T.lo_at)
    T.gb_at = M.region(2 * D * 4)
    T.gb = M.put("gb", [P, 2, D], F32, T.gb_at)
    T.silu = M.put("silu", [P, TOK], F32, T.gb_at)
    T.hf = M.put("hf", [P, 2, TOK], F32, T.gb_at + TOK * 4)
    T.small_at = M.region(8192)
    M2 = Map(nc, T.small_at)
    T.ident = M2.put("ident", [P, P], F32, M2.region(P * 4))
    T.eps = M2.put("eps", [P, 2], F32, M2.region(8))
    T.stats = M2.put("stats", [P, 2, 6], F32, M2.region(48))
    T.mv = M2.put("mv", [P, TILES, 2], F32, M2.region(40))
    T.std = M2.put("std", [P, TILES], F32, M2.region(20))
    T.rstd = M2.put("rstd", [P, TILES], F32, M2.region(20))
    T.nb = M2.put("nb", [P, TILES], F32, M2.region(20))
    T.rope = M2.put("rope", [P, TILES, 2 * ROPE_W], F32, M2.region(TILES * 2 * ROPE_W * 4))
    T.qdelta = M2.put("qdelta", [P, DEC_T], F32, M2.region(DEC_T * 4))
    T.tri8 = M2.put("tri8", [P, DEC_T], F32, M2.region(DEC_T * 4))
    T.identb = M2.put("identb", [P, P], BF16, M2.region(P * 2))
    T.trib = M2.put("trib", [P, P], BF16, M2.region(P * 2))
    T.selb = M2.put("selb", [SAMPLE, DEC_B // 2, P], BF16, M2.region(DEC_B // 2 * P * 2))
    T.tri8b = M2.put("tri8b", [P, DEC_T], BF16, M2.region(DEC_T * 2))
    T.iw = M2.put("iw", [P, TILES, IH], F32, M2.region(TILES * IH * 4))
    T.pages = M2.put("pages", [P, DEC_B, PAGES], I32, M2.region(DEC_B * PAGES * 4))
    T.pagef = M2.put("pagef", [P, DEC_B, PAGES], F32, M2.region(DEC_B * PAGES * 4))
    T.rowf = M2.put("rowf", [P, DEC_B], F32, M2.region(DEC_B * 4))
    T.rows = M2.put("rows", [P, DEC_B], mybir.dt.uint32, M2.region(DEC_B * 4))
    T.misc = M2.put("misc", [P, 256], F32, M2.region(1024))
    assert M2.top <= T.small_at + 8192
    T.arena = M.region(2 * KF * TOK * 4)
    T.hth = M.put("hth", [P, KF, TOK], F32R, T.arena)
    T.cin = M.put("cin", [P, C_END], F32, T.arena)
    T.htl = M.put("htl", [P, KF, TOK], F32R, T.arena + KF * TOK * 4)
    T.M = M
    assert M.top <= nc.sbuf_usable_end, (M.top, nc.sbuf_usable_end)
    return T


ZC = N_IN // 4
ZK = [(0, 3), (3, 6), (6, 8)]
UC = QB // 2
IW_SCALE = (IH * ID) ** -0.5
PROJ_SEMS = STREAM_SEMS + [
    "row_step", "wuk_zero",
    "par_in", "pad_zero", "z_act", "z_dve", "sq_done", "rms_std", "rms_rstd", "dve_step", "rope_done",
    "norm_q", "norm_kv", "rows_out", "stacked", "sb_done", "stack_zero", "late_done", "rows_back", "kcomb_done", "kdup_done", "icomb_done", "iw_done",
    "turned", "turned_act", "turned_dve", "cqh_done", "cql_done", "qb_act", "qb_dve", "qlat_ps", "qlat_done"]


def proj_tensors(T):
    A = Map(T.nc, T.arena)
    T.pg = T.M.put("pg", [P, 4, PAGES, ROW], F32, A.top)
    p = lambda name, shape, at=None: T.M.put(name, shape, F32, A.region(int(np.prod(shape[1:])) * 4) if at is None else at)
    T.qlatT = p("qlatT", [P, BH, TOK])
    T.qaT = p("qaT", [P, AH // 2, TOK])
    T.combT = p("combT", [P, 4, TOK])
    T.kT2 = p("kT2", [P, TOK])
    T.kcT = p("kcT", [P, TOK])
    T.ckvT = p("ckvT", [P, TOK])
    r = lambda name, shape, at=None: T.M.put(name, shape, F32R, A.region(int(np.prod(shape[1:])) * 4) if at is None else at)
    T.QLh = r("QLh", [P, DEC_B, P], T.gb_at + 4096)
    T.QLl = r("QLl", [P, DEC_B, P], T.gb_at - 4096)
    T.newT_at = A.top
    T.newT = r("newT", [P, 3, SAMPLE])
    T.newcT = r("newcT", [P, 2, SAMPLE])
    T.z_at = A.top
    T.z = p("z", [P, TILES, N_IN])
    T.comb_at = A.top
    T.QI_at = A.top
    T.QI = r("QI", [P, DEC_B, P], A.top)
    T.QP = r("QP", [P, DEC_B, P], A.top + 4096)
    T.QA = r("QA", [P, DEC_B, P], A.top + 8192)
    T.QB = r("QB", [P, DEC_B, P], A.top + 12288)
    T.score_at = A.top + 16384
    T.comb = p("comb", [P, TILES, IH, ID + PE_D])
    T.qn = p("qn", [P, TILES, BH * NOPE])
    T.qpe = p("qpe", [P, TILES, BH, PE_D])
    assert A.top <= T.arena + 2 * KF * TOK * 4, A.top - T.arena
    X = Map(T.nc, T.xth_at)
    T.cqh = T.M.put("cqh", [P, 2, TOK], F32R, X.region(2 * TOK * 4))
    T.cql = T.M.put("cql", [P, 2, TOK], F32R, X.region(2 * TOK * 4))
    T.qnT = T.M.put("qnT", [P, BH // 2, TOK], F32, X.region(BH // 2 * TOK * 4))
    T.wukT = T.M.put("wukT", [P, BH, P], F32, X.region(BH * P * 4))
    T.kcomb = T.M.put("kcomb", [P, TILES, 2, ID + PE_D], F32, X.region(TILES * P * 4))
    T.kdup = T.M.put("kdup", [P, TILES, 2, AD], F32, X.region(TILES * P * 4))
    T.sI = T.M.put("sI", [SAMPLE, IH, P], F32R, X.region(IH * P * 4))
    T.sA = T.M.put("sA", [SAMPLE, AH, P], F32R, T.xth_at)
    T.sB = T.M.put("sB", [SAMPLE, AH, P], F32R, T.xth_at + 4096)
    T.sN = T.M.put("sN", [SAMPLE, 3, P], F32R, T.gb_at + 2048)
    T.tmp_at = X.top
    T.tmp = [T.M.put(f"rope{i}", [P, TILES * 8 * 16], F32, X.region(TILES * 8 * 16 * 4)) for i in range(2)]
    T.sP = T.M.put("sP", [SAMPLE, BH, P], F32R, T.tmp_at)
    assert X.top <= T.xth_at + 2 * KD * TOK * 4
    G = Map(T.nc, T.gb_at)
    T.wuv = T.M.put("wuv", [P, BH, VD], F32, G.region(BH * VD * 4))
    T.wuk = T.M.put("wuk", [P, BH, NOPE], F32, G.region(BH * NOPE * 4))
    T.gains = T.M.put("gains", [P, QL + RL], F32, G.region((QL + RL) * 4))
    T.tmp += [T.M.put("rope2", [P, TILES * 8 * 16], F32, G.region(TILES * 8 * 16 * 4))]
    assert G.top <= T.gb_at + 2 * D * 4
    T.ssq = T.misc[:, 0:10]
    T.sstd = T.misc[:, 10:20]
    T.srstd = T.misc[:, 20:30]
    T.wcol = T.misc[:, 32:40]
    T.stop = T.misc[0:SAMPLE, 48:56]


def proj_block(nc, T, S, l, W, O):
    load, hi, lo = stream_ops(T, S)
    NZ = 12

    class Group:
        def __init__(s, src, dst, wait, engine, only=None):
            s.src, s.dst, s.wait, s.engine, s.only = src, dst, wait, engine, only

    z = T.z
    tiles = range(TILES)

    def colsT(bank, w=TOK):
        return T.ps[:, :, :].rearrange("p b c -> p (b c)")[:, bank * 512:bank * 512 + w]

    def half_cols(q, half):
        return q[:, :, :].rearrange("p (b u) (w h t) -> p b u w h t", u=2, w=2, h=8)[:, :, half, half]

    def aq(i):
        return lambda r, t: z[0:r, t, i * P:(i + 1) * P]

    g1 = [Group(lambda r, h: T.wuk[:, 2 * h:2 * h + 2, :].rearrange("p h c -> p (h c)"), T.wukT,
                ("par_in", 64), "act", "wuk")]
    g1 += [Group(aq(i), T.qaT[:, i, :], ("rope_done", 2), "act") for i in range(4)]
    g1 += [Group(lambda r, t: z[0:r, t, Z_CQ:Z_CQ + P], 0, ("norm_q", TILES), "both"),
           Group(lambda r, t: z[0:r, t, Z_CQ + P:Z_CQ + 2 * P], 1, ("norm_q", TILES), "both"),
           Group(lambda r, t: T.kdup[0:r, t, :, :].rearrange("p a c -> p (a c)"), T.kT2[:, :], ("kdup_done", 2), "dve")]
    g2 = [Group(lambda r, t, i=i: T.qn[0:r, t, i * P:(i + 1) * P],
                T.qnT[:, i, :], ("qb_dve", 8), "dve" if i % 2 else "act") for i in range(4)]
    g2 += [Group(lambda r, t: T.kcomb[0:r, t, :, :].rearrange("p a c -> p (a c)"), T.kcT[:, :], ("kcomb_done", 4), "act"),
           Group(lambda r, t: z[0:r, t, Z_CKV:Z_KPE], T.ckvT[:, :], ("norm_kv", TILES), "dve")]
    N_CKV = len(g1) + len(g2) - 1
    g2 += [Group(lambda r, t, i=i: T.comb[0:r, t, 2 * i:2 * i + 2, :].rearrange("p h c -> p (h c)"), T.combT[:, i, :],
                 ("icomb_done", 1), "act" if i % 2 else "dve") for i in range(4)]
    NQ = len(g1) + len(g2)
    for i, (src, dst) in enumerate(((T.sA, T.QA), (T.sB, T.QB), (T.sI, T.QI), (T.sP, T.QP))):
        g2.append(Group(lambda r, h, src=src: src[:, h, :].bitcast(F32), dst, ("stacked", 12), "act" if i % 2 else "dve", "heads"))
    g2.append(Group(lambda r, h: T.sN[:, h, :].bitcast(F32), T.newT, ("stacked", 12), "act", "new"))
    groups = g1 + g2
    outs = []
    nact = ndve = 0
    for g in groups:
        if g.engine == "both":
            outs.append(("cql_done", g.dst + 1))
        elif g.engine == "act":
            nact += 1
            outs.append(("turned_act", nact))
        else:
            ndve += 1
            outs.append(("turned_dve", ndve))

    def turn(e, gi, first_bank_wait):
        g = groups[gi]
        e.wait_ge(S.all[g.wait[0]], g.wait[1])
        if g.wait[0] == "stacked":
            e.wait_ge(S.sb_done, 2)
        if g.wait[0] == "icomb_done":
            e.wait_ge(S.rope_done, 8)
        if NQ <= gi < NQ + 4:
            e.wait_ge(S.qlat_done, 5 + gi % 4)
        elif first_bank_wait is not None:
            e.wait_ge(S.all[outs[first_bank_wait][0]], outs[first_bank_wait][1])
        b = 2 * (gi % 4)
        if g.only is None:
            for t in tiles:
                r = ROWS[t]
                mm = e.transpose(colsT(b)[:, t * P:t * P + r], g.src(r, t), T.ident[0:r, 0:r])
        elif g.only == "new":
            for h in range(3):
                mm = e.transpose(colsT(b)[:, h * SAMPLE:(h + 1) * SAMPLE], g.src(0, h), T.ident[0:SAMPLE, 0:SAMPLE])
        elif g.only == "heads":
            for h in range(8):
                mm = e.transpose(colsT(b)[:, h * SAMPLE:(h + 1) * SAMPLE], g.src(0, h), T.ident[0:SAMPLE, 0:SAMPLE])
        else:
            for h in range(4):
                mm = e.transpose(colsT(b)[:, h * P:(h + 1) * P], g.src(0, h), T.ident[:, :])
        mm.then_inc(S.turned, 1)

    def out(e, gi, who):
        g = groups[gi]
        if g.engine != who and g.engine != "both":
            return
        e.wait_ge(S.turned, gi + 1)
        b = 2 * (gi % 4)
        if g.engine == "both":
            if who == "act":
                e.activation(T.cqh[:, g.dst, :], colsT(b), ACT.Copy).then_inc(S.cqh_done, 1)
            else:
                e.wait_ge(S.cqh_done, g.dst + 1)
                e.tensor_tensor(T.cql[:, g.dst, :], colsT(b), T.cqh[:, g.dst, :].bitcast(F32), ALU.subtract)\
                 .then_inc(S.cql_done, 1)
            return
        if g.only is None:
            dst, src = g.dst, colsT(b)
        elif g.only == "new":
            dst, src = g.dst[:, :, :].rearrange("p n c -> p (n c)"), colsT(b, 3 * SAMPLE)
        elif g.only == "heads":
            for half in range(2):
                dst = half_cols(g.dst, half)
                src = colsT(b, 512).rearrange("p (h b u t) -> p b u h t", h=8, b=DEC_B // 2, u=2)[:, :, half]
                e.wait_ge(S.stack_zero, 4)
                ins = e.activation(dst, src, ACT.Copy) if who == "act" else e.tensor_copy(dst, src)
            ins.then_inc(S.turned_act if who == "act" else S.turned_dve, 1)
            return
        else:
            e.wait_ge(S.wuk_zero, 1)
            for par in range(2):
                rows = slice(64 * par, 64 * par + 64)
                ins = e.activation(T.wukT[rows, :, :].rearrange("p (a u) c -> p a u c", u=2)[:, :, par],
                                   colsT(b, 512)[rows, :].rearrange("p (a c) -> p a c", a=4), ACT.Copy)
            ins.then_inc(S.turned_act, 1)
            return
        if who == "act":
            e.activation(dst, src, ACT.Copy).then_inc(S.turned_act, 1)
        else:
            e.tensor_copy(dst, src).then_inc(S.turned_dve, 1)

    def q_out(copy, c, t):
        r = ROWS[t]
        q = T.ps[0:r, (5 * c + t) % 8, 0:UC].rearrange("p (h c) -> p h c", h=4)
        copy(T.qn[0:r, t, c * 4 * NOPE:(c + 1) * 4 * NOPE].rearrange("p (h c) -> p h c", h=4), q[:, :, 0:NOPE])
        copy(T.qpe[0:r, t, 4 * c:4 * c + 4, :], q[:, :, NOPE:NOPE + PE_D])

    def z_free(e, ev):
        c, t = ev // 5, ev % 5
        e.wait_ge(*((S.z_act, 3 * c + t // 2 + 1) if t % 2 == 0 else (S.z_dve, 2 * c + t // 2 + 1)))

    with nc.Block() as block:
        @block.sync
        def _(e):
            e.dma_start(T.gains[:, 0:QL], W["mla_q_norm"][bass.ds(l, 1), :].partition_broadcast(P)).then_inc(S.par_in, 16)
            e.dma_start(T.gains[:, QL:QL + RL], W["mla_kv_norm"][bass.ds(l, 1), :].partition_broadcast(P)).then_inc(S.par_in, 16)
            e.dma_start(T.wuk[:, :, :], W["mla_w_uk"][bass.ds(l, 1)].rearrange("l r h n -> r (l h) n")).then_inc(S.par_in, 16)
            e.dma_start(T.wuv[:, :, :], W["mla_w_uv"][bass.ds(l, 1)].rearrange("l r h n -> r (l h) n")).then_inc(S.par_in, 16)
            for n in range(NZ + 2):
                if n < NZ:
                    c, (k0, k1) = n // 3, ZK[n % 3]
                    src = W["w_in"][bass.ds(l, 1), k0 * P:k1 * P, c * ZC:(c + 1) * ZC].rearrange("l (k p) c -> p (l k) c", p=P)
                    load(e, n, n % RAW, src, shape=(k1 - k0, ZC), first=n < RAW)
                else:
                    c = n - NZ
                    src = W["mla_w_uq"][bass.ds(l, 1), :, c * UC:(c + 1) * UC].rearrange("l (k p) c -> p (l k) c", p=P)
                    load(e, n, n % RAW, src, shape=(2, UC))
            e.wait_ge(S.rope_done, 6)
            e.wait_ge(S.norm_kv, TILES)
            for pr, sm, lo_, hi_, at in (("dsa_p", "dsa_s", Z_AK, Z_IQ, 0), ("dsa_p", "dsa_s", Z_IK, Z_IW, 2 * AD),
                                         ("mla_p", "mla_s", Z_CKV, N_IN, 0)):
                w = hi_ - lo_
                e.dma_start(O[pr][bass.ds(l, 1), 0, 0:S0, at:at + w].rearrange("l (t p) c -> p (l t) c", p=P),
                            z[:, 0:4, lo_:hi_]).then_inc(S.rows_out, 16)
                e.dma_start(O[pr][bass.ds(l, 1), 0, S0:PROMPT, at:at + w].rearrange("l p c -> (l p) c"),
                            z[SAMPLE:ROWS[4], 4, lo_:hi_]).then_inc(S.rows_out, 16)
                e.dma_start(O[sm][bass.ds(l, 1), :, :, at:at + w].rearrange("l b t c -> (l b t) c"),
                            z[0:SAMPLE, 4, lo_:hi_]).then_inc(S.rows_out, 16)
            e.wait_ge(S.iw_done, 1)
            e.dma_start(O["iw_scratch"][:, :], T.iw[0:SAMPLE, 4, :]).then_inc(S.rows_out, 16)
            e.wait_ge(S.rows_out, 160)
            e.wait_ge(S.norm_q, TILES)
            for h in range(IH):
                for b2 in range(2):
                    e.dma_start(T.wcol[64 * b2 + 8 * h:64 * b2 + 8 * h + 8, :],
                                O["iw_scratch"].rearrange("(b t) h -> t b h", t=DEC_T)[:, :, h:h + 1]
                                .rearrange("t b h -> t (b h)"), allow_slow_non_contiguous=True)\
                     .then_inc(S.rows_back, 16)
            e.wait_ge(S.rows_back, 16 * 16)

        @block.gpsimd
        def _(e):
            e.tensor_scalar(T.rowf[:, :], T.rowf[:, :], float(CHUNKS * POOL_PAGES), None, ALU.add)\
             .then_inc(S.row_step, 1)
            e.wait_ge(S.row_step, 1)
            e.tensor_copy(T.rows[:, :], T.rowf[:, :])
            e.wait_ge(S.w_used, NZ)
            e.memset(T.wukT[:, :, :], 0.0).then_inc(S.wuk_zero, 1)
            e.wait_ge(S.rope_done, 2)
            for i in range(2):
                e.tensor_copy(T.kdup[:, :, i, :], z[:, :, Z_AK:Z_AV]).then_inc(S.kdup_done, 1)
            e.wait_ge(S.rope_done, 4)
            e.tensor_copy(T.comb[:, :, :, 0:ID], z[:, :, Z_IQ:Z_IK].rearrange("p t (h c) -> p t h c", h=IH))\
             .then_inc(S.icomb_done, 1)
            for i in range(2):
                e.tensor_copy(T.kcomb[:, :, i, 0:ID], z[:, :, Z_IK:Z_IW]).then_inc(S.kcomb_done, 1)
            e.tensor_scalar(T.iw[:, :, :], z[:, :, Z_IW:Z_CQ], IW_SCALE, 1.0, ALU.mult, ALU.mult).then_inc(S.iw_done, 1)
            e.wait_ge(S.rope_done, 6)
            for i in range(2):
                e.tensor_copy(T.kcomb[:, :, i, ID:ID + PE_D], z[:, :, Z_KPE:N_IN]).then_inc(S.kcomb_done, 1)
            e.wait_ge(S.rope_done, 8)
            e.wait_ge(S.w_used, NZ + 2)
            e.wait_ge(S.turned, len(g1))
            zs = z[0:SAMPLE, 4, :]
            nst = 0

            def halves(hi_dst, lo_dst, src, shape=None):
                nonlocal nst
                e.tensor_copy(hi_dst, src).then_inc(S.stacked, 1)
                nst += 1
                e.wait_ge(S.stacked, nst)
                e.tensor_tensor(lo_dst, src, hi_dst.bitcast(F32), ALU.subtract).then_inc(S.stacked, 1)
                nst += 1

            def four(dst, src, heads):
                return src.unsqueeze(2).to_broadcast([SAMPLE, heads, 2, 32])

            halves(T.sA[:, :, 0:AD], T.sA[:, :, AD:P], zs[:, 0:Z_AK].rearrange("p (h c) -> p h c", h=AH))
            for dst, c in ((T.sI, 0), (T.sP, ID)):
                v = dst[:, :, :].rearrange("p h (a b c) -> p h a b c", a=2, b=2)
                halves(v[:, :, :, 0], v[:, :, :, 1], four(dst, T.comb[0:SAMPLE, 4, :, c:c + 32], 8))
            halves(T.sN[:, 0, 0:AD], T.sN[:, 0, AD:P], zs[:, Z_AK:Z_AV])
            for i, c in ((1, Z_IK), (2, Z_KPE)):
                v = T.sN[:, i, :].rearrange("p (a b c) -> p a b c", a=2, b=2)
                halves(v[:, 0], v[:, 1], zs[:, c:c + 32].unsqueeze(1).to_broadcast([SAMPLE, 2, 32]))
            e.wait_ge(S.stacked, nst)
            e.tensor_copy(T.sB[:, :, 0:AD], T.sA[:, :, AD:P].bitcast(F32)).then_inc(S.sb_done, 1)
            e.tensor_copy(T.sB[:, :, AD:P], T.sA[:, :, 0:AD].bitcast(F32)).then_inc(S.sb_done, 1)

        @block.scalar
        def _(e):
            def z_out(c):
                for t in range(0, TILES, 2):
                    if c == 0 and t == 0:
                        e.wait_ge(S.pad_zero, 1)
                        e.wait_ge(S.w_used, 3)
                    elif t == 0:
                        e.wait_ge(S.w_used, 3 * c + 3)
                    r = ROWS[t]
                    e.activation(z[0:r, t, c * ZC:(c + 1) * ZC], T.ps[0:r, (5 * c + t) % 8, 0:ZC], ACT.Copy)\
                     .then_inc(S.z_act, 1)
            for n in range(NZ + 2):
                w = (ZK[n % 3][1] - ZK[n % 3][0]) * ZC if n < NZ else QB
                hi(e, n, n % RAW, n // RAW, width=w, first=n < SPLIT)
                if n >= 4 and (n - 4) % 3 == 0:
                    z_out((n - 4) // 3)
            e.wait_ge(S.z_act, 12)
            e.wait_ge(S.z_dve, 8)
            for i, (c0, c1) in enumerate(((Z_CQ, Z_CKV), (Z_CKV, Z_KPE))):
                for t in tiles:
                    e.activation(T.ps[:, t, QL * i:QL * i + c1 - c0], z[:, t, c0:c1], ACT.Square,
                                 accum_out=T.ssq[:, 5 * i + t:5 * i + t + 1]).then_inc(S.sq_done, 1)
            for i, w in enumerate((QL, RL)):
                e.wait_ge(S.sq_done, 5 * i + 5)
                e.activation(T.sstd[:, 5 * i:5 * i + 5], T.ssq[:, 5 * i:5 * i + 5], ACT.Sqrt, scale=1.0 / w,
                             bias=T.eps[:, 1:2]).then_inc(S.rms_std, 1)
            for gi in range(len(g1)):
                out(e, gi, "act")
            for c in range(2):
                e.wait_ge(S.w_used, NZ + 1 + c)
                if c == 0:
                    e.wait_ge(S.pad_zero, 2)
                for t in (0, 2, 4):
                    r = ROWS[t]
                    q_out(lambda d, s_: e.activation(d, s_, ACT.Copy).then_inc(S.qb_act, 1), c, t)
            for gi in range(len(g1), NQ):
                out(e, gi, "act")
            for h in range(BH):
                e.wait_ge(S.qlat_ps, h + 1)
                b = 2 * (h % 4)
                e.activation(T.qlatT[:, h, :].rearrange("p (a c) -> p a c", a=2), T.ps[:, b:b + 2, 0:HALF], ACT.Copy)\
                 .then_inc(S.qlat_done, 1)
            e.wait_ge(S.qlat_done, BH)
            e.wait_ge(S.late_done, 2)
            e.wait_ge(S.turned_dve, outs[N_CKV][1])
            for half in range(2):
                src = T.qlatT[:, :, S0:TAIL].rearrange("p h (b u t) -> p b u h t", u=2, t=DEC_T)[:, :, half]
                e.activation(half_cols(T.QLh, half), src, ACT.Copy).then_inc(S.late_done, 1)
            e.activation(T.newcT[:, 0, :], T.ckvT[:, S0:TAIL], ACT.Copy).then_inc(S.late_done, 1)
            for gi in range(NQ, len(groups)):
                out(e, gi, "act")

        @block.vector
        def _(e):
            step = [0]

            def chain(ins):
                step[0] += 1
                ins.then_inc(S.dve_step, 1)
                e.wait_ge(S.dve_step, step[0])

            def z_out(c):
                for t in (1, 3):
                    if t == 1:
                        e.wait_ge(S.w_used, 3 * c + 3)
                    e.tensor_copy(z[:, t, c * ZC:(c + 1) * ZC], T.ps[:, (5 * c + t) % 8, 0:ZC]).then_inc(S.z_dve, 1)

            def rope(x, heads, half, off, dst):
                def table(o):
                    return T.rope[:, :, o:o + half].unsqueeze(2).to_broadcast([P, TILES, heads, half])
                n = TILES * heads * half
                m = [t[:, 0:n].rearrange("p (t h c) -> p t h c", t=TILES, h=heads) for t in T.tmp]
                x1, x2 = x[:, :, :, 0:half], x[:, :, :, half:2 * half]
                cos, sin = table(off), table(ROPE_W + off)
                e.tensor_tensor(m[0], x1, cos, ALU.mult)
                e.tensor_tensor(m[1], x2, sin, ALU.mult)
                chain(e.tensor_tensor(m[2], x1, sin, ALU.mult))
                chain(e.tensor_tensor(m[0], m[0], m[1], ALU.subtract))
                chain(e.tensor_tensor(m[1], x2, cos, ALU.mult))
                e.tensor_copy(dst[:, :, :, 0:half], m[0]).then_inc(S.rope_done, 1)
                e.tensor_tensor(dst[:, :, :, half:2 * half], m[1], m[2], ALU.add).then_inc(S.rope_done, 1)
                rope.n += 2
                e.wait_ge(S.rope_done, rope.n)
            rope.n = 0

            e.memset(z[64:P, 4, :], 0.0).then_inc(S.pad_zero, 1)
            e.memset(T.qpe[64:P, 4, :, :], 0.0).then_inc(S.pad_zero, 1)
            for n in range(NZ + 2):
                w = (ZK[n % 3][1] - ZK[n % 3][0]) * ZC if n < NZ else QB
                lo(e, n, n % RAW, width=w)
                if n >= 4 and (n - 4) % 3 == 0:
                    z_out((n - 4) // 3)
            e.wait_ge(S.z_act, 12)
            e.wait_ge(S.z_dve, 8)
            v = z[:, :, 0:Z_AV].rearrange("p t (h c) -> p t h c", h=AH + 1)
            rope(v, AH + 1, AROT // 2, 0, v)
            def norm(i, c0, c1, sem):
                e.wait_ge(S.rms_std, i + 1)
                e.reciprocal(T.srstd[:, 5 * i:5 * i + 5], T.sstd[:, 5 * i:5 * i + 5]).then_inc(S.rms_rstd, 1)
                e.wait_ge(S.rms_rstd, i + 1)
                if i == 0:
                    e.wait_ge(S.par_in, 64)
                for t in tiles:
                    e.scalar_tensor_tensor(z[:, t, c0:c1], z[:, t, c0:c1], T.srstd[:, 5 * i + t:5 * i + t + 1],
                                           T.gains[:, c0 - Z_CQ:c1 - Z_CQ], ALU.mult, ALU.mult).then_inc(sem, 1)
            norm(0, Z_CQ, Z_CKV, S.norm_q)
            v = z[:, :, Z_IQ:Z_IW].rearrange("p t (h c) -> p t h c", h=IH + 1)
            rope(v, IH + 1, IROT // 2, AROT // 2, v)
            v = z[:, :, Z_KPE:N_IN].rearrange("p t (h c) -> p t h c", h=1)
            rope(v, 1, PE_D // 2, AROT // 2 + IROT // 2, v)
            norm(1, Z_CKV, Z_KPE, S.norm_kv)
            for gi in range(len(g1)):
                out(e, gi, "dve")
            for c in range(2):
                e.wait_ge(S.w_used, NZ + 1 + c)
                for t in (1, 3):
                    q_out(lambda d, s_: e.tensor_copy(d, s_).then_inc(S.qb_dve, 1), c, t)
            e.wait_ge(S.qb_act, 12)
            e.wait_ge(S.qb_dve, 8)
            rope(T.qpe[:, :, :, :], BH, PE_D // 2, AROT // 2 + IROT // 2, T.comb[:, :, :, ID:ID + PE_D])
            for gi in range(len(g1), NQ):
                out(e, gi, "dve")
            for q in (T.QLh, T.QLl):
                e.memset(q[:, :, :].bitcast(F32), 0.0).then_inc(S.late_done, 1)
            e.wait_ge(S.turned, NQ)
            e.wait_ge(S.stacked, 6)
            for q in (T.QA, T.QB, T.QI, T.QP):
                e.memset(q[:, :, :].bitcast(F32), 0.0).then_inc(S.stack_zero, 1)
            e.wait_ge(S.late_done, 5)
            for half in range(2):
                src = T.qlatT[:, :, S0:TAIL].rearrange("p h (b u t) -> p b u h t", u=2, t=DEC_T)[:, :, half]
                e.tensor_tensor(half_cols(T.QLl, half), src, half_cols(T.QLh, half).bitcast(F32), ALU.subtract)
            e.tensor_tensor(T.newcT[:, 1, :], T.ckvT[:, S0:TAIL], T.newcT[:, 0, :].bitcast(F32), ALU.subtract)
            for gi in range(NQ, len(groups)):
                out(e, gi, "dve")

        @block.tensor
        def _(e):
            for n in range(NZ):
                c, (k0, k1) = n // 3, ZK[n % 3]
                s = n % SPLIT
                e.wait_ge(S.split_done, n + 1)
                for t in tiles:
                    ev = 5 * c + t
                    if n % 3 == 0 and ev >= 8:
                        z_free(e, ev - 8)
                    o = slice(t * P, t * P + ROWS[t])
                    for k in range(k0, k1):
                        w = slice((k - k0) * ZC, (k - k0 + 1) * ZC)
                        mm = three(e, T.ps[0:ROWS[t], ev % 8, 0:ZC], T.xth[:, k, o], T.xtl[:, k, o],
                                   T.whi[:, s, w], T.wlo[:, s, w], k == 0, k == KD - 1)
                mm.then_inc(S.w_used, 1)
            for gi in range(len(g1)):
                if gi == 0:
                    e.wait_ge(S.z_act, 12)
                    e.wait_ge(S.z_dve, 8)
                    e.wait_ge(S.sq_done, 10)
                turn(e, gi, gi - 4 if gi >= 4 else None)
            for gi in range(len(g1) - 4, len(g1)):
                e.wait_ge(S.all[outs[gi][0]], outs[gi][1])
            for c in range(2):
                n = NZ + c
                s = n % SPLIT
                e.wait_ge(S.split_done, n + 1)
                e.wait_ge(S.cql_done, 2)
                for t in tiles:
                    if 5 * c + t >= 8:
                        e.wait_ge(S.qb_act, 2)
                        e.wait_ge(S.qb_dve, 2)
                    o = slice(t * P, t * P + ROWS[t])
                    for k in range(2):
                        w = slice(k * UC, (k + 1) * UC)
                        mm = three(e, T.ps[0:ROWS[t], (5 * c + t) % 8, 0:UC], T.cqh[:, k, o], T.cql[:, k, o],
                                   T.whi[:, s, w], T.wlo[:, s, w], k == 0, k == 1)
                mm.then_inc(S.w_used, 1)
            e.wait_ge(S.qb_act, 12)
            e.wait_ge(S.qb_dve, 8)
            for gi in range(len(g1), NQ):
                turn(e, gi, gi - 4 if gi >= len(g1) + 4 else None)
            for gi in range(NQ - 8, NQ):
                e.wait_ge(S.all[outs[gi][0]], outs[gi][1])
            for h in range(BH):
                if h >= 4:
                    e.wait_ge(S.qlat_done, h - 3)
                for a in range(2):
                    mm = e.matmul(T.ps[:, 2 * (h % 4) + a, 0:HALF], T.wukT[:, h, :],
                                  T.qnT[:, h // 2, a * HALF:(a + 1) * HALF], start=True, stop=True)
                mm.then_inc(S.qlat_ps, 1)
            for gi in range(NQ, len(groups)):
                turn(e, gi, gi - 4)
    nc.all_engine_barrier(sems_to_clear=S.range)


PROMPT_SEMS = ["s_round_max", "s_round_done", "tail_in", "given_set", "weighted", "pads_zero", "pe_keys", "key_step", "s_ps", "s_read", "scored", "max_done", "nmax_done", "round_max", "round_done",
               "biased", "bias_done", "b_ps", "b_out", "pv_done", "rinv_done", "o_done", "mix_lo", "mix_hi"]
ROUNDS = (TOPK_P + 7) // 8
GIVEN = ROUNDS * 8 - TOPK_P
QT = [P, P, P, P, PROMPT - 4 * P]
QC = [0, P, 2 * P, 3 * P, TAIL]
NK = [P, 2 * P, 3 * P, 4 * P, PROMPT]
D_SCALE = AD ** -0.5
M_SCALE = (NOPE + PE_D) ** -0.5


STEP_UNITS = [("M", 0), ("D", 0), ("D", 1), ("D", 2), ("D", 3), ("D", 4)]
STEPS_HERE = 8 * len(STEP_UNITS)
STEPS_THERE = 2 * TOPK_S // 8 - STEPS_HERE


def sample_step(e, T, S, j):
    if j % 2 == 0:
        if j > 0:
            e.wait_ge(S.s_round_done, j // 2)
        e.max(T.stop[:, :], T.score[:, :]).then_inc(S.s_round_max, 1)
    else:
        e.wait_ge(S.s_round_max, j // 2 + 1)
        e.match_replace(T.score[:, :], T.stop[:, :], T.score[:, :], TAKEN).then_inc(S.s_round_done, 1)


def prompt_block(nc, T, S):
    units = [(kind, t, h) for t in range(5) for kind in "MD" for h in range(8)]
    rounds = [3, 3, 3, 3, 3, 2, 0, 0]
    assert sum(rounds) == ROUNDS
    n = len(units)
    A = Map(T.nc, T.raw_at)
    Pb = T.M.put("pP", [P, 3, PROMPT], F32, A.region(3 * PROMPT * 4))
    PT = T.M.put("pPT", [P, 2, 512], F32, A.region(2 * 512 * 4))
    work = T.M.put("pwork", [P, GIVEN + PROMPT], F32, A.region((GIVEN + PROMPT) * 4))
    relu = T.M.put("prelu", [P, 2, PROMPT], F32, A.region(2 * PROMPT * 4))
    osb = T.M.put("posb", [P, 1024], F32, A.region(4096))
    olT = T.M.put("polT", [P, 8, P], F32, A.region(4096))
    G = Map(T.nc, T.gb_at + BH * VD * 4)
    bias = T.M.put("pbias", [P, PROMPT], BF16, G.region(PROMPT * 2))
    vt = T.M.put("pvt", [P, AD + RL], F32, G.region((AD + RL) * 4))
    assert G.top <= T.gb_at + 4096
    iwt = T.M.put("piwt", [P, IH], F32, A.region(IH * 4))
    mx = T.M.put("pmx", [P, 3], F32, A.region(12))
    nmx = T.M.put("pnmx", [P, 3], F32, A.region(12))
    top = T.M.put("ptop", [P, 8], F32, A.region(32))
    rsum = T.M.put("prsum", [P, 2, 8], F32, A.region(64))
    rinv = T.M.put("prinv", [P, 2, 8], F32, A.region(64))
    tail = T.score_at + (SKEYS * 4 + 63) // 64 * 64
    pads = [T.M.put(f"pkeys{i}", [P, PROMPT], F32, at) for i, at in
            enumerate((tail, tail + PROMPT * 4, T.QI_at, A.region(PROMPT * 4)))]
    assert tail + 2 * PROMPT * 4 <= T.arena + 2 * KF * TOK * 4
    pe_keys = pads[0:2]
    i_keys = [T.kcT, pads[2]]
    a_keys = [T.kT2, pads[3]]
    assert A.top <= T.gb_at - 4096
    flat = T.ps[:, :, :].rearrange("p b c -> p (b c)")
    SB = lambda s, r, w: flat[0:r, (s % 2) * 1024:(s % 2) * 1024 + w]
    BB = lambda q: flat[:, (4 + q % 2) * 512:(5 + q % 2) * 512]

    plan, s_job, b_job = [], 0, 0
    b_kind = []
    lag = n + 6
    last = {}
    for i in range(lag):
        p = dict(idx=None, s=None, t=None, pv=None, norm=None, ot=[], uv=None)
        if i < n:
            kind, t, h = units[i]
            if kind == "D" and t < 4:
                p["idx"] = (s_job, t + 1, h)
                s_job += 1
            p["s"] = s_job
            s_job += 1
            if h == 7:
                last[i] = (kind, t)
        if 0 <= i - 1 < n:
            p["t"] = b_job
            b_kind.append("P")
            b_job += 1
        if 0 <= i - 2 < n:
            p["pv"] = i - 2
        if i - 2 in last:
            p["norm"] = last[i - 2]
        if i - 3 in last:
            kind, t = last[i - 3]
            for a in range(2 if kind == "M" else 1):
                p["ot"].append((b_job, kind, t, a))
                b_kind.append("O" if kind == "M" else "X")
                b_job += 1
        if i - 4 in last and last[i - 4][0] == "M":
            p["uv"] = (b_job, last[i - 4][1])
            b_kind.append("X")
            b_job += 1
        plan.append(p)
    tjob = {i - 1: p["t"] for i, p in enumerate(plan) if p["t"] is not None}

    def b_free(e, q):
        if q < 2:
            return
        kinds = b_kind[:q - 1]
        if kinds[-1] == "X":
            e.wait_ge(S.mix_lo, kinds.count("X"))
        else:
            e.wait_ge(S.b_out, len(kinds) - kinds.count("X"))

    def groups_before(i):
        return sum(1 for g in last if g <= i)

    def k_at(pad, k0, w):
        if k0 == TAIL and pad in pads:
            k0 = S0
        return pad[:, k0:k0 + w]

    def pad_copy(pad, src, rows):
        return [(pad[rows, c:c + w], src[rows, k0:k0 + w]) for c, k0, w in ((0, 0, S0), (S0, TAIL, PROMPT - S0))]

    def keys(t):
        return [(0, 0, min(NK[t], 512))] + ([(512, TAIL, 16)] if t == 4 else [])

    def key_tiles(t):
        return [(k, P) for k in range(min(t + 1, 4))] + ([(4, 16)] if t == 4 else [])

    with nc.Block() as block:
        @block.sync
        def _(e):
            src = T.z[SAMPLE:ROWS[4], 4, :]
            e.dma_start(vt[0:16, 0:AD], src[:, Z_AV:Z_IQ]).then_inc(S.tail_in, 16)
            e.dma_start(vt[0:16, AD:AD + RL], src[:, Z_CKV:Z_KPE]).then_inc(S.tail_in, 16)
            e.dma_start(iwt[0:16, :], T.iw[SAMPLE:ROWS[4], 4, :]).then_inc(S.tail_in, 16)

        @block.gpsimd
        def _(e):
            for pad in pads:
                e.memset(pad[:, :], 0.0).then_inc(S.pads_zero, 1)
            e.memset(work[:, 0:GIVEN], 3.0e38).then_inc(S.given_set, 1)
            nw = [0]
            for i, p in enumerate(plan):
                if p["idx"]:
                    s, t, h = p["idx"]
                    r = QT[t]
                    if t > 1 and h == 0:
                        e.wait_ge(S.biased, t - 1)
                        e.memset(work[:, 0:GIVEN], 3.0e38).then_inc(S.given_set, 1)
                    if t == 4 and h == 0:
                        e.wait_ge(S.tail_in, 48)
                    e.wait_ge(S.s_read, s + 1)
                    w = T.iw[0:r, t, h:h + 1] if t < 4 else iwt[0:r, h:h + 1]
                    sc, re = work[0:r, GIVEN:GIVEN + NK[t]], relu[0:r, (8 * (t - 1) + h) % 2, 0:NK[t]]
                    if h == 0:
                        e.tensor_scalar(sc, re, w, 1.0, ALU.mult, ALU.mult).then_inc(S.scored, 1)
                    else:
                        nw[0] += 1
                        e.tensor_scalar(re, re, w, 1.0, ALU.mult, ALU.mult).then_inc(S.weighted, 1)
                        e.wait_ge(S.weighted, nw[0])
                        e.wait_ge(S.scored, 8 * (t - 1) + h)
                        e.tensor_tensor(sc, sc, re, ALU.add).then_inc(S.scored, 1)

        @block.tensor
        def _(e):
            for i, p in enumerate(plan):
                if p["idx"]:
                    s, t, h = p["idx"]
                    if s >= 2:
                        e.wait_ge(S.s_read, s - 1)
                    r = QT[t]
                    if t == 1 and h == 0:
                        e.wait_ge(S.key_step, 7)
                    for c, k0, w in keys(t):
                        mm = e.matmul(SB(s, r, PROMPT)[:, c:c + w], T.combT[:, h // 2, QC[t]:QC[t] + r],
                                      k_at(i_keys[h % 2], k0, w), start=True, stop=True)
                    mm.then_inc(S.s_ps, 1)
                if p["s"] is not None:
                    kind, t, h = units[i]
                    s = p["s"]
                    r, q = QT[t], slice(QC[t], QC[t] + QT[t])
                    if i == 0:
                        e.wait_ge(S.pe_keys, 4)
                    if s >= 2:
                        e.wait_ge(S.s_read, s - 1)
                    if kind == "D" and h == 0:
                        e.wait_ge(S.bias_done, t + 1)
                    for c, k0, w in keys(t):
                        out = SB(s, r, PROMPT)[:, c:c + w]
                        if kind == "M":
                            e.matmul(out, T.qlatT[:, h, q], T.ckvT[:, k0:k0 + w], start=True, stop=False)
                            diag = t if t < 4 else (4 if c else None)
                            mm = e.matmul(out, T.combT[:, h // 2, q], k_at(pe_keys[h % 2], k0, w),
                                          start=False, stop=diag is None)
                            if diag is not None:
                                d = SB(s, r, PROMPT)[:, diag * P:diag * P + r]
                                mm = e.matmul(d, T.identb[:, 0:r], T.trib[:, 0:r], start=False, stop=True)
                        else:
                            e.matmul(out, T.qaT[:, h // 2, q], k_at(a_keys[h % 2], k0, w), start=True, stop=False)
                            mm = e.matmul(out, T.identb[:, 0:r], bias[:, c:c + w], start=False, stop=True)
                    mm.then_inc(S.s_ps, 1)
                if p["t"] is not None:
                    u = i - 1
                    kind, t, h = units[u]
                    q = p["t"]
                    e.wait_ge(S.s_read, plan[u]["s"] + 1)
                    b_free(e, q)
                    r = QT[t]
                    for k, kr in key_tiles(t):
                        mm = e.transpose(BB(q)[0:kr, k * P:k * P + r] if t < 4 else BB(q)[0:kr, k * 16:k * 16 + 16],
                                         Pb[0:r, u % 3, k * P:k * P + kr], T.ident[0:r, 0:r])
                    mm.then_inc(S.b_ps, 1)
                if p["pv"] is not None:
                    u = p["pv"]
                    kind, t, h = units[u]
                    q = tjob[u]
                    e.wait_ge(S.b_out, sum(1 for x in b_kind[:q + 1] if x != "X"))
                    if h == 0 and u > 0:
                        e.wait_ge(S.o_done, groups_before(u - 1))
                    r = QT[t]
                    w, at = (RL, Z_CKV) if kind == "M" else (AD, Z_AV)
                    kts = key_tiles(t)
                    if t == 4:
                        e.wait_ge(S.tail_in, 48)
                    for k, kr in kts:
                        lhs = PT[0:kr, u % 2, k * P:k * P + r] if t < 4 else PT[0:kr, u % 2, k * 16:k * 16 + 16]
                        if k < 4:
                            v = T.z[0:kr, k, at:at + w]
                        else:
                            v = vt[0:16, 0:AD] if kind == "D" else vt[0:16, AD:AD + RL]
                        mm = e.matmul(flat[0:r, 6 * 512 + h * w:6 * 512 + (h + 1) * w], lhs, v,
                                      start=k == kts[0][0], stop=k == kts[-1][0])
                    mm.then_inc(S.pv_done, 1)
                for q, kind, t, a in p["ot"]:
                    r = QT[t]
                    e.wait_ge(S.o_done, groups_before(i - 3))
                    b_free(e, q)
                    for k in range(4):
                        c = (4 * a + k) * P
                        mm = e.transpose(BB(q)[:, k * P:k * P + r], osb[0:r, c:c + P], T.ident[0:r, 0:r])
                    mm.then_inc(S.b_ps, 1)
                if p["uv"]:
                    q, t = p["uv"]
                    r = QT[t]
                    b_free(e, q)
                    e.wait_ge(S.b_out, sum(1 for x in b_kind[:q] if x != "X"))
                    for h in range(8):
                        b = 64 * (h % 2)
                        mm = e.matmul(BB(q)[b:b + VD, (h // 2) * P:(h // 2) * P + r], T.wuv[:, h, :], olT[:, h, 0:r],
                                      start=True, stop=True)
                    mm.then_inc(S.b_ps, 1)

        def mix(t, kind):
            return slice(4 if kind == "M" else 0, 8 if kind == "M" else 4), slice(QC[t], QC[t] + QT[t])

        @block.scalar
        def _(e):
            nx = [0]
            e.wait_ge(S.pads_zero, 2)
            for pad, rows in ((pe_keys[0], slice(32, 64)), (pe_keys[1], slice(96, 128))):
                for dst, src in pad_copy(pad, T.kcT, rows):
                    e.activation(dst, src, ACT.Copy).then_inc(S.pe_keys, 1)

            def mix_hi(q, kind, t):
                k, c = mix(t, kind)
                e.wait_ge(S.b_ps, q + 1)
                nx[0] += 1
                e.activation(T.xth[:, k, c], BB(q).rearrange("p (k c) -> p k c", k=4)[:, :, 0:QT[t]], ACT.Copy)\
                 .then_inc(S.mix_hi, 1)

            for i, p in enumerate(plan):
                if p["idx"]:
                    s, t, h = p["idx"]
                    j = 8 * (t - 1) + h
                    e.wait_ge(S.s_ps, s + 1)
                    if j >= 2:
                        e.wait_ge(S.scored, j - 1)
                    e.activation(relu[0:QT[t], j % 2, 0:NK[t]], SB(s, QT[t], NK[t]), ACT.Relu).then_inc(S.s_read, 1)
                if p["s"] is not None:
                    kind, t, h = units[i]
                    r = QT[t]
                    e.wait_ge(S.nmax_done, i + 1)
                    if i >= 3:
                        e.wait_ge(S.b_ps, tjob[i - 3] + 1)
                    e.activation(Pb[0:r, i % 3, 0:NK[t]], SB(p["s"], r, NK[t]), ACT.Exp, bias=nmx[0:r, i % 3:i % 3 + 1],
                                 scale=M_SCALE if kind == "M" else D_SCALE,
                                 accum_out=rsum[0:r, 0 if kind == "M" else 1, h:h + 1]).then_inc(S.s_read, 1)
                if p["t"] is not None:
                    u, q = i - 1, p["t"]
                    kind, t, h = units[u]
                    e.wait_ge(S.b_ps, q + 1)
                    if u >= 2:
                        e.wait_ge(S.pv_done, u - 1)
                    if t < 4:
                        e.activation(PT[:, u % 2, 0:NK[t]], BB(q)[:, 0:NK[t]], ACT.Copy).then_inc(S.b_out, 1)
                    else:
                        e.activation(PT[:, u % 2, 0:64], BB(q)[:, 0:64], ACT.Copy)
                        e.activation(PT[0:16, u % 2, 64:80], BB(q)[0:16, 64:80], ACT.Copy).then_inc(S.b_out, 1)
                for q, kind, t, a in p["ot"]:
                    if kind == "D":
                        mix_hi(q, kind, t)
                    else:
                        e.wait_ge(S.b_ps, q + 1)
                        e.activation(olT[:, 4 * a:4 * a + 4, 0:QT[t]],
                                     BB(q).rearrange("p (k c) -> p k c", k=4)[:, :, 0:QT[t]], ACT.Copy).then_inc(S.b_out, 1)
                if p["uv"]:
                    mix_hi(p["uv"][0], "M", p["uv"][1])

        @block.vector
        def _(e):
            nround, nlo, nsround = [0], [0], [0]

            def mix_lo(q, kind, t):
                k, c = mix(t, kind)
                nlo[0] += 1
                e.wait_ge(S.mix_hi, nlo[0])
                e.tensor_tensor(T.xtl[:, k, c], BB(q).rearrange("p (k c) -> p k c", k=4)[:, :, 0:QT[t]],
                                T.xth[:, k, c].bitcast(F32), ALU.subtract).then_inc(S.mix_lo, 1)

            e.wait_ge(S.pads_zero, 4)
            for pad, src, rows in ((pads[2], T.kcT, slice(64, 96)), (pads[3], T.kT2, slice(64, 128))):
                for to, of in pad_copy(pad, src, rows):
                    e.tensor_copy(to, of).then_inc(S.key_step, 1)
            e.wait_ge(S.pe_keys, 4)
            e.wait_ge(S.key_step, 4)
            for src, rows in ((T.kcT, slice(32, 64)), (T.kcT, slice(64, 128)), (T.kT2, slice(64, 128))):
                e.memset(src[rows, :], 0.0).then_inc(S.key_step, 1)
            e.memset(bias[:, 4 * P:PROMPT], 0.0)
            e.tensor_copy(bias[:, 0:P], T.trib[:, :]).then_inc(S.bias_done, 1)
            for i, p in enumerate(plan):
                if i < n:
                    kind, t, h = units[i]
                    r = QT[t]
                    e.wait_ge(S.s_ps, p["s"] + 1)
                    if i >= 3:
                        e.wait_ge(S.s_read, plan[i - 3]["s"] + 1)
                    e.tensor_reduce(mx[0:r, i % 3:i % 3 + 1], SB(p["s"], r, NK[t]), AX, ALU.max).then_inc(S.max_done, 1)
                    e.wait_ge(S.max_done, i + 1)
                    e.tensor_scalar(nmx[0:r, i % 3:i % 3 + 1], mx[0:r, i % 3:i % 3 + 1],
                                    -(M_SCALE if kind == "M" else D_SCALE), None, ALU.mult).then_inc(S.nmax_done, 1)
                    if kind == "M" and t > 0:
                        ww = work[0:r, 0:GIVEN + NK[t]]
                        if h == 0:
                            d = work[0:r, GIVEN + t * P:GIVEN + t * P + r]
                            e.wait_ge(S.scored, 8 * t)
                            e.tensor_tensor(d, d, T.trib[0:r, 0:r], ALU.add).then_inc(S.round_done, 1)
                            nround[0] += 1
                            e.wait_ge(S.given_set, t)
                            e.wait_ge(S.round_done, nround[0])
                        for _ in range(rounds[h]):
                            e.max(top[0:r, :], ww).then_inc(S.round_max, 1)
                            e.wait_ge(S.round_max, nround[0] - (t - 1))
                            e.match_replace(ww, top[0:r, :], ww, TAKEN).then_inc(S.round_done, 1)
                            nround[0] += 1
                            e.wait_ge(S.round_done, nround[0])
                        if h == 7:
                            e.tensor_scalar(bias[0:r, 0:NK[t]], work[0:r, GIVEN:GIVEN + NK[t]], 2 / 3 * TAKEN, NEG,
                                            ALU.is_gt, ALU.mult).then_inc(S.biased, 1)
                            e.wait_ge(S.biased, t)
                            d = bias[0:r, t * P:t * P + r]
                            e.tensor_tensor(d, d, T.trib[0:r, 0:r], ALU.add).then_inc(S.bias_done, 1)
                if i < n and units[i][:2] in STEP_UNITS:
                    sample_step(e, T, S, nsround[0])
                    nsround[0] += 1
                if p["norm"]:
                    kind, t = p["norm"]
                    r = QT[t]
                    g = groups_before(i - 2)
                    a = 0 if kind == "M" else 1
                    w = RL if kind == "M" else AD
                    e.wait_ge(S.pv_done, i - 1)
                    e.reciprocal(rinv[0:r, a, :], rsum[0:r, a, :]).then_inc(S.rinv_done, 1)
                    e.wait_ge(S.rinv_done, g)
                    if g >= 2:
                        prev = [q for pp in plan[:i] for q, *_ in pp["ot"]]
                        e.wait_ge(S.b_ps, prev[-1] + 1)
                    e.tensor_tensor(osb[0:r, 0:8 * w].rearrange("p (h c) -> p h c", h=8),
                                    flat[0:r, 6 * 512:6 * 512 + 8 * w].rearrange("p (h c) -> p h c", h=8),
                                    rinv[0:r, a, :].unsqueeze(2).to_broadcast([r, 8, w]), ALU.mult).then_inc(S.o_done, 1)
                for q, kind, t, a in p["ot"]:
                    if kind == "D":
                        mix_lo(q, kind, t)
                if p["uv"]:
                    mix_lo(p["uv"][0], "M", p["uv"][1])
    nc.all_engine_barrier(sems_to_clear=S.range)


SKEYS = PAST + DEC_T
INDEX_SEMS = ["w_zero", "w_set", "kh_done", "kl_done", "turned",
              "out_act", "out_dve", "dots_done", "relu_done", "weighed", "scored", "newv_in"]


PAGE_SEMS = ["page_in0", "page_in1", "page_in2", "page_in3"]
INDEX_FILLS, SAMPLE_FILLS = DEC_B // 2, DEC_B // 4


def pages_there(e, T, l, stage, slot, fill):
    index = INDEX_FILLS if slot < 2 else 0
    a_layer = index + 2 * SAMPLE_FILLS
    before = 0 if stage == 0 else index + (stage - 1) * SAMPLE_FILLS
    e.wait_ge(T.page_in[slot], l * (16 * a_layer) + 16 * (before + fill + 1))


def page_load(e, T, r, dst, cache, slot):
    e.indirect_dma_start(dst.rearrange("p i c -> p (i c)"), None,
                         cache.rearrange("l n (c i) w -> (l n c) (i w)", i=P // CHUNKS),
                         bass.IndirectOffsetOnAxis(ap=T.rows[:, r:r + 1], axis=0)).then_inc(T.page_in[slot], 16)


def index_block(nc, T, S, l, cache_dsa):
    A = Map(T.nc, T.raw_at)
    ks = T.M.put("iks", [P, 2, PAGES, P], F32R, A.region(2 * PAGES * P * 4))
    ip = [T.M.put("ip0", [P, PAGES, ROW], F32, A.region(PAGES * ROW * 4))]
    wall = T.M.put("wall", [P, DEC_B // 2, SAMPLE], F32, A.region(DEC_B // 2 * SAMPLE * 4))
    X = Map(T.nc, T.xth_at)
    kT = T.M.put("ikT", [P, 2, PAST], F32R, X.region(2 * PAST * 4))
    R = T.M.put("irelu", [P, SKEYS], F32, X.region(SKEYS * 4))
    ip.append(T.M.put("ip1", [P, PAGES, ROW], F32, X.region(PAGES * ROW * 4)))
    assert A.top <= T.gb_at - 4096 and X.top <= T.xth_at + 2 * KD * TOK * 4
    T.score = T.M.put("score", [SAMPLE, SKEYS], F32, T.score_at)
    flat = T.ps[:, :, :].rearrange("p b c -> p (b c)")
    jobs = [(r, g) for r in range(DEC_B) for g in range(4)]

    def freed(e, q):
        if q >= 0:
            e.wait_ge(S.out_dve if jobs[q][1] % 2 else S.out_act, q // 2 + 1)

    with nc.Block() as block:
        @block.gpsimd
        def _(e):
            for r in range(DEC_B):
                if r >= 2:
                    e.wait_ge(S.kl_done, r - 1)
                page_load(e, T, r, ip[r % 2][:, :, :], cache_dsa, r % 2)

        @block.tensor
        def _(e):
            def turn(r):
                e.wait_ge(S.kl_done, r + 1)
                for g in range(4):
                    q = 4 * r + g
                    freed(e, q - 3)
                    for k in range(4):
                        mm = e.transpose(T.ps[:, 5 + q % 3, k * P:(k + 1) * P], ks[:, r % 2, 4 * g + k, :].bitcast(F32),
                                         T.ident[:, :])
                    mm.then_inc(S.turned, 1)

            def dots(r):
                if r % 2 == 0 and r > 0:
                    e.wait_ge(S.scored, r)
                e.wait_ge(S.out_act, 2 * r + 2)
                e.wait_ge(S.out_dve, 2 * r + 2)
                for c in range(5):
                    out = T.ps[:, c, :] if c < 4 else T.ps[:, 4, 0:DEC_T]
                    rhs = kT[:, r % 2, c * 512:(c + 1) * 512] if c < 4 else T.newT[:, 1, r * DEC_T:(r + 1) * DEC_T]
                    mm = e.matmul(out, T.QI[:, r, :], rhs, start=r % 2 == 0, stop=r % 2 == 1)
                mm.then_inc(S.dots_done, 1)

            def weigh(p):
                e.wait_ge(S.relu_done, p + 1)
                if p == 0:
                    e.wait_ge(S.w_set, DEC_B)
                for c in range(5):
                    w = 512 if c < 4 else DEC_T
                    mm = e.matmul(T.ps[0:SAMPLE, c, 0:w], wall[:, p, :], R[:, c * 512:c * 512 + w], start=True, stop=True)
                mm.then_inc(S.weighed, 1)
            turn(0)
            turn(1)
            for p in range(DEC_B // 2):
                dots(2 * p)
                dots(2 * p + 1)
                for r in (2 * p + 2, 2 * p + 3):
                    if r < DEC_B:
                        turn(r)
                weigh(p)

        def outs(e, r, par, copy, sem):
            for g in (par, par + 2):
                q = 4 * r + g
                e.wait_ge(S.turned, q + 1)
                if r >= 2:
                    e.wait_ge(S.dots_done, r - 1)
                copy(kT[:, r % 2, g * 512:(g + 1) * 512], T.ps[:, 5 + q % 3, :]).then_inc(sem, 1)

        @block.scalar
        def _(e):
            def high(r):
                pages_there(e, T, l, 0, r % 2, r // 2)
                if r >= 2:
                    e.wait_ge(S.turned, 4 * (r - 1))
                e.activation(ks[:, r % 2, :, 0:64].rearrange("p i (a c) -> p i a c", a=2),
                             ip[r % 2][:, :, 2 * AD:ROW].unsqueeze(2).to_broadcast([P, PAGES, 2, ID]), ACT.Copy).then_inc(S.kh_done, 1)
            cp = lambda d, s: e.activation(d, s, ACT.Copy)
            high(0)
            high(1)
            outs(e, 0, 0, cp, S.out_act)
            outs(e, 1, 0, cp, S.out_act)
            for p in range(DEC_B // 2):
                for r in (2 * p + 2, 2 * p + 3):
                    if r < DEC_B:
                        high(r)
                e.wait_ge(S.dots_done, 2 * p + 2)
                if p > 0:
                    e.wait_ge(S.weighed, p)
                e.activation(R[:, :], flat[:, 0:SKEYS], ACT.Relu).then_inc(S.relu_done, 1)
                for r in (2 * p + 2, 2 * p + 3):
                    if r < DEC_B:
                        outs(e, r, 0, cp, S.out_act)

        @block.vector
        def _(e):
            def low(r):
                e.wait_ge(S.kh_done, r + 1)
                e.tensor_tensor(ks[:, r % 2, :, 64:P].rearrange("p i (a c) -> p i a c", a=2),
                                ip[r % 2][:, :, 2 * AD:ROW].unsqueeze(2).to_broadcast([P, PAGES, 2, ID]),
                                ks[:, r % 2, :, 0:64].rearrange("p i (a c) -> p i a c", a=2).bitcast(F32),
                                ALU.subtract).then_inc(S.kl_done, 1)
            e.memset(wall[:, :, :], 0.0).then_inc(S.w_zero, 1)
            e.wait_ge(S.w_zero, 1)
            for r in range(DEC_B):
                h = slice(64 * (r % 2), 64 * (r % 2) + 64)
                e.tensor_scalar(wall[h, r // 2, r * DEC_T:(r + 1) * DEC_T], T.qdelta[h, :], T.wcol[h, r:r + 1], None,
                                ALU.mult).then_inc(S.w_set, 1)
            low(0)
            low(1)
            outs(e, 0, 1, e.tensor_copy, S.out_dve)
            outs(e, 1, 1, e.tensor_copy, S.out_dve)
            for p in range(DEC_B // 2):
                for r in (2 * p + 2, 2 * p + 3):
                    if r < DEC_B:
                        low(r)
                for r in (2 * p + 2, 2 * p + 3):
                    if r < DEC_B:
                        outs(e, r, 1, e.tensor_copy, S.out_dve)
                e.wait_ge(S.weighed, p + 1)
                for new in range(2):
                    dst, src = T.score[:, PAST:SKEYS], flat[0:SAMPLE, PAST:SKEYS]
                    if not new:
                        dst = T.score[:, 0:PAST].rearrange("t (p i) -> t i p", i=PAGES)
                        src = flat[0:SAMPLE, 0:PAST].rearrange("t (i p) -> t i p", i=PAGES)
                    if p == 0:
                        e.tensor_copy(dst, src).then_inc(S.scored, 1)
                    else:
                        e.wait_ge(S.scored, 2 * p)
                        e.tensor_tensor(dst, dst, src, ALU.add).then_inc(S.scored, 1)
            e.wait_ge(S.scored, DEC_B)
            new = T.score[:, PAST:SKEYS]
            e.tensor_tensor(new, new, T.tri8[0:SAMPLE, :], ALU.add)
    nc.all_engine_barrier(sems_to_clear=S.range)


STEP_CHUNKS = [1, 2, 4, 5]
SAMPLE_SEMS = ["s_round_max", "s_round_done", "newv_in", "kh_done", "kl_done", "bank_ps", "out_act", "out_dve",
               "chunk_used", "part_done", "s_done", "max_done", "nmax_done", "exp_done", "pv_done", "rinv_done", "o_done", "o_ps", "ol_done",
               "uv_ps", "mix_hi", "mix_lo", "bias_set"]


def sample_block(nc, T, S, l, kind, cache, new_rows, next_cache=None):
    M = kind == "M"
    VW, VAT = (RL, 0) if M else (AD, AD)
    n = kind
    C1 = Map(T.nc, T.arena)
    C1.region(4 * PAGES * ROW * 4)
    pg = T.pg
    olS = T.M.put(n + "olS", [P, DEC_B, BH, DEC_T], F32, C1.region(2048))
    osb = T.M.put(n + "osb", [P, P], F32, C1.region(512))
    st = T.M.put(n + "st", [P, 10], F32, C1.region(40))
    assert C1.top <= T.newT_at
    Z = Map(T.nc, T.z_at)
    ks = T.M.put(n + "ks", [P, 2, PAGES, P], F32R, Z.region(2 * PAGES * P * 4))
    Pb = T.M.put(n + "P", [P, SKEYS], F32, Z.region(SKEYS * 4))
    assert Z.top <= T.comb_at
    A = Map(T.nc, T.raw_at)
    kT = T.M.put(n + "kT", [P, 3, 512], F32R, A.region(3 * 2048))
    if M:
        cTh = T.M.put(n + "cTh", [P, 3, 512], F32R, A.region(3 * 2048))
        cTl = T.M.put(n + "cTl", [P, 3, 512], F32R, A.region(3 * 2048))
    else:
        bias = T.M.put("sbias", [SAMPLE, SKEYS], BF16, A.region(SKEYS * 2))
    PT = T.M.put(n + "PT", [P, 2, 512], F32, A.region(4096))
    newv = T.M.put(n + "newv", [DEC_T, DEC_B, VW], F32, A.region(DEC_B * VW * 4))
    assert A.top <= T.gb_at - 4096
    flat = T.ps[:, :, :].rearrange("p b c -> p (b c)")
    stage = 1 if M else 2
    PAIRS = DEC_B // 2
    scale = M_SCALE if M else D_SCALE

    order = []
    PRE = 2

    def own(p):
        return range(8 * p + (PRE if p > 0 else 0), 8 * p + 8)

    def early(p):
        return range(8 * p + 8, 8 * p + 8 + PRE) if p + 1 < PAIRS else range(0)

    for p in range(PAIRS):
        for ch in [*own(p), *early(p)]:
            order += ([("c", ch)] if M else []) + [("k", ch)]
        if p > 0:
            order.append(("o", p - 1))
        order += [("p", p, g) for g in range(5)]
    order.append(("o", PAIRS - 1))
    jobs, na, nd = {}, 0, 0
    for q, j in enumerate(order):
        who = {"c": "AD", "k": "D" if j[1] % 2 and M else "A", "p": "A" if j[-1] % 2 else "D", "o": "A" if M else "O"}[j[0]]
        if not M and j[0] == "k":
            who = "A" if j[1] % 2 else "D"
        if "A" in who:
            na += 1
        if "D" in who:
            nd += 1
        jobs[j] = (q, who, na, nd)

    def gone(e, j):
        q, who, a, d = jobs[j]
        if who == "O":
            e.wait_ge(S.mix_lo, 2 * (j[1] + 1))
        elif "D" in who:
            e.wait_ge(S.out_dve, d)
        else:
            e.wait_ge(S.out_act, a)

    def bank(j):
        return T.ps[:, 6 + jobs[j][0] % 2, :]

    def take(e, j):
        q = jobs[j][0]
        if q >= 2:
            gone(e, order[q - 2])

    with nc.Block() as block:
        @block.sync
        def _(e):
            c0 = 0 if M else AD
            e.dma_start(newv[:, :, :], new_rows[bass.ds(l, 1), :, :, c0:c0 + VW].rearrange("l b t c -> t (l b) c"))\
             .then_inc(S.newv_in, 16)

        def kview(r, part):
            if M:
                d = ks[:, r % 2, :, 64 * part:64 * part + 64].rearrange("p i (a c) -> p i a c", a=2)
                return d, pg[:, r % 4, :, RL:RL + PE_D].unsqueeze(2).to_broadcast([P, PAGES, 2, PE_D])
            return ks[:, r % 2, :, 64 * part:64 * part + 64], pg[:, r % 4, :, 0:AD]

        def low(e, r):
            e.wait_ge(S.kh_done, r + 1)
            d, s = kview(r, 1)
            e.tensor_tensor(d, s, kview(r, 0)[0].bitcast(F32), ALU.subtract).then_inc(S.kl_done, 1)

        @block.gpsimd
        def _(e):
            for r in range(0 if M else 2, 4):
                page_load(e, T, r, pg[:, r, :, :], cache, r)
            for r in range(DEC_B):
                if r >= 4 and r % 2 == 0:
                    e.wait_ge(S.pv_done, r // 2 - 1)
                    for r_ in (r, r + 1):
                        page_load(e, T, r_, pg[:, r_ % 4, :, :], cache, r_ % 4)
                low(e, r)
            if M:
                e.wait_ge(S.pv_done, 3)
                for r in (0, 1):
                    page_load(e, T, r, pg[:, r, :, :], next_cache, r)

        @block.tensor
        def _(e):
            def turn_chunk(ch):
                r, g = ch // 4, ch % 4
                if M:
                    take(e, ("c", ch))
                    if g == 0:
                        pages_there(e, T, l, stage, r % 4, r // 4)
                    for k in range(4):
                        mm = e.transpose(bank(("c", ch))[:, k * P:(k + 1) * P], pg[:, r % 4, 4 * g + k, 0:RL], T.ident[:, :])
                    mm.then_inc(S.bank_ps, 1)
                take(e, ("k", ch))
                if g == 0:
                    e.wait_ge(S.kl_done, r + 1)
                for k in range(4):
                    mm = e.transpose(bank(("k", ch))[:, k * P:(k + 1) * P], ks[:, r % 2, 4 * g + k, :].bitcast(F32),
                                     T.ident[:, :])
                mm.then_inc(S.bank_ps, 1)

            def scores(ch):
                r, g = ch // 4, ch % 4
                b0, s = r % 2 == 0, ch % 3
                if b0 and g == 0 and r > 0:
                    e.wait_ge(S.exp_done, r)
                gone(e, ("k", ch))
                out = T.ps[:, g, :]
                if M:
                    gone(e, ("c", ch))
                    ops = [(T.QLh, cTh), (T.QLh, cTl), (T.QLl, cTh), (T.QP, kT)]
                else:
                    ops = [(T.QA, kT), (T.QB, kT)]
                for i, (q, k) in enumerate(ops):
                    mm = e.matmul(out, q[:, r, :], k[:, s, :], start=b0 and i == 0, stop=not b0 and i == len(ops) - 1 and M)
                if not M and not b0:
                    if ch == 4:
                        e.wait_ge(S.bias_set, 3)
                    mm = e.matmul(out, T.selb[:, r // 2, :], bias[:, g * 512:(g + 1) * 512], start=False, stop=True)
                mm.then_inc(S.chunk_used, 1)
                if g == 3:
                    out = T.ps[:, 4, 0:DEC_T]
                    c = slice(r * DEC_T, (r + 1) * DEC_T)
                    if M:
                        ops = [(T.QLh, T.newcT[:, 0, c]), (T.QLh, T.newcT[:, 1, c]), (T.QLl, T.newcT[:, 0, c]),
                               (T.QP, T.newT[:, 2, c])]
                    else:
                        ops = [(T.QA, T.newT[:, 0, c]), (T.QB, T.newT[:, 0, c])]
                    for i, (q, k) in enumerate(ops):
                        mm = e.matmul(out, q[:, r, :], k, start=b0 and i == 0, stop=False)
                    if not b0:
                        if M:
                            mm = e.matmul(out, T.identb[:, :], T.tri8b[:, :], start=False, stop=True)
                        else:
                            mm = e.matmul(out, T.selb[:, r // 2, :], bias[:, PAST:SKEYS], start=False, stop=True)
                        mm.then_inc(S.s_done, 1)

            def turn_p(p, g):
                j = ("p", p, g)
                take(e, j)
                if g in (0, 2):
                    e.wait_ge(S.exp_done, 2 * p + 1 + g // 2)
                if g < 4:
                    for k in range(4):
                        c = (4 * g + k) * P
                        mm = e.transpose(bank(j)[:, k * P:(k + 1) * P], Pb[:, c:c + P], T.ident[:, :])
                else:
                    mm = e.transpose(bank(j)[0:DEC_T, 0:P], Pb[:, PAST:SKEYS], T.ident[:, :])
                mm.then_inc(S.bank_ps, 1)

            def values(p, g):
                gone(e, ("p", p, g))
                if g == 0 and p > 0:
                    e.wait_ge(S.o_done, p)
                if p == 0 and g == 4:
                    e.wait_ge(S.newv_in, 16)
                for b in range(2):
                    r = 2 * p + b
                    out = T.ps[64 * b:64 * b + 64, 5, 0:VW]
                    for k in range(4 if g < 4 else 1):
                        kr = P if g < 4 else DEC_T
                        c = k * P + 64 * b
                        rhs = pg[:, r % 4, 4 * g + k, VAT:VAT + VW] if g < 4 else newv[:, r, :]
                        mm = e.matmul(out, PT[0:kr, (5 * p + g) % 2, c:c + 64], rhs, start=g == 0 and k == 0, stop=g == 4)
                mm.then_inc(S.pv_done, 1) if g == 4 else mm.then_inc(S.o_ps, 1)

            def turn_o(p):
                j = ("o", p)
                take(e, j)
                e.wait_ge(S.o_done, p + 1)
                e.transpose(bank(j)[:, 0:P], osb[:, :], T.ident[:, :]).then_inc(S.bank_ps, 1)

            for p in range(PAIRS):
                if p == 0:
                    turn_chunk(0)
                for ch in range(8 * p, 8 * p + 8):
                    if ch + 1 in own(p):
                        turn_chunk(ch + 1)
                    scores(ch)
                for ch in early(p):
                    turn_chunk(ch)
                if p > 0:
                    turn_o(p - 1)
                turn_p(p, 0)
                for g in range(5):
                    if g < 4:
                        turn_p(p, g + 1)
                    values(p, g)
            turn_o(PAIRS - 1)
            if M:
                e.wait_ge(S.ol_done, PAIRS)
                for h in range(BH):
                    b = 64 * (h % 2)
                    mm = e.matmul(T.ps[b:b + VD, 0, (h // 2) * SAMPLE:(h // 2 + 1) * SAMPLE], T.wuv[:, h, :],
                                  olS[:, :, h, :], start=True, stop=True)
                mm.then_inc(S.uv_ps, 1)

        def dsa_out(p, par):
            rows = slice(64 * par, 64 * par + 64)
            c = S0 + 2 * p * DEC_T
            dst = lambda x: x[rows, 0:4, c:c + 2 * DEC_T].rearrange("p k (b t) -> p k b t", b=2)
            src = bank(("o", p))[rows, 0:P].rearrange("p (b k u t) -> p u k b t", b=2, u=2, k=4)[:, par]
            return dst, src

        def pt_out(e, p, g, me):
            j = ("p", p, g)
            q, who, a, d = jobs[j]
            if who != me:
                return
            i = 5 * p + g
            e.wait_ge(S.bank_ps, q + 1)
            if i >= 2:
                if g >= 2:
                    e.wait_ge(S.o_ps, 4 * p + g - 1)
                elif g == 1:
                    e.wait_ge(S.pv_done, p)
                else:
                    e.wait_ge(S.o_ps, 4 * p)
            rows, w = (P, 512) if g < 4 else (DEC_T, P)
            if me == "A":
                e.activation(PT[0:rows, i % 2, 0:w], bank(j)[0:rows, 0:w], ACT.Copy).then_inc(S.out_act, 1)
            else:
                e.tensor_copy(PT[0:rows, i % 2, 0:w], bank(j)[0:rows, 0:w]).then_inc(S.out_dve, 1)

        def mix_out(e, p):
            act = e.engine == mybir.EngineType.Activation
            e.wait_ge(S.bank_ps, jobs[("o", p)][0] + 1)
            for par in range(2):
                dst, src = dsa_out(p, par)
                if act:
                    e.activation(dst(T.xth), src, ACT.Copy).then_inc(S.mix_hi, 1)
                else:
                    e.wait_ge(S.mix_hi, 2 * p + par + 1)
                    e.tensor_tensor(dst(T.xtl), src, dst(T.xth).bitcast(F32), ALU.subtract).then_inc(S.mix_lo, 1)

        @block.scalar
        def _(e):
            def high(r):
                pages_there(e, T, l, stage, r % 4, r // 4)
                if r >= 2:
                    e.wait_ge(S.bank_ps, jobs[("k", 4 * (r - 2) + 3)][0] + 1)
                d, s = kview(r, 0)
                e.activation(d, s, ACT.Copy).then_inc(S.kh_done, 1)

            def chunk_out(ch):
                s = ch % 3
                for kd in ("c", "k"):
                    if (kd, ch) not in jobs:
                        continue
                    q, who, a, d = jobs[(kd, ch)]
                    if "A" in who:
                        e.wait_ge(S.bank_ps, q + 1)
                        if ch >= 3:
                            e.wait_ge(S.chunk_used, ch - 2)
                        e.activation(cTh[:, s, :] if kd == "c" else kT[:, s, :], bank((kd, ch)), ACT.Copy).then_inc(S.out_act, 1)

            high(0)
            high(1)
            for p in range(PAIRS):
                for ch in range(8 * p, 8 * p + 8):
                    if ch in own(p):
                        chunk_out(ch)
                    if ch % 4 == 3 and ch // 4 + 2 < DEC_B:
                        high(ch // 4 + 2)
                for ch in early(p):
                    chunk_out(ch)
                e.wait_ge(S.nmax_done, p + 1)
                if p > 0:
                    e.wait_ge(S.bank_ps, jobs[("p", p - 1, 4)][0] + 1)
                if p > 0:
                    e.wait_ge(S.rinv_done, 2 * p)
                for half, c in enumerate((slice(0, 1024), slice(1024, SKEYS))):
                    e.activation(Pb[:, c], flat[:, c], ACT.Exp, bias=st[:, 1:2], scale=scale,
                                 accum_out=st[:, 8 + half:9 + half]).then_inc(S.exp_done, 1)
                if p > 0 and M:
                    j = ("o", p - 1)
                    e.wait_ge(S.bank_ps, jobs[j][0] + 1)
                    e.activation(olS[:, 2 * p - 2:2 * p, :, :].rearrange("p b h t -> p (b h t)"), bank(j)[:, 0:P], ACT.Copy)\
                     .then_inc(S.out_act, 1)
                if p > 0 and not M:
                    mix_out(e, p - 1)
                for g in range(5):
                    pt_out(e, p, g, "A")
            if M:
                j = ("o", PAIRS - 1)
                e.wait_ge(S.bank_ps, jobs[j][0] + 1)
                e.activation(olS[:, DEC_B - 2:DEC_B, :, :].rearrange("p b h t -> p (b h t)"), bank(j)[:, 0:P], ACT.Copy)\
                 .then_inc(S.ol_done, PAIRS)
                e.wait_ge(S.uv_ps, 1)
                e.activation(T.xth[:, 4:8, S0:TAIL], T.ps[:, 0, 0:4 * SAMPLE].rearrange("p (k c) -> p k c", k=4), ACT.Copy)\
                 .then_inc(S.mix_hi, 1)
            else:
                mix_out(e, PAIRS - 1)

        @block.vector
        def _(e):
            nround = [0]
            if not M:
                e.tensor_scalar(bias[:, 0:PAST].rearrange("t (i p) -> t i p", i=PAGES),
                                T.score[:, 0:PAST].rearrange("t (p i) -> t i p", i=PAGES),
                                2 / 3 * TAKEN, NEG, ALU.is_gt, ALU.mult).then_inc(S.bias_set, 1)
                e.tensor_scalar(bias[:, PAST:SKEYS], T.score[:, PAST:SKEYS], 2 / 3 * TAKEN, NEG, ALU.is_gt, ALU.mult)\
                 .then_inc(S.bias_set, 1)
                e.wait_ge(S.bias_set, 2)
                e.tensor_tensor(bias[:, PAST:SKEYS], bias[:, PAST:SKEYS], T.tri8b[0:SAMPLE, :], ALU.add).then_inc(S.bias_set, 1)
            def chunk_out(ch):
                s = ch % 3
                for kd in ("c", "k"):
                    if (kd, ch) not in jobs:
                        continue
                    q, who, a, d = jobs[(kd, ch)]
                    if "D" not in who:
                        continue
                    e.wait_ge(S.bank_ps, q + 1)
                    if ch >= 3:
                        e.wait_ge(S.chunk_used, ch - 2)
                    if kd == "c":
                        e.wait_ge(S.out_act, a)
                        e.tensor_tensor(cTl[:, s, :], bank((kd, ch)), cTh[:, s, :].bitcast(F32), ALU.subtract)\
                         .then_inc(S.out_dve, 1)
                    else:
                        e.tensor_copy(kT[:, s, :], bank((kd, ch))).then_inc(S.out_dve, 1)

            def part_max(p, g):
                e.wait_ge(*((S.chunk_used, 8 * p + 5 + g) if g < 3 else (S.s_done, p + 1)))
                e.tensor_reduce(st[:, 4 + g:5 + g], flat[:, g * 512:(g + 1) * 512 if g < 3 else SKEYS], AX, ALU.max)\
                 .then_inc(S.part_done, 1)

            for p in range(PAIRS):
                for ch in range(8 * p, 8 * p + 8):
                    if ch in own(p):
                        chunk_out(ch)
                    if ch >= 8 * p + 6:
                        part_max(p, ch - 8 * p - 6)
                    if M and ch % 8 in STEP_CHUNKS:
                        sample_step(e, T, S, nround[0])
                        nround[0] += 1
                part_max(p, 2)
                part_max(p, 3)
                e.wait_ge(S.part_done, 4 * p + 4)
                e.tensor_reduce(st[:, 0:1], st[:, 4:8], AX, ALU.max).then_inc(S.max_done, 1)
                e.wait_ge(S.max_done, p + 1)
                if p > 0:
                    e.wait_ge(S.exp_done, 2 * p)
                e.tensor_scalar(st[:, 1:2], st[:, 0:1], -scale, None, ALU.mult).then_inc(S.nmax_done, 1)
                for ch in early(p):
                    chunk_out(ch)
                if M:
                    for _ in range(STEPS_THERE // PAIRS - len(STEP_CHUNKS)):
                        sample_step(e, T, S, nround[0])
                        nround[0] += 1
                if p > 0 and not M:
                    mix_out(e, p - 1)
                for g in range(5):
                    pt_out(e, p, g, "D")
                e.wait_ge(S.exp_done, 2 * p + 2)
                e.tensor_tensor(st[:, 2:3], st[:, 8:9], st[:, 9:10], ALU.add).then_inc(S.rinv_done, 1)
                e.wait_ge(S.rinv_done, 2 * p + 1)
                e.reciprocal(st[:, 3:4], st[:, 2:3]).then_inc(S.rinv_done, 1)
                e.wait_ge(S.rinv_done, 2 * p + 2)
                e.wait_ge(S.pv_done, p + 1)
                if p > 0:
                    e.wait_ge(S.bank_ps, jobs[("o", p - 1)][0] + 1)
                if M:
                    e.tensor_scalar(osb[:, :], T.ps[:, 5, 0:P], st[:, 3:4], None, ALU.mult).then_inc(S.o_done, 1)
                else:
                    e.tensor_scalar(osb[:, :].rearrange("p (a c) -> p a c", a=2),
                                    T.ps[:, 5, 0:AD].unsqueeze(1).to_broadcast([P, 2, AD]), st[:, 3:4], None,
                                    ALU.mult).then_inc(S.o_done, 1)
            if M:
                assert nround[0] == STEPS_THERE
                e.wait_ge(S.mix_hi, 1)
                e.tensor_tensor(T.xtl[:, 4:8, S0:TAIL], T.ps[:, 0, 0:4 * SAMPLE].rearrange("p (k c) -> p k c", k=4),
                                T.xth[:, 4:8, S0:TAIL].bitcast(F32), ALU.subtract).then_inc(S.mix_lo, 1)
            else:
                mix_out(e, PAIRS - 1)
    nc.all_engine_barrier(sems_to_clear=S.range)




def mix_out_block(nc, T, S, l, w_o, ln_g, ln_b):
    load, hi, lo = stream_ops(T, S)
    T.gb_free = lambda S_: None
    sp2, act2, dve2, pool2, pe2 = out_stage(nc, T, S, KD, 0, T.xth, T.xtl, 1.0, lambda e, g, k, t: None)
    with nc.Block() as block:
        @block.sync
        def _(e):
            sp2(e, lambda k: w_o[bass.ds(l, 1), k * P:(k + 1) * P, :].rearrange("l p n -> p (l n)"), ln_g, ln_b, l)

        @block.scalar
        def _(e):
            hi(e, 0, 0, 0, first=True)
            hi(e, 1, 1, 0, first=True)
            act2(e)

        @block.vector
        def _(e):
            lo(e, 0, 0)
            lo(e, 1, 1)
            dve2(e)

        @block.gpsimd
        def _(e):
            for t in range(TILES):
                x = T.x[0:ROWS[t], t, :]
                e.tensor_scalar(x, x, ALPHA, 1.0, ALU.mult, ALU.mult).then_inc(S.alpha_done, 1)
            pool2(e)

        @block.tensor
        def _(e):
            pe2(e)
    nc.all_engine_barrier(sems_to_clear=S.range)


def build(nc, W, O):
    with ExitStack() as ctx:
        T = make_tensors(nc, ctx)
        proj_tensors(T)
        init_s = Sems(ctx, nc, "init", INIT_SEMS)
        ffn_s = Sems(ctx, nc, "ffn", FFN_SEMS)
        proj_s = Sems(ctx, nc, "proj", PROJ_SEMS)
        index_s = Sems(ctx, nc, "index", INDEX_SEMS)
        prompt_s = Sems(ctx, nc, "prompt", PROMPT_SEMS)
        sample_s = Sems(ctx, nc, "sample", SAMPLE_SEMS)
        page_s = Sems(ctx, nc, "gather", PAGE_SEMS)
        T.page_in = [page_s.all[n] for n in PAGE_SEMS]
        y_out = ctx.enter_context(nc.semaphore("y_out"))
        init_block(nc, T, init_s, W["x_prompt"], W["x_sample"], W["meta_tokens"], W["consts"], W["page_table"])
        with nc.Fori(0, DEPTH) as l:
            ffn_block(nc, T, ffn_s, l, W["ffn1_w_in"], W["ffn1_w_out"], W["ln1_g"], W["ln1_b"])
            proj_block(nc, T, proj_s, l, W, O)
            index_block(nc, T, index_s, l, W["cache_dsa"])
            prompt_block(nc, T, prompt_s)
            sample_block(nc, T, sample_s, l, "M", W["cache_mla"], O["mla_s"], W["cache_dsa"])
            sample_block(nc, T, sample_s, l, "D", W["cache_dsa"], O["dsa_s"])
            mix_out_block(nc, T, ffn_s, l, W["w_o"], W["ln2_g"], W["ln2_b"])
            ffn_block(nc, T, ffn_s, l, W["ffn2_w_in"], W["ffn2_w_out"], W["ln3_g"], W["ln3_b"])
        with nc.Block() as block:
            @block.sync
            def _(e):
                e.dma_start(O["y_prompt"][0, 0:P - N_META, :], T.x[N_META:P, 0, :]).then_inc(y_out, 16)
                e.dma_start(O["y_prompt"][0, P - N_META:S0 - N_META, :].rearrange("(t p) d -> p t d", p=P),
                            T.x[:, 1:4, :]).then_inc(y_out, 16)
                e.dma_start(O["y_prompt"][0, S0 - N_META:SEQ, :], T.x[SAMPLE:ROWS[4], 4, :]).then_inc(y_out, 16)
                e.dma_start(O["y_sample"].rearrange("b t d -> (b t) d"), T.x[0:SAMPLE, 4, :]).then_inc(y_out, 16)
                e.wait_ge(y_out, 64)


_OUTS = [("y_prompt", (1, SEQ, D)), ("y_sample", (DEC_B, DEC_T, D)), ("dsa_p", (DEPTH, 1, PROMPT, ROW)),
         ("mla_p", (DEPTH, 1, PROMPT, ROW)), ("dsa_s", (DEPTH, DEC_B, DEC_T, ROW)), ("mla_s", (DEPTH, DEC_B, DEC_T, ROW))]


def kernel(**inputs):
    import concourse.bacc as _bacc
    from concourse.bass_utils import run_bass_kernel_spmd as _run

    nc = _bacc.Bacc("TRN2", target_bir_lowering=False, num_devices=1)
    arrays, W, O = {}, {}, {}
    for name, a in [*inputs.items(), ("consts", constants())]:
        a = np.ascontiguousarray(a)
        arrays[f"in_{name}"] = a
        W[name] = nc.dram_tensor(f"in_{name}", a.shape, mybir.dt.from_np(a.dtype), kind="ExternalInput").ap()
    for name, shape in _OUTS:
        O[name] = nc.dram_tensor(f"out_{name}", shape, F32, kind="ExternalOutput").ap()
    O["iw_scratch"] = nc.dram_tensor("iw_scratch", (SAMPLE, IH), F32, kind="Internal").ap()
    build(nc, W, O)
    r = _run(nc, [arrays], core_ids=[0])
    return tuple(r.results[0][f"out_{name}"] for name, _ in _OUTS)
```
